# Optimizing a Trainium2 kernel written in Bass

```python
import jax, jax.numpy as jnp
from jax import lax
import numpy as np

D_MODEL = 1024
BATCH = 1
SEQ = 256
DEPTH = 2

CHUNK = 64
N_MIXERS = 2
HEAD_SIZE = 64
N_HEADS = D_MODEL // HEAD_SIZE
D_FF = 4 * D_MODEL
CONV_WIDTH = 3
D_DECAY_LORA = 64
D_AAA_LORA = 64
D_MV_LORA = 32
D_GATE_LORA = 160
N_CONV_LAYERS = (DEPTH + 1) // 2
N_RWKV_LAYERS = DEPTH // 2
N_VRES = max(N_RWKV_LAYERS - 1, 0)
N_MOD = 6
NORM_EPS = 1e-6
GN_EPS = 64e-5


def _rmsnorm(x, g):
    x32 = x.astype(jnp.float32)
    y = x32 * lax.rsqrt(jnp.mean(x32 * x32, axis=-1, keepdims=True) + NORM_EPS)
    return (y * g.astype(jnp.float32)).astype(x.dtype)

def _modulate(h, shift, scale):
    return h * (1 + scale[:, None, :]) + shift[:, None, :]

def _short_conv_mixer(h, w_in, conv_w, w_out):
    bch = h @ w_in
    b_gate, c_gate, hv = jnp.split(bch, 3, axis=-1)
    u = c_gate * hv
    conv = lax.conv_general_dilated(
        u, conv_w[:, None, :], window_strides=(1,),
        padding=[(CONV_WIDTH - 1, 0)],
        dimension_numbers=('NWC', 'WIO', 'NWC'),
        feature_group_count=D_MODEL)
    return (b_gate * conv) @ w_out

def _wkv7_scan(r, w, k, v, a, b):
    bsz, seq = r.shape[0], r.shape[1]

    def to_chunks(t):
        return t.transpose(1, 0, 2, 3).reshape(seq // CHUNK, CHUNK, bsz, N_HEADS, HEAD_SIZE)

    def frame_step(state, inp):
        r_t, w_t, k_t, v_t, a_t, b_t = inp
        sa = jnp.einsum('bhvk,bhk->bhv', state, a_t)
        state = (state * w_t[:, :, None, :]
                 + sa[..., None] * b_t[:, :, None, :]
                 + v_t[..., None] * k_t[:, :, None, :])
        y_t = jnp.einsum('bhvk,bhk->bhv', state, r_t)
        return state, y_t

    def chunk_step(state, inp_chunk):
        return lax.scan(frame_step, state, inp_chunk)

    s0 = jnp.zeros((bsz, N_HEADS, HEAD_SIZE, HEAD_SIZE), jnp.float32)
    inputs = (to_chunks(r), to_chunks(w), to_chunks(k), to_chunks(v), to_chunks(a), to_chunks(b))
    _, y = lax.scan(chunk_step, s0, inputs)
    return y.reshape(seq, bsz, N_HEADS, HEAD_SIZE).transpose(1, 0, 2, 3)

def _rwkv7_mixer(h, v_first, vres, mu, w_rkv, w_o, w0, w1, w2, a0, a1, a2,
                 g1, g2, k_k, k_a, r_k, ln_w, ln_b):
    bsz, seq, d = h.shape
    h_prev = jnp.pad(h, ((0, 0), (1, 0), (0, 0)))[:, :-1]
    xx = h_prev - h
    xr, xw, xk, xv, xa, xg = h[None] + xx[None] * mu[:, None, None, :]
    r, k, v = jnp.einsum('nbsd,nde->nbse', jnp.stack([xr, xk, xv]), w_rkv)
    w = -jax.nn.softplus(-(w0 + jnp.tanh(xw @ w1) @ w2)) - 0.5
    a = jax.nn.sigmoid(a0 + (xa @ a1) @ a2)
    g = jax.nn.sigmoid(xg @ g1) @ g2
    if vres is None:
        v_first = v
    else:
        v0, v1, v2 = vres
        v = v + (v_first - v) * jax.nn.sigmoid(v0 + (xv @ v1) @ v2)

    def heads(t):
        return t.reshape(bsz, seq, N_HEADS, HEAD_SIZE).astype(jnp.float32)

    kk = heads(k * k_k)
    kk = kk / jnp.maximum(jnp.sqrt(jnp.sum(kk * kk, axis=-1, keepdims=True)), 1e-12)
    k = k * (1 + (a - 1) * k_a)
    rh, kh, vh, ah = heads(r), heads(k), heads(v), heads(a)
    decay = jnp.exp(-jnp.exp(heads(w)))
    y = _wkv7_scan(rh, decay, kh, vh, -kk, kk * ah)
    mean = jnp.mean(y, axis=-1, keepdims=True)
    var = jnp.mean(jnp.square(y - mean), axis=-1, keepdims=True)
    y = (y - mean) * lax.rsqrt(var + GN_EPS)
    y = y * ln_w.reshape(N_HEADS, HEAD_SIZE) + ln_b.reshape(N_HEADS, HEAD_SIZE)
    bonus = jnp.sum(rh * kh * r_k, axis=-1, keepdims=True) * vh
    out = ((y + bonus).reshape(bsz, seq, d).astype(h.dtype) * g) @ w_o
    return out, v_first

def first_inputs(seed: int = 0) -> dict:
    key = jax.random.key(seed)
    ks = iter(jax.random.split(key, 40))
    D = D_MODEL
    nrm = lambda shape, s: jax.random.normal(next(ks), shape, jnp.float32) * s
    uni = lambda shape, lo, hi: jax.random.uniform(next(ks), shape, jnp.float32, lo, hi)
    NC, NR, NV = N_CONV_LAYERS, N_RWKV_LAYERS, N_VRES
    return {
        "x": nrm((BATCH, SEQ, D), 1.0),
        "c": nrm((BATCH, D), 1.0),
        "norm_g": 1.0 + nrm((DEPTH, 2, D), 0.05),
        "final_g": 1.0 + nrm((D,), 0.05),
        "ada_w": nrm((DEPTH, D, N_MOD * D), 0.5 * D ** -0.5),
        "ada_b": nrm((DEPTH, N_MOD * D), 0.02),
        "conv_w_in": nrm((NC, D, 3 * D), D ** -0.5),
        "conv_w": nrm((NC, CONV_WIDTH, D), CONV_WIDTH ** -0.5),
        "conv_w_out": nrm((NC, D, D), D ** -0.5),
        "rw_mu": uni((NR, 6, D), 0.0, 1.0),
        "rw_w_rkv": nrm((NR, 3, D, D), D ** -0.5),
        "rw_w_o": nrm((NR, D, D), D ** -0.5),
        "rw_w0": uni((NR, D), -6.5, -1.5),
        "rw_w1": nrm((NR, D, D_DECAY_LORA), D ** -0.5),
        "rw_w2": nrm((NR, D_DECAY_LORA, D), 0.1 * D_DECAY_LORA ** -0.5),
        "rw_a0": nrm((NR, D), 0.1),
        "rw_a1": nrm((NR, D, D_AAA_LORA), D ** -0.5),
        "rw_a2": nrm((NR, D_AAA_LORA, D), 0.1 * D_AAA_LORA ** -0.5),
        "rw_g1": nrm((NR, D, D_GATE_LORA), D ** -0.5),
        "rw_g2": nrm((NR, D_GATE_LORA, D), D_GATE_LORA ** -0.5),
        "rw_k_k": 0.85 + nrm((NR, D), 0.05),
        "rw_k_a": 1.0 + nrm((NR, D), 0.05),
        "rw_r_k": nrm((NR, N_HEADS, HEAD_SIZE), 0.1),
        "rw_ln_w": 1.0 + nrm((NR, D), 0.05),
        "rw_ln_b": nrm((NR, D), 0.02),
        "rw_v0": 1.0 + nrm((NV, D), 0.1),
        "rw_v1": nrm((NV, D, D_MV_LORA), D ** -0.5),
        "rw_v2": nrm((NV, D_MV_LORA, D), 0.1 * D_MV_LORA ** -0.5),
        "mlp_w1": nrm((DEPTH, D, D_FF), D ** -0.5),
        "mlp_w2": nrm((DEPTH, D_FF, D), D_FF ** -0.5),
    }

def first_block(x, c, norm_g, final_g, ada_w, ada_b, conv_w_in, conv_w, conv_w_out,
              rw_mu, rw_w_rkv, rw_w_o, rw_w0, rw_w1, rw_w2, rw_a0, rw_a1, rw_a2,
              rw_g1, rw_g2, rw_k_k, rw_k_a, rw_r_k, rw_ln_w, rw_ln_b,
              rw_v0, rw_v1, rw_v2, mlp_w1, mlp_w2):
    c_act = jax.nn.silu(c)
    v_first = None
    for i in range(DEPTH):
        mod = c_act @ ada_w[i] + ada_b[i]
        sh1, sc1, gt1, sh2, sc2, gt2 = jnp.split(mod, N_MOD, axis=-1)
        h = _modulate(_rmsnorm(x, norm_g[i, 0]), sh1, sc1)
        j = i // N_MIXERS
        if i % N_MIXERS == 0:
            y = _short_conv_mixer(h, conv_w_in[j], conv_w[j], conv_w_out[j])
        else:
            vres = None if v_first is None else (rw_v0[j - 1], rw_v1[j - 1], rw_v2[j - 1])
            y, v_first = _rwkv7_mixer(
                h, v_first, vres, rw_mu[j], rw_w_rkv[j], rw_w_o[j], rw_w0[j], rw_w1[j],
                rw_w2[j], rw_a0[j], rw_a1[j], rw_a2[j], rw_g1[j], rw_g2[j], rw_k_k[j],
                rw_k_a[j], rw_r_k[j], rw_ln_w[j], rw_ln_b[j])
        x = x + gt1[:, None, :] * y
        h = _modulate(_rmsnorm(x, norm_g[i, 1]), sh2, sc2)
        x = x + gt2[:, None, :] * (jnp.square(jax.nn.relu(h @ mlp_w1[i])) @ mlp_w2[i])
    return _rmsnorm(x, final_g)


Q_BLOCK = 128
HEAD_DIM = 64
A_HEADS = D_MODEL // HEAD_DIM
A_KV_HEADS = 4
IDX_HEADS = 8
IDX_DIM = 64
TOPK_MAX = 256
B_HEADS = D_MODEL // HEAD_DIM
D_FF_2 = 4 * D_MODEL
ROPE_THETA = 10000.0
EPS = 1e-6
N_A = DEPTH // 2
N_B = DEPTH - N_A

A_Q = A_HEADS * HEAD_DIM
A_KV = A_KV_HEADS * HEAD_DIM
A_QI = IDX_HEADS * IDX_DIM
A_IN = A_Q + 2 * A_KV + A_QI + IDX_DIM + IDX_HEADS
A_SPLITS = [A_Q, A_Q + A_KV, A_Q + 2 * A_KV, A_Q + 2 * A_KV + A_QI, A_Q + 2 * A_KV + A_QI + IDX_DIM]
B_QK = B_HEADS * HEAD_DIM
B_KV_IN = 2 * B_QK + B_HEADS


def rms_norm(x, g):
    x32 = x.astype(jnp.float32)
    y = x32 * lax.rsqrt(jnp.mean(x32 * x32, axis=-1, keepdims=True) + EPS)
    return (y * g.astype(jnp.float32)).astype(x.dtype)

def apply_rope(x):
    s, d = x.shape[1], x.shape[-1]
    half = d // 2
    inv = 1.0 / (ROPE_THETA ** (jnp.arange(0, d, 2, dtype=jnp.float32) / d))
    ang = jnp.arange(s, dtype=jnp.float32)[:, None] * inv[None, :]
    c = jnp.cos(ang)[None, :, None, :]
    sn = jnp.sin(ang)[None, :, None, :]
    x1 = x[..., :half].astype(jnp.float32)
    x2 = x[..., half:].astype(jnp.float32)
    return jnp.concatenate([x1 * c - x2 * sn, x1 * sn + x2 * c], axis=-1).astype(x.dtype)

def to_blocks(a):
    b, s = a.shape[:2]
    return jnp.moveaxis(a.reshape(b, s // Q_BLOCK, Q_BLOCK, *a.shape[2:]), 1, 0)

def from_blocks(a):
    a = jnp.moveaxis(a, 0, 1)
    return a.reshape(a.shape[0], a.shape[1] * a.shape[2], *a.shape[3:])

def dsa_attention(xn, w_in, w_o):
    b, s, _ = xn.shape
    q, k, v, qi, ki, wi = jnp.split(xn @ w_in, A_SPLITS, axis=-1)
    q = apply_rope(q.reshape(b, s, A_HEADS, HEAD_DIM))
    k = apply_rope(k.reshape(b, s, A_KV_HEADS, HEAD_DIM))
    v = v.reshape(b, s, A_KV_HEADS, HEAD_DIM)
    qi = apply_rope(qi.reshape(b, s, IDX_HEADS, IDX_DIM))
    ki = apply_rope(ki[:, :, None, :])[:, :, 0]
    wi = wi * (IDX_HEADS ** -0.5 * IDX_DIM ** -0.5)
    n_sel = min(TOPK_MAX, s // 4)
    key_pos = jnp.arange(s)
    t_pos = key_pos.reshape(s // Q_BLOCK, Q_BLOCK)
    group = A_HEADS // A_KV_HEADS
    scale = HEAD_DIM ** -0.5

    def block(args):
        qb, qib, wib, tb = args
        limit = (tb // CHUNK + 1) * CHUNK
        admissible = key_pos[None, :] < limit[:, None]
        idx_logits = jnp.einsum('bqhd,bsd->bqhs', qib, ki).astype(jnp.float32)
        score = jnp.einsum('bqhs,bqh->bqs', jax.nn.relu(idx_logits), wib.astype(jnp.float32))
        score = jnp.where(admissible[None], score, -jnp.inf)
        _, sel = lax.top_k(score, n_sel)
        valid = sel < limit[None, :, None]
        k_sel = jax.vmap(lambda kk, ii: kk[ii])(k, sel)
        v_sel = jax.vmap(lambda vv, ii: vv[ii])(v, sel)
        qg = qb.reshape(b, Q_BLOCK, A_KV_HEADS, group, HEAD_DIM)
        logits = jnp.einsum('bqngd,bqknd->bqngk', qg, k_sel).astype(jnp.float32) * scale
        logits = jnp.where(valid[:, :, None, None, :], logits, -jnp.inf)
        p = jax.nn.softmax(logits, axis=-1).astype(v.dtype)
        o = jnp.einsum('bqngk,bqknd->bqngd', p, v_sel)
        return o.reshape(b, Q_BLOCK, A_Q)

    o = lax.map(block, (to_blocks(q), to_blocks(qi), to_blocks(wi), t_pos))
    return from_blocks(o) @ w_o

def shared_kv(h, g_kv, w_kv, b_f):
    b, s, _ = h.shape
    k, v, f_logit = jnp.split(rms_norm(h, g_kv) @ w_kv, [B_QK, 2 * B_QK], axis=-1)
    log_f = jax.nn.log_sigmoid((f_logit + b_f).astype(jnp.float32))
    cum = jnp.moveaxis(jnp.cumsum(log_f, axis=1), 2, 1)
    return (k.reshape(b, s, B_HEADS, HEAD_DIM), v.reshape(b, s, B_HEADS, HEAD_DIM), cum)

def fox_attention(xn, w_q, w_o, k, v, cum):
    b, s, _ = xn.shape
    q = (xn @ w_q).reshape(b, s, B_HEADS, HEAD_DIM)
    key_pos = jnp.arange(s)
    t_pos = key_pos.reshape(s // Q_BLOCK, Q_BLOCK)
    cum_q = to_blocks(jnp.moveaxis(cum, 1, 2))
    scale = HEAD_DIM ** -0.5

    def block(args):
        qb, cqb, tb = args
        logits = jnp.einsum('bqhd,bshd->bhqs', qb, k).astype(jnp.float32) * scale
        decay = jnp.moveaxis(cqb, 1, 2)[..., None] - cum[:, :, None, :]
        causal = key_pos[None, :] <= tb[:, None]
        logits = jnp.where(causal[None, None], logits + decay, -jnp.inf)
        p = jax.nn.softmax(logits, axis=-1).astype(v.dtype)
        o = jnp.einsum('bhqs,bshd->bqhd', p, v)
        return o.reshape(b, Q_BLOCK, B_QK)

    o = lax.map(block, (to_blocks(q), cum_q, t_pos))
    return from_blocks(o) @ w_o

def sq_relu_mlp(xn, w_up, w_down):
    return jnp.square(jax.nn.relu(xn @ w_up)) @ w_down

def second_inputs(seed: int = 0) -> dict:
    key = jax.random.key(seed)
    ks = jax.random.split(key, 16)
    f32 = jnp.float32

    def w(k, shape, fan_in):
        return jax.random.normal(k, shape, f32) * (fan_in ** -0.5)

    def gain(k, shape):
        return 1.0 + 0.01 * jax.random.normal(k, shape, f32)

    return {
        "x": jax.random.normal(ks[0], (BATCH, SEQ, D_MODEL), f32),
        "g_attn_a": gain(ks[1], (N_A, D_MODEL)),
        "w_in_a": w(ks[2], (N_A, D_MODEL, A_IN), D_MODEL),
        "w_o_a": w(ks[3], (N_A, A_Q, D_MODEL), A_Q),
        "g_kv": gain(ks[4], (D_MODEL,)),
        "w_kv_b": w(ks[5], (D_MODEL, B_KV_IN), D_MODEL),
        "b_f": jax.random.uniform(ks[6], (B_HEADS,), f32, minval=1.0, maxval=5.0),
        "g_attn_b": gain(ks[7], (N_B, D_MODEL)),
        "w_q_b": w(ks[8], (N_B, D_MODEL, B_QK), D_MODEL),
        "w_o_b": w(ks[9], (N_B, B_QK, D_MODEL), B_QK),
        "g_mlp": gain(ks[10], (DEPTH, D_MODEL)),
        "w_up": w(ks[11], (DEPTH, D_MODEL, D_FF_2), D_MODEL),
        "w_down": w(ks[12], (DEPTH, D_FF_2, D_MODEL), D_FF_2),
        "g_final": gain(ks[13], (D_MODEL,)),
    }

def second_block(x, g_attn_a, w_in_a, w_o_a, g_kv, w_kv_b, b_f, g_attn_b, w_q_b, w_o_b,
              g_mlp, w_up, w_down, g_final):
    h = x
    k_sh = v_sh = cum_sh = None
    for layer in range(DEPTH):
        if layer < N_A:
            h = h + dsa_attention(rms_norm(h, g_attn_a[layer]), w_in_a[layer], w_o_a[layer])
        else:
            if layer == N_A:
                k_sh, v_sh, cum_sh = shared_kv(h, g_kv, w_kv_b, b_f)
            j = layer - N_A
            h = h + fox_attention(rms_norm(h, g_attn_b[j]), w_q_b[j], w_o_b[j], k_sh, v_sh, cum_sh)
        h = h + sq_relu_mlp(rms_norm(h, g_mlp[layer]), w_up[layer], w_down[layer])
    return rms_norm(h, g_final)


def setup_inputs(seed=0):
    out = dict(first_inputs(seed))
    for name, value in second_inputs(seed + 1).items():
        if name != "x":
            out[name + "_2"] = value
    return out


def reference(
    x, c, norm_g, final_g, ada_w, ada_b, conv_w_in, conv_w, conv_w_out, rw_mu, rw_w_rkv, rw_w_o,
    rw_w0, rw_w1, rw_w2, rw_a0, rw_a1, rw_a2, rw_g1, rw_g2, rw_k_k, rw_k_a, rw_r_k, rw_ln_w,
    rw_ln_b, rw_v0, rw_v1, rw_v2, mlp_w1, mlp_w2, g_attn_a_2, w_in_a_2, w_o_a_2, g_kv_2,
    w_kv_b_2, b_f_2, g_attn_b_2, w_q_b_2, w_o_b_2, g_mlp_2, w_up_2, w_down_2, g_final_2,
):
    x = first_block(
        x, c, norm_g, final_g, ada_w, ada_b, conv_w_in, conv_w, conv_w_out, rw_mu, rw_w_rkv,
        rw_w_o, rw_w0, rw_w1, rw_w2, rw_a0, rw_a1, rw_a2, rw_g1, rw_g2, rw_k_k, rw_k_a, rw_r_k,
        rw_ln_w, rw_ln_b, rw_v0, rw_v1, rw_v2, mlp_w1, mlp_w2,
    )
    return second_block(
        x, g_attn_a_2, w_in_a_2, w_o_a_2, g_kv_2, w_kv_b_2, b_f_2, g_attn_b_2, w_q_b_2, w_o_b_2,
        g_mlp_2, w_up_2, w_down_2, g_final_2,
    )


_drawn_inputs = setup_inputs


def setup_inputs(seed=0):
    import zlib

    import numpy as np

    out = dict(_drawn_inputs(seed))
    spreads = {}
    factors = {'rw_w1': 6.603,
     'rw_w2': 5.769,
     'rw_a0': 2.797,
     'rw_a1': 3.127,
     'rw_a2': 2.884,
     'rw_ln_w': 2.964,
     'rw_ln_b': 4.306,
     'g_kv_2': 29.45,
     'g_attn_b_2': 28.976,
     'g_mlp_2': 4.816,
     'g_final_2': 30.468}
    for name, (base, spread) in spreads.items():
        noise = np.random.default_rng([zlib.crc32(name.encode()), seed]).standard_normal(out[name].shape)
        drawn = base * np.exp(spread * noise) if base else spread * noise
        out[name] = __import__('jax').numpy.asarray(drawn.astype(out[name].dtype))
    for name, factor in factors.items():
        out[name] = (out[name] * factor).astype(out[name].dtype)
    return out
```

```python
from contextlib import ExitStack

import concourse.bass as bass
import numpy as np
from concourse import mybir

ALU = mybir.AluOpType
ACT = mybir.ActivationFunctionType
F32 = mybir.dt.float32
F32R = mybir.dt.float32r
AX_X = mybir.AxisListType.X

P = 128
SEQ = 256
D = 1024
KT = D // P
QT = SEQ // P
FF = 4 * D
GROUPS = FF // D
HD = 64
HEADS = D // HD
PAIRS = HEADS // 2
CHUNK = 64
CHUNKS = SEQ // CHUNK
UC = 256
UPD = D // UC
KV_HEADS = 4
IDX_HEADS = 8
TOPK = min(256, SEQ // 4)
RD, RA, RG = 64, 64, 160
DECAY = float(np.exp(-0.5))
NORM_EPS = 1e-6
GN_EPS = 64e-5
NEG = -1e30
TAKEN = -3e38

VEC_ADA_B, VEC_NORM_G, VEC_CONV_W, VEC_MU = 0, 96, 128, 152
VEC_W0, VEC_A0, VEC_KK, VEC_KA, VEC_RK, VEC_LNW, VEC_LNB = 200, 208, 216, 224, 232, 240, 248
VEC_C, VEC_FINAL, VEC_GA, VEC_GKV, VEC_GB, VEC_GMLP, VEC_GFIN = 256, 264, 272, 280, 288, 296, 312
N_VEC = 320

CONST_PARTS = ((("ident", P), ("mean", P), ("ones", P), ("rot", P)),
               (("head_ones", P), ("head_mean", P), ("level_t", 6 * P), ("before", P), ("upto", CHUNK), ("resets", SEQ)),
               (("cos", SEQ), ("sin", SEQ), ("admit", QT * SEQ), ("causal", QT * SEQ)))
CONST_COLS, CONST_AT = {}, [0]
for _part in CONST_PARTS:
    _at = CONST_AT[-1]
    for _name, _n in _part:
        CONST_COLS[_name] = (_at, _at + _n)
        _at += _n
    CONST_AT.append(_at)
N_CONST = CONST_AT[-1]


def constant_table():
    t = np.zeros((P, N_CONST), np.float32)

    def put(name, a):
        lo, hi = CONST_COLS[name]
        t[:, lo:hi] = np.asarray(a, np.float32).reshape(P, hi - lo)

    i = np.arange(P)
    same_head = (i[:, None] // HD) == (i[None, :] // HD)
    put("ident", np.eye(P))
    put("mean", np.full((P, P), 1.0 / D))
    put("ones", np.ones((P, P)))
    put("head_ones", same_head)
    put("head_mean", same_head / HD)
    rot = np.zeros((P, P))
    for m in range(P):
        d = m % HD
        rot[m + HD // 2 if d < HD // 2 else m - HD // 2, m] = -1.0 if d < HD // 2 else 1.0
    put("rot", rot)
    s, q = i[:, None], i[None, :]
    levels = [same_head & (s >> (j + 1) == q >> (j + 1)) & ((q >> j) & 1 == 1) & ((s >> j) & 1 == 0) for j in range(6)]
    put("level_t", np.stack(levels, 1))
    put("before", same_head & (s < q))
    put("upto", (i[:, None] % CHUNK) <= np.arange(CHUNK)[None, :])
    pos = np.arange(SEQ)
    put("resets", np.broadcast_to(pos % CHUNK != 0, (P, SEQ)))
    inv = np.float32(1.0) / (np.float32(10000.0) ** (np.arange(0, HD, 2, dtype=np.float32) / np.float32(HD)))
    ang = inv.astype(np.float32)[:, None] * pos.astype(np.float32)[None, :]
    put("cos", np.tile(np.cos(ang), (4, 1)))
    put("sin", np.tile(np.sin(ang), (4, 1)))
    tok = np.arange(QT)[None, :, None] * P + i[:, None, None]
    put("admit", np.where(pos[None, None, :] < (tok // CHUNK + 1) * CHUNK, 0.0, NEG))
    put("causal", np.where(pos[None, None, :] <= tok, 0.0, NEG))
    return t


def build(nc, A, out):
    with ExitStack() as ctx:
        sems = {}

        def sem(name):
            if name not in sems:
                sems[name] = ctx.enter_context(nc.semaphore(name))
            return sems[name]

        base = (nc.sbuf_base + 63) // 64 * 64
        top = [base]

        def here(nbytes):
            off = top[0]
            top[0] += (nbytes + 63) // 64 * 64
            return off

        def at(name, shape, off, dt=F32):
            return nc.alloc_sbuf_tensor_at(name, shape, dt, offset=off)

        def new(name, shape, dt=F32):
            return at(name, shape, here(4 * int(np.prod(shape[1:]))), dt)

        FM = [P, KT, SEQ]
        FMB = 4 * KT * SEQ
        NSTAGE = 4
        stage = [new(f"stage{i}", [P, KT, UC]) for i in range(NSTAGE)]
        w_hi = [new(f"w_hi{i}", [P, KT, UC], F32R) for i in range(2)]
        w_lo = [new(f"w_lo{i}", [P, KT, UC], F32R) for i in range(2)]
        x = new("x", FM)
        act_off = [here(FMB) for _ in range(4)]
        h_hi, h_lo, z_hi, z_lo = (at(n, FM, o, F32R) for n, o in zip(("h_hi", "h_lo", "z_hi", "z_lo"), act_off))
        tmp = new("tmp", FM)
        sq = new("sq", FM)
        r_off = [here(FMB) for _ in range(6)]
        scr_off = here(26 * 1024)
        part_cols = [CONST_AT[i + 1] - CONST_AT[i] for i in range(3)]
        const_off = [here(4 * part_cols[0])]
        const_off += [here(4 * max(part_cols[1:]))] * 2
        const = [at(f"const{i}", [P, n], o) for i, (n, o) in enumerate(zip(part_cols, const_off))]
        vecT = new("vecT", [P, N_VEC])
        mods = [new(f"mod{i}", [P, 48]) for i in range(2)]
        gain = new("gain", [P, 4, KT])
        small = new("small", [P, 64])
        rstd = new("rstd", [P, 3, SEQ])
        pool_tmp = at("pool_tmp", [P, UC], r_off[5])

        def c_(name):
            lo, hi = CONST_COLS[name]
            i = max(i for i in range(3) if CONST_AT[i] <= lo)
            return const[i][:, lo - CONST_AT[i]:hi - CONST_AT[i]]

        ident, mean_w, ones_w, head_ones, head_mean, rot_w = (c_(n) for n in ("ident", "mean", "ones", "head_ones", "head_mean", "rot"))
        level_t = c_("level_t").rearrange("p (j q) -> p j q", j=6)
        admit = c_("admit").rearrange("p (a s) -> p a s", a=QT)
        causal = c_("causal").rearrange("p (a s) -> p a s", a=QT)

        x_in = at("x_in", [P, QT, D], scr_off)
        vec_in = at("vec_in", [P, 3, P], scr_off + 8192)
        ada_acc = at("ada_acc", [P, 6 * D], r_off[0])
        ada_ring = [at(f"ada_ring{i}", [P, KT, UC], r_off[3 + i]) for i in range(2)]
        c_silu = small[:, 0:8]
        b_gate = at("b_gate", FM, r_off[5])
        PADT = SEQ + 2
        u_pad = at("u_pad", [P, KT, PADT], scr_off)
        conv_y = at("conv_y", [P, 2, SEQ], scr_off + 8320)
        zf = [at(f"zf{i}", [P, 2, SEQ], scr_off + 12 * 1024 + 2048 * i) for i in range(2)]
        relu_b = [at(f"relu{i}", [P, 2, SEQ], scr_off + 16 * 1024 + 2048 * i) for i in range(2)]
        RW = [at(f"rw{i}", FM, r_off[i]) for i in range(6)]
        rw_r, rw_k, rw_v, rw_c, rw_a, rw_kk = RW
        lora1 = at("lora1", [P, KT, RD + RA + RG], scr_off)
        lora_w2 = at("lora_w2", [P, D], scr_off + 9216)
        lora_a2 = lora_w2
        lora_g2a = at("lora_g2a", [P, D], scr_off + 13312)
        lora_g2b = at("lora_g2b", [32, D], scr_off + 17408)
        lora_h = at("lora_h", [P, 4, SEQ], scr_off + 21504)
        mixf = at("mixf", [P, 4, SEQ], r_off[5])
        BD = [P, CHUNKS, P]
        pair_at = [act_off[0]]

        def pair_new(name, shape):
            off = pair_at[0]
            pair_at[0] += 4 * int(np.prod(shape[1:]))
            assert pair_at[0] <= act_off[3] + FMB
            return at(name, shape, off)

        ar = pair_new("ar", [P, CHUNKS, P + CHUNK])
        b_bd, k_bd, v_bd = (pair_new(n, BD) for n in ("b_bd", "k_bd", "v_bd"))
        b_tok, k_tok, v_tok = (pair_new(n, BD) for n in ("b_tok", "k_tok", "v_tok"))
        n_t, n_m, inv_x, inv_t, t1, lak_t = (pair_new(n, BD) for n in ("n_t", "n_m", "inv_x", "inv_t", "t1", "lak_t"))
        lrb_t, lrk_t = (pair_new(n, [P, CHUNKS, CHUNK]) for n in ("lrb_t", "lrk_t"))
        state = [at(f"state{i}", [P, P], scr_off + 1536 * i) for i in range(2)]
        state_kept = at("state_kept", [P, P], scr_off + 10240)
        wkv_rhs = at("wkv_rhs", [P, P], scr_off + 512)
        wkv_u = at("wkv_u", [P, P], scr_off + 1024)
        w_cum = at("w_cum", [P, SEQ], scr_off + 2048)
        w_inv = at("w_inv", [P, SEQ], scr_off + 3072)
        kk_s = at("kk_s", [P, 2, SEQ], scr_off + 4096)
        gn_a = at("gn_a", [P, 2, SEQ], scr_off + 6144)
        gn_b = at("gn_b", [P, 2, SEQ], scr_off + 8192)
        y_wkv, g_wkv = tmp, sq
        q_fm = at("q_fm", FM, r_off[0])
        kA_fm = at("kA_fm", [P, 2, SEQ], r_off[1])
        k_dup = at("k_dup", [P, KV_HEADS, SEQ], r_off[1] + 2048)
        qi_fm = at("qi_fm", [P, 4, SEQ], r_off[2])
        ki_fm = at("ki_fm", [P, 1, SEQ], r_off[2] + 4096)
        vA_tok = at("vA_tok", [P, QT, 256], r_off[2] + 5120)
        kB_fm = at("kB_fm", FM, r_off[1])
        vB_tok = at("vB_tok", [P, QT, D], r_off[2])
        rope_in = [at(f"rope_in{i}", [P, 2, SEQ], r_off[3] + 2048 * i) for i in range(2)]
        rope_c = at("rope_c", [P, 2, SEQ], r_off[3] + 4096)
        sel_bias = at("sel_bias", [P, QT, SEQ], r_off[3] + 6144)
        score = at("score", [P, QT, SEQ], r_off[4])
        score_t = [at(f"score_t{i}", [P, SEQ], r_off[4] + 2048 + 1024 * i) for i in range(2)]
        top8 = at("top8", [P, 8], r_off[4] + 4096)
        wi_tok = at("wi_tok", [P, QT, IDX_HEADS], r_off[4] + 4160)
        cum_k = at("cum_k", [P, HEADS, SEQ], r_off[3])
        f_z = at("f_z", [HEADS, SEQ], scr_off + 10 * 1024)
        f_e = at("f_e", [HEADS, SEQ], scr_off + 11 * 1024)
        f_l = at("f_l", [HEADS, SEQ], scr_off + 16 * 1024)
        f_cum = at("f_cum", [HEADS, SEQ], scr_off + 17 * 1024)
        f_neg = at("f_neg", [HEADS, SEQ], scr_off + 18 * 1024)
        b_f = at("b_f", [HEADS, 1], scr_off + 24 * 1024)
        cum_q = at("cum_q", [P, QT, HEADS], scr_off + 24 * 1024 + 64)
        head_bias = [at(f"head_bias{i}", [P, QT, SEQ], scr_off + 18 * 1024 + 1024 + 2048 * i) for i in range(2)]
        NA = 3
        logit = [at(f"logit{i}", [P, QT, SEQ], r_off[5] + 2048 * i) for i in range(NA)]
        probs = [at(f"probs{i}", [P, QT, SEQ], scr_off + 2048 * i) for i in range(NA)]
        probs_t = [at(f"probs_t{i}", [P, 3, P], scr_off + 6144 + 1536 * i) for i in range(2)]
        stat = [at(f"stat{i}", [P, 8], scr_off + 9344 + 64 * i) for i in range(NA)]
        out_tok = at("out_tok", [P, QT, D], scr_off)
        assert top[0] <= nc.sbuf_usable_end, (top[0], nc.sbuf_usable_end)

        acc = [ctx.enter_context(nc.psum_tensor(f"acc{i}", [P, 2, SEQ], F32)) for i in range(4)]
        un = [ctx.enter_context(nc.psum_tensor(f"un{i}", [P, 2, SEQ], F32)) for i in range(2)]
        stat_ps = ctx.enter_context(nc.psum_tensor("stat_ps", [P, 2, SEQ], F32))
        misc = ctx.enter_context(nc.psum_tensor("misc", [P, 2, SEQ], F32))

        def bank4(b):
            return b[:, :, :].rearrange("p a s -> p (a s)").rearrange("p (c q) -> p c q", c=CHUNKS)

        units = []

        def cols(w, c0, n=UC, r0=0):
            return [(0, n, w[r0:r0 + D, c0:c0 + n].rearrange("(t p) n -> p t n", p=P))]

        def add(sources):
            units.append(sources)
            return len(units) - 1

        def add_dense(w, n):
            first = len(units)
            for j in range(n // UC):
                add(cols(w, j * UC))
            return first

        def add_mlp(w1, w2):
            first = len(units)
            for g in range(GROUPS):
                for j in range(UPD):
                    add(cols(w1, g * D + j * UC))
                for j in range(UPD):
                    add(cols(w2, j * UC, r0=g * D))
            return first

        w_in_a, w_kv = A["w_in_a_2"][0], A["w_kv_b_2"]
        U_CONV_IN = add_dense(A["conv_w_in"][0], 3 * D)
        U_CONV_OUT = add_dense(A["conv_w_out"][0], D)
        U_MLP = [add_mlp(A["mlp_w1"][0], A["mlp_w2"][0])]
        U_RWK = add_dense(A["rw_w_rkv"][0, 1], D)
        U_RWR = add_dense(A["rw_w_rkv"][0, 0], D)
        U_RWV = add_dense(A["rw_w_rkv"][0, 2], D)
        U_RWO = add_dense(A["rw_w_o"][0], D)
        U_MLP.append(add_mlp(A["mlp_w1"][1], A["mlp_w2"][1]))
        A_K, A_V, A_QI, A_KI = D, D + 256, D + 512, D + 1024
        KI_COLS = HD + HD + IDX_HEADS
        U_KI = add([(0, HD, cols(w_in_a, A_KI, HD)[0][2]), (HD, KI_COLS, cols(w_in_a, A_KI, HD + IDX_HEADS)[0][2])])
        U_QI = add(cols(w_in_a, A_QI))
        add(cols(w_in_a, A_QI + UC))
        U_KA = add(cols(w_in_a, A_K))
        U_VA = add(cols(w_in_a, A_V))
        U_QA = len(units)
        for j in range(UPD):
            add(cols(w_in_a, j * UC))
        U_OA = add_dense(A["w_o_a_2"][0], D)
        U_MLP.append(add_mlp(A["w_up_2"][0], A["w_down_2"][0]))
        U_F = add([(0, HEADS, cols(w_kv, 2 * D, HEADS)[0][2]), (HEADS, P, cols(w_kv, 0, P - HEADS)[0][2])])
        U_KB = len(units)
        for j in range(2 * UPD):
            add(cols(w_kv, j * UC))
        U_VB = U_KB + UPD
        U_QB = add_dense(A["w_q_b_2"][0], D)
        U_OB = add_dense(A["w_o_b_2"][0], D)
        U_MLP.append(add_mlp(A["w_up_2"][1], A["w_down_2"][1]))
        NU = len(units)

        def unit_cols(u):
            return max(hi for _, hi, _ in units[u])

        V_VEC, V_X, V_CONV = 0, 1, 5
        V_MLP = [17]
        V_RKV = V_MLP[0] + 16
        V_MLP.append(V_RKV + 12)
        V_A = V_MLP[1] + 16
        V_MLP.append(V_A + 9)
        V_B = V_MLP[2] + 16
        V_MLP.append(V_B + 13)
        V_OUT = V_MLP[3] + 16
        Z_CONV, Z_MLP0, Z_RW, Z_MLP1, Z_A, Z_MLP2, Z_B, Z_MLP3 = 0, 4, 20, 24, 40, 44, 60, 64
        Z_MLP = [Z_MLP0, Z_MLP1, Z_MLP2, Z_MLP3]
        N_CONV, N_MLP0, N_RW, N_MLP1, N_FIN1, N_A, N_MLP2, N_B, N_MLP3, N_OUT = range(10)
        N_MLP = [N_MLP0, N_MLP1, N_MLP2, N_MLP3]
        H_BASE = {N_CONV: 0, N_MLP0: 8, N_MLP1: 16, N_A: 24, N_MLP2: 32, N_B: 40, "B_q": 48, N_MLP3: 56}
        ROPE_KI, ROPE_QI, ROPE_K, ROPE_Q, N_ROPE = 0, 1, 3, 4, 8

        const_in, const_b_in, x_loaded, vec_loaded, lora_loaded, bf_loaded = (sem(n) for n in ("const_in", "const_b_in", "x_loaded", "vec_loaded", "lora_loaded", "bf_loaded"))
        landed = [sem(f"unit_landed{i}") for i in range(NSTAGE)]
        hi_made, lo_made, unit_done, un_free = (sem(n) for n in ("hi_made", "lo_made", "unit_done", "un_free"))
        VEC_DMAS = 19

        def freed(v):
            return v + 1 if v < V_X else v - 3

        block = ctx.enter_context(nc.Block())

        @block.sync
        def _(sp):
            for i in range(2):
                sp.dma_start(const[i][:], A["const_table"][:, CONST_AT[i]:CONST_AT[i + 1]]).then_inc(const_in, 16)
            sp.dma_start(x_in[:], A["x"][0].rearrange("(a p) d -> p a d", p=P)).then_inc(x_loaded, 16)

            def rows(tile, r0, ap, n):
                sp.dma_start(vec_in[r0:r0 + n, tile, :], ap).then_inc(vec_loaded, 16)

            flat = lambda ap, n: ap.rearrange("(r q) -> r q", q=P)
            rows(0, 0, flat(A["ada_b"][0], 48), 48)
            rows(0, 48, flat(A["ada_b"][1], 48), 48)
            rows(0, 96, A["norm_g"].rearrange("a b (r q) -> (a b r) q", q=P), 32)
            rows(1, 0, A["conv_w"][0].rearrange("a (r q) -> (a r) q", q=P), 24)
            rows(1, 24, A["rw_mu"][0].rearrange("a (r q) -> (a r) q", q=P), 48)
            for r0, name in ((72, "rw_w0"), (80, "rw_a0"), (88, "rw_k_k"), (96, "rw_k_a"), (112, "rw_ln_w"), (120, "rw_ln_b")):
                rows(1, r0, flat(A[name][0], 8), 8)
            rows(1, 104, A["rw_r_k"][0].rearrange("(r a) d -> r (a d)", a=2), 8)
            rows(2, 0, flat(A["c"][0], 8), 8)
            rows(2, 8, flat(A["final_g"], 8), 8)
            rows(2, 16, flat(A["g_attn_a_2"][0], 8), 8)
            rows(2, 24, flat(A["g_kv_2"], 8), 8)
            rows(2, 32, flat(A["g_attn_b_2"][0], 8), 8)
            rows(2, 40, A["g_mlp_2"].rearrange("a (r q) -> (a r) q", q=P), 16)
            rows(2, 56, flat(A["g_final_2"], 8), 8)

            def load_unit(u):
                if u >= NSTAGE:
                    sp.wait_ge(lo_made, u - NSTAGE + 1)
                for lo, hi, src in units[u]:
                    sp.dma_start(stage[u % NSTAGE][:, :, lo:hi], src).then_inc(landed[u % NSTAGE], 32 // len(units[u]))

            for u in range(NU):
                if u == U_RWK + NSTAGE:
                    sp.wait_ge(sem("x_ready"), 8 * N_RW + 8)
                    sp.dma_start(lora1[:, :, 0:RD], A["rw_w1"][0].rearrange("(t p) n -> p t n", p=P)).then_inc(lora_loaded, 16)
                    sp.dma_start(lora1[:, :, RD:RD + RA], A["rw_a1"][0].rearrange("(t p) n -> p t n", p=P)).then_inc(lora_loaded, 16)
                    sp.dma_start(lora1[:, :, RD + RA:], A["rw_g1"][0].rearrange("(t p) n -> p t n", p=P)).then_inc(lora_loaded, 16)
                    sp.dma_start(lora_w2[0:RD, :], A["rw_w2"][0]).then_inc(lora_loaded, 16)
                    sp.dma_start(lora_w2[RD:RD + RA, :], A["rw_a2"][0]).then_inc(lora_loaded, 16)
                    sp.dma_start(lora_g2a[:, :], A["rw_g2"][0, 0:P, :]).then_inc(lora_loaded, 16)
                    sp.dma_start(lora_g2b[:, :], A["rw_g2"][0, P:RG, :]).then_inc(lora_loaded, 16)
                if u == U_MLP[1] + UPD:
                    sp.wait_ge(sem("x_ready"), 8 * N_MLP1 + 8)
                    sp.dma_start(const[2][:], A["const_table"][:, CONST_AT[2]:]).then_inc(const_b_in, 16)
                if u == U_F:
                    sp.wait_ge(sem("x_ready"), 8 * N_MLP2 + 8)
                    sp.dma_start(b_f[:], A["b_f_2"].rearrange("(h a) -> h a", a=1)).then_inc(bf_loaded, 16)
                load_unit(u)
            out_v = out[0].rearrange("(a p) d -> p a d", p=P)
            sp.wait_ge(un_free, freed(V_OUT + 3))
            sp.dma_start(out_v, out_tok[:]).then_inc(sem("stored"), 16)
            sp.wait_ge(sem("stored"), 16)

        ada_landed = [sem("ada_landed0"), sem("ada_landed1")]
        ada_free, ada_acc_ready, ada_summed = sem("ada_free"), sem("ada_acc_ready"), sem("ada_summed")
        N_ADA = 6 * D // UC

        @block.gpsimd
        def _(pool):
            chain = sem("pool_chain")
            count = [0]

            def link(ins):
                count[0] += 1
                ins.then_inc(chain, 1)
                pool.wait_ge(chain, count[0])

            def load_ada(a):
                if a >= 2:
                    pool.wait_ge(ada_free, a - 1)
                pool.dma_start(ada_ring[a % 2][:], cols(A["ada_w"][a // N_ADA], a % N_ADA * UC)[0][2]).then_inc(ada_landed[a % 2], 16)

            for a in range(N_ADA + 2):
                load_ada(a)
            pool.wait_ge(sem("silu_ready"), 1)
            pool.wait_ge(ada_summed, 4)
            for a in range(N_ADA, 2 * N_ADA):
                pool.wait_ge(ada_landed[a % 2], 16 * (a // 2 + 1))
                ring = ada_ring[a % 2]
                dst = ada_acc[:, a % N_ADA * UC:(a % N_ADA + 1) * UC]
                link(nc.gpsimd.tensor_scalar(dst, ring[:, 0, :], c_silu[:, 0:1], None, ALU.mult))
                for t in range(1, KT):
                    link(nc.gpsimd.tensor_scalar(pool_tmp[:], ring[:, t, :], c_silu[:, t:t + 1], None, ALU.mult))
                    if t < KT - 1:
                        link(nc.gpsimd.tensor_tensor(dst, dst, pool_tmp[:], ALU.add))
                nc.gpsimd.tensor_tensor(dst, dst, pool_tmp[:], ALU.add).then_inc(ada_free, 1)
                if a + 2 < 2 * N_ADA:
                    load_ada(a + 2)

            for i in range(HEADS):
                if i == 0:
                    pool.wait_ge(const_b_in, 16)
                    pool.wait_ge(sem("cumk_ready"), 8)
                if i >= 2:
                    pool.wait_ge(sem("max_ready"), HEADS + i - 1)
                nc.gpsimd.tensor_tensor(head_bias[i % 2][:], causal, cum_k[:, i, :].unsqueeze(1).to_broadcast([P, QT, SEQ]), ALU.add)\
                    .then_inc(sem("bias_ready"), 1)

        tp_done, x_ready = sem("tp_done"), sem("x_ready")
        sq_ready, stat_done, ms_ready, std_ready = (sem(n) for n in ("sq_ready", "stat_done", "ms_ready", "std_ready"))
        normed, h_hi_made, h_lo_made = (sem(n) for n in ("normed", "h_hi_made", "h_lo_made"))
        zf_ready, z_hi_made, z_lo_made, relu_ready = (sem(n) for n in ("zf_ready", "z_hi_made", "z_lo_made", "relu_ready"))
        lora_mixed, lora1_done, lora1_out, lora2_done, lora2_out = (sem(n) for n in ("lora_mixed", "lora1_done", "lora1_out", "lora2_done", "lora2_out"))
        mix_ready, mix_hi, mix_lo = (sem(n) for n in ("mix_ready", "mix_hi", "mix_lo"))
        kk0_ready, kksq_ready, ss_done, ss_ready, ss_root = (sem(n) for n in ("kk0_ready", "kksq_ready", "ss_done", "ss_ready", "ss_root"))
        cum_ready, exp_ready, built = (sem(n) for n in ("cum_ready", "exp_ready", "built"))
        g_done, tok_done, tok_out, masks_ready, inv_ready = (sem(n) for n in ("g_done", "tok_done", "tok_out", "masks_ready", "inv_ready"))
        x1_done, x1_out, nm_ready, t1_done, t1_out, dx_done = (sem(n) for n in ("x1_done", "x1_out", "nm_ready", "t1_done", "t1_out", "dx_done"))
        rhs_done, rhs_out, u_done, u_out, y_done, y_out, s_done, state_ready = (
            sem(n) for n in ("rhs_done", "rhs_out", "u_done", "u_out", "y_done", "y_out", "s_done", "state_ready"))
        rk_ready, gn_mean_done, yc_ready, ycsq_ready, gn_var_done, gv_ready, gv_root, bonus_done = (
            sem(n) for n in ("rk_ready", "gn_mean_done", "yc_ready", "ycsq_ready", "gn_var_done", "gv_ready", "gv_root", "bonus_done"))
        rot_done, rope_done, ki_loaded, kdup_ready = (sem(n) for n in ("rot_done", "rope_done", "ki_loaded", "kdup_ready"))
        score_done, score_used = sem("score_done"), sem("score_used")
        f_abs, f_exp, f_one, f_log, f_ready, f_bcast, cumk_ready, cumq_ready = (
            sem(n) for n in ("f_abs", "f_exp", "f_one", "f_log", "f_ready", "f_bcast", "cumk_ready", "cumq_ready"))
        qk_done, max_ready, exp_done, p_ready, pt_done, pt_out, pv_done = (
            sem(n) for n in ("qk_done", "max_ready", "exp_done", "p_ready", "pt_done", "pt_out", "pv_done"))
        silu_e, silu_ready, ada_summed_pe = sem("silu_e"), sem("silu_ready"), sem("ada_summed_pe")

        @block.scalar
        def _(act):
            A_ = nc.scalar.activation

            def split(u):
                if u >= NU:
                    return
                n = unit_cols(u)
                act.wait_ge(landed[u % NSTAGE], 32 * (u // NSTAGE + 1))
                if u >= 2:
                    act.wait_ge(unit_done, u - 1)
                A_(w_hi[u % 2][:, :, 0:n], stage[u % NSTAGE][:, :, 0:n], ACT.Copy).then_inc(hi_made, 1)

            def norm_stats(n):
                for t in range(KT):
                    act.wait_ge(x_ready, 8 * n + t + 1)
                    if t == 0 and n:
                        act.wait_ge(stat_done, n)
                    A_(sq[:, t, :], x[:, t, :], ACT.Square).then_inc(sq_ready, 1)
                act.wait_ge(ms_ready, n + 1)
                A_(rstd[:, 1, :], rstd[:, 0, :], ACT.Sqrt).then_inc(std_ready, 1)

            def norm_split(base, hi, shift):
                for t in range(KT):
                    act.wait_ge(normed, base + t + 1)
                    if shift is None:
                        A_(hi[:, t, :], tmp[:, t, :], ACT.Copy).then_inc(h_hi_made, 1)
                    else:
                        A_(hi[:, t, :], tmp[:, t, :], ACT.Identity, bias=shift[:, t:t + 1]).then_inc(h_hi_made, 1)

            def z_split(zc, j):
                act.wait_ge(zf_ready, zc + 1)
                A_(z_hi[:, 2 * j:2 * j + 2, :], zf[zc % 2][:], ACT.Copy).then_inc(z_hi_made, 1)

            def evac(u, v, dst, scale=1.0):
                act.wait_ge(unit_done, u + 1)
                A_(dst, un[v % 2][:], ACT.Copy, scale=scale).then_inc(un_free, 1)

            def mlp(m):
                u, v, zc = U_MLP[m], V_MLP[m], Z_MLP[m]
                for g in range(GROUPS):
                    for j in range(UPD):
                        uu = u + 2 * UPD * g + j
                        act.wait_ge(unit_done, uu + 1)
                        A_(relu_b[j % 2][:], un[(v + j) % 2][:], ACT.Relu).then_inc(relu_ready, 1)
                        if j < UPD - 1:
                            split(uu + 2)
                            z_split(zc + UPD * g + j, j)
                        else:
                            z_split(zc + UPD * g + j, j)
                            split(uu + 2)
                    for j in range(UPD):
                        split(u + 2 * UPD * g + UPD + j + 2)

            act.wait_ge(un_free, freed(V_VEC))
            A_(small[:, 8:16], vecT[:, VEC_C:VEC_C + KT], ACT.Exp, scale=-1.0).then_inc(silu_e, 1)
            norm_stats(N_CONV)
            split(0)
            split(1)
            norm_split(H_BASE[N_CONV], h_hi, mods[0][:, 0:8])
            for j in range(12):
                if j < 8:
                    dst = (b_gate if j < 4 else tmp)[:, 2 * (j % 4):2 * (j % 4) + 2, :]
                    evac(U_CONV_IN + j, V_CONV + j, dst)
                split(U_CONV_IN + j + 2)
                if j >= 8:
                    z_split(Z_CONV + j - 8, j - 8)
            for j in range(UPD):
                split(U_CONV_OUT + j + 2)
            norm_stats(N_MLP0)
            norm_split(H_BASE[N_MLP0], h_hi, mods[0][:, 24:32])
            mlp(0)
            norm_stats(N_RW)
            mix_dst = (h_hi, z_hi, h_hi)

            def mix_split(m):
                act.wait_ge(mix_ready, m + 1)
                A_(mix_dst[m // KT][:, m % KT, :], mixf[:, m % 4, :], ACT.Copy).then_inc(mix_hi, 1)

            for m in range(2 * KT):
                mix_split(m)
            act.wait_ge(lora1_done, 1)
            A_(lora_h[0:RD, 0, :], acc[0][0:RD, 0, :], ACT.Tanh).then_inc(lora1_out, 1)
            act.wait_ge(lora1_done, 2)
            A_(lora_h[RD:RD + RA, 1, :], acc[1][RD:RD + RA, 0, :], ACT.Copy).then_inc(lora1_out, 1)
            act.wait_ge(lora1_done, 3)
            A_(lora_h[:, 2, :], acc[2][:, 0, :], ACT.Sigmoid).then_inc(lora1_out, 1)
            A_(lora_h[0:RG - P, 3, :], acc[3][0:RG - P, 0, :], ACT.Sigmoid).then_inc(lora1_out, 1)
            for which, (dst, vec) in enumerate(((rw_c, VEC_W0), (rw_a, VEC_A0))):
                for t in range(KT):
                    if t % 2 == 0:
                        act.wait_ge(lora2_done, 4 * which + t // 2 + 1)
                    A_(dst[:, t, :], acc[t // 2][:, t % 2, :], ACT.Sigmoid, bias=vecT[:, vec + t:vec + t + 1]).then_inc(lora2_out, 1)
            for j in range(12):
                dst = (rw_k, rw_r, rw_v)[j // 4]
                evac(U_RWK + j, V_RKV + j, dst[:, 2 * (j % 4):2 * (j % 4) + 2, :])
                split(U_RWK + j + 2)
                if j == 3:
                    for m in range(2 * KT, 3 * KT):
                        mix_split(m)
            for j in range(4):
                act.wait_ge(kk0_ready, j + 1)
                A_(tmp[:, 2 * j:2 * j + 2, :], rw_kk[:, 2 * j:2 * j + 2, :], ACT.Square).then_inc(kksq_ready, 1)
            for j in range(4):
                act.wait_ge(ss_ready, j + 1)
                A_(tmp[:, 2 * j:2 * j + 2, :], tmp[:, 2 * j:2 * j + 2, :], ACT.Sqrt).then_inc(ss_root, 1)
            for j in range(4):
                act.wait_ge(lora2_done, 8 + j + 1)
                A_(g_wkv[:, 2 * j:2 * j + 2, :], acc[j][:], ACT.Copy).then_inc(lora2_out, 1)
            act.wait_ge(cum_ready, 1)
            for p in range(PAIRS):
                if p:
                    act.wait_ge(y_out, CHUNKS * p)
                A_(w_cum[:], rw_c[:, p, :], ACT.Exp, scale=-DECAY).then_inc(exp_ready, 1)
                A_(w_inv[:], rw_c[:, p, :], ACT.Exp, scale=DECAY).then_inc(exp_ready, 1)
                for n, (dst, src) in enumerate(((v_tok, stat_ps), (b_tok, misc), (k_tok, un[0]))):
                    act.wait_ge(tok_done, 3 * p + n + 1)
                    A_(dst[:], bank4(src), ACT.Copy).then_inc(tok_out, 1)
                act.wait_ge(x1_done, p + 1)
                A_(inv_x[:], bank4(un[1]), ACT.Copy).then_inc(x1_out, 1)
                for j in range(1, 6):
                    act.wait_ge(t1_done, 5 * p + j)
                    A_(t1[:], bank4(acc[0]), ACT.Copy).then_inc(t1_out, 1)
                for c in range(CHUNKS):
                    i = CHUNKS * p + c
                    act.wait_ge(rhs_done, i + 1)
                    A_(wkv_rhs[:], acc[3][:, 0, 0:P], ACT.Copy).then_inc(rhs_out, 1)
                    act.wait_ge(u_done, i + 1)
                    A_(wkv_u[:], stat_ps[:, 0, 0:P], ACT.Copy).then_inc(u_out, 1)
            for j in range(4):
                act.wait_ge(yc_ready, j + 1)
                A_(rw_kk[:, 2 * j:2 * j + 2, :], y_wkv[:, 2 * j:2 * j + 2, :], ACT.Square).then_inc(ycsq_ready, 1)
            for j in range(4):
                act.wait_ge(gv_ready, j + 1)
                A_(rw_kk[:, 2 * j:2 * j + 2, :], rw_kk[:, 2 * j:2 * j + 2, :], ACT.Sqrt).then_inc(gv_root, 1)
            for j in range(4):
                z_split(Z_RW + j, j)
            for j in range(UPD):
                split(U_RWO + j + 2)
            norm_stats(N_MLP1)
            norm_split(H_BASE[N_MLP1], h_hi, mods[1][:, 24:32])
            mlp(1)
            norm_stats(N_FIN1)

            def attention(kind, z0):
                b = HEADS * kind
                for i in range(HEADS + 6):
                    if i < HEADS:
                        act.wait_ge(max_ready, b + i + 1)
                        if b + i >= NA:
                            act.wait_ge(pt_done, b + i - NA + 1)
                        for qt in range(QT):
                            A_(probs[i % NA][:, qt, :], logit[i % NA][:, qt, :], ACT.Exp, bias=stat[i % NA][:, qt:qt + 1],
                               accum_out=stat[i % NA][:, 2 + qt:3 + qt]).then_inc(exp_done, 1)
                    if 2 <= i < HEADS + 2:
                        k = i - 2
                        act.wait_ge(pt_done, b + k + 1)
                        if b + k >= 2:
                            act.wait_ge(pv_done, b + k - 1)
                        A_(probs_t[k % 2][:], (stat_ps, misc)[k % 2][:, :, :].rearrange("p a s -> p (a s)")[:, 0:3 * P]
                           .rearrange("p (c q) -> p c q", c=3), ACT.Copy).then_inc(pt_out, 1)
                    if i >= 9 and (i - 9) % 4 == 0:
                        z_split(z0 + (i - 9) // 4, (i - 9) // 4)

            norm_stats(N_A)
            norm_split(H_BASE[N_A], h_hi, None)

            def rope_load(u, v, r, n, scale=1.0, signal=None):
                act.wait_ge(unit_done, u + 1)
                if r >= 2:
                    act.wait_ge(rope_done, r - 1)
                A_(rope_in[r % 2][:, 0:n, :], un[v % 2][:, 0:n, :], ACT.Copy, scale=scale).then_inc(signal or un_free, 1)

            rope_load(U_KI, V_A, ROPE_KI, 1, signal=ki_loaded)
            split(U_KI + 2)
            act.wait_ge(un_free, freed(V_A))
            for j in range(2):
                rope_load(U_QI + j, V_A + 1 + j, ROPE_QI + j, 2)
                split(U_QI + j + 2)
            rope_load(U_KA, V_A + 3, ROPE_K, 2)
            split(U_KA + 2)
            evac(U_VA, V_A + 4, vA_tok[:])
            split(U_VA + 2)
            act.wait_ge(rope_done, ROPE_K + 1)
            for j in range(KV_HEADS):
                src = kA_fm[HD * (j % 2):HD * (j % 2) + HD, j // 2, :]
                A_(k_dup[0:HD, j, :], src, ACT.Copy)
                A_(k_dup[HD:P, j, :], src, ACT.Copy).then_inc(kdup_ready, 1)
            for j in range(UPD):
                rope_load(U_QA + j, V_A + 5 + j, ROPE_Q + j, 2, scale=HD ** -0.5)
                split(U_QA + j + 2)
            attention(0, Z_A)
            for j in range(UPD):
                split(U_OA + j + 2)
            norm_stats(N_MLP2)
            norm_split(H_BASE[N_MLP2], h_hi, None)
            mlp(2)
            norm_stats(N_B)
            norm_split(H_BASE[N_B], h_hi, None)
            norm_split(H_BASE["B_q"], z_hi, None)
            split(U_F + 2)
            act.wait_ge(f_abs, 1)
            A_(f_l[:], f_e[:], ACT.Exp, scale=-1.0).then_inc(f_exp, 1)
            act.wait_ge(f_one, 1)
            A_(f_l[:], f_l[:], ACT.Ln).then_inc(f_log, 1)
            for j in range(UPD):
                evac(U_KB + j, V_B + 1 + j, kB_fm[:, 2 * j:2 * j + 2, :])
                split(U_KB + j + 2)
            for r in range(8):
                act.wait_ge(f_bcast, r + 1)
                A_(cum_k[:, 2 * r:2 * r + 2, :], acc[r % 4][:], ACT.Copy).then_inc(cumk_ready, 1)
            for j in range(UPD):
                evac(U_VB + j, V_B + 5 + j, vB_tok[:, :, UC * j:UC * (j + 1)])
                split(U_VB + j + 2)
            for j in range(UPD):
                evac(U_QB + j, V_B + 9 + j, q_fm[:, 2 * j:2 * j + 2, :], scale=HD ** -0.5)
                split(U_QB + j + 2)
            attention(1, Z_B)
            for j in range(UPD):
                split(U_OB + j + 2)
            norm_stats(N_MLP3)
            norm_split(H_BASE[N_MLP3], h_hi, None)
            mlp(3)
            norm_stats(N_OUT)

        @block.vector
        def _(dve):
            V = nc.vector
            chain = sem("dve_chain")
            count = [0]

            def link(ins):
                count[0] += 1
                ins.then_inc(chain, 1)
                dve.wait_ge(chain, count[0])

            def split(u):
                if u >= NU:
                    return
                n = unit_cols(u)
                dve.wait_ge(hi_made, u + 1)
                V.tensor_tensor(w_lo[u % 2][:, :, 0:n], stage[u % NSTAGE][:, :, 0:n], w_hi[u % 2][:, :, 0:n].bitcast(F32),
                                ALU.subtract).then_inc(lo_made, 1)

            def norm_stats(n):
                dve.wait_ge(stat_done, n + 1)
                V.tensor_scalar(rstd[:, 0, :], stat_ps[:, 0, :], NORM_EPS, None, ALU.add).then_inc(ms_ready, 1)
                dve.wait_ge(std_ready, n + 1)
                link(V.reciprocal(rstd[:, 2, :], rstd[:, 1, :]))
                link(V.tensor_tensor(rstd[:, 1, :], rstd[:, 2, :], rstd[:, 2, :], ALU.mult))
                link(V.tensor_tensor(rstd[:, 1, :], rstd[:, 1, :], rstd[:, 0, :], ALU.mult))
                link(V.tensor_scalar(rstd[:, 1, :], rstd[:, 1, :], -0.5, 1.5, ALU.mult, ALU.add))
                link(V.tensor_tensor(rstd[:, 2, :], rstd[:, 2, :], rstd[:, 1, :], ALU.mult))

            def norm_mul(dst, t, g):
                return V.scalar_tensor_tensor(out=dst[:, t, :], in0=x[:, t, :], scalar=g[:, t:t + 1], in1=rstd[:, 2, :],
                                              op0=ALU.mult, op1=ALU.mult)

            def norm_split(base, g, shift, hi, lo):
                for t in range(KT + 2):
                    if t < KT:
                        norm_mul(tmp, t, g).then_inc(normed, 1)
                    if t >= 2:
                        k = t - 2
                        dve.wait_ge(h_hi_made, base + k + 1)
                        if shift is None:
                            ins = V.tensor_tensor(lo[:, k, :], tmp[:, k, :], hi[:, k, :].bitcast(F32), ALU.subtract)
                        else:
                            ins = V.scalar_tensor_tensor(out=lo[:, k, :], in0=tmp[:, k, :], scalar=shift[:, k:k + 1],
                                                         in1=hi[:, k, :].bitcast(F32), op0=ALU.add, op1=ALU.subtract)
                        ins.then_inc(h_lo_made, 1)

            def z_split(zc, j):
                dve.wait_ge(z_hi_made, zc + 1)
                V.tensor_tensor(z_lo[:, 2 * j:2 * j + 2, :], zf[zc % 2][:], z_hi[:, 2 * j:2 * j + 2, :].bitcast(F32),
                                ALU.subtract).then_inc(z_lo_made, 1)

            def residual(u, gate, j, b):
                dve.wait_ge(unit_done, u + 1)
                for m in range(2):
                    t = 2 * j + m
                    if gate is None:
                        ins = V.tensor_tensor(x[:, t, :], b[:, m, :], x[:, t, :], ALU.add)
                    else:
                        ins = V.scalar_tensor_tensor(out=x[:, t, :], in0=b[:, m, :], scalar=gate[:, t:t + 1], in1=x[:, t, :],
                                                     op0=ALU.mult, op1=ALU.add)
                    ins.then_inc(x_ready, 1)

            def mlp(m, gate):
                u, v, zc = U_MLP[m], V_MLP[m], Z_MLP[m]
                for g in range(GROUPS):
                    for j in range(UPD):
                        uu = u + 2 * UPD * g + j
                        k = zc + UPD * g + j
                        dve.wait_ge(relu_ready, 4 * GROUPS * m + UPD * g + j + 1)
                        V.scalar_tensor_tensor(out=zf[k % 2][:], in0=un[(v + j) % 2][:], scalar=0.0, in1=relu_b[j % 2][:],
                                               op0=ALU.max, op1=ALU.mult).then_inc(zf_ready, 1)
                        dve.wait_ge(zf_ready, k + 1)
                        V.engine_nop().then_inc(un_free, 1)
                        if j < UPD - 1:
                            split(uu + 2)
                            z_split(k, j)
                        else:
                            z_split(k, j)
                            split(uu + 2)
                    for j in range(UPD):
                        split(u + 2 * UPD * g + UPD + j + 2)
                        if g == GROUPS - 1:
                            residual(u + 2 * UPD * g + UPD + j, gate, j, acc[j])

            dve.wait_ge(tp_done, 1)
            V.tensor_copy(vecT[:], un[0][:, :, :].rearrange("p a s -> p (a s)")[:, 0:N_VEC]).then_inc(un_free, 1)
            for j in range(4):
                dve.wait_ge(tp_done, 2 + j)
                V.tensor_copy(x[:, 2 * j:2 * j + 2, :], un[(V_X + j) % 2][:]).then_inc(x_ready, 2)
            dve.wait_ge(silu_e, 1)
            link(V.tensor_scalar(small[:, 16:24], small[:, 8:16], 1.0, None, ALU.add))
            link(V.reciprocal(small[:, 24:32], small[:, 16:24]))
            V.tensor_tensor(c_silu, vecT[:, VEC_C:VEC_C + KT], small[:, 24:32], ALU.mult).then_inc(silu_ready, 1)
            dve.wait_ge(silu_ready, 1)
            norm_stats(N_CONV)

            def ada(a):
                dve.wait_ge(ada_landed[a % 2], 16 * (a // 2 + 1))
                dst = ada_acc[:, a * UC:(a + 1) * UC]
                link(V.tensor_scalar(dst, ada_ring[a % 2][:, 0, :], c_silu[:, 0:1], None, ALU.mult))
                for t in range(1, KT):
                    ins = V.scalar_tensor_tensor(out=dst, in0=ada_ring[a % 2][:, t, :], scalar=c_silu[:, t:t + 1], in1=dst,
                                                 op0=ALU.mult, op1=ALU.add)
                    if t < KT - 1:
                        link(ins)
                    else:
                        ins.then_inc(ada_free, 1)

            def mod_out(layer, c0, c1, k):
                dve.wait_ge(ada_summed_pe, k)
                V.tensor_tensor(mods[layer][:, c0:c1], misc[:, 0, c0:c1], vecT[:, VEC_ADA_B + 48 * layer + c0:VEC_ADA_B + 48 * layer + c1],
                                ALU.add).then_inc(ada_summed, 1)
                dve.wait_ge(ada_summed, k)

            def mod_gain(layer, sub):
                link(V.scalar_tensor_tensor(out=gain[:, 2 * layer + sub, :], in0=mods[layer][:, 24 * sub + 8:24 * sub + 16], scalar=1.0,
                                            in1=vecT[:, VEC_NORM_G + 8 * (2 * layer + sub):VEC_NORM_G + 8 * (2 * layer + sub) + 8],
                                            op0=ALU.add, op1=ALU.mult))

            for a in range(8):
                ada(a)
            split(0)
            split(1)
            mod_out(0, 0, 16, 1)
            mod_gain(0, 0)
            norm_split(H_BASE[N_CONV], gain[:, 0, :], mods[0][:, 0:8], h_hi, h_lo)
            link(V.memset(u_pad[:, :, 0:2], 0.0))
            conv_w = [vecT[:, VEC_CONV_W + 8 * k:VEC_CONV_W + 8 * k + 8] for k in range(3)]
            for j in range(12):
                if j < 8:
                    split(U_CONV_IN + j + 2)
                else:
                    k = j - 8
                    t0 = 2 * k
                    dve.wait_ge(unit_done, U_CONV_IN + j + 1)
                    dve.wait_ge(un_free, freed(V_CONV + 7))
                    V.tensor_tensor(u_pad[:, t0:t0 + 2, 2:PADT], un[(V_CONV + j) % 2][:], tmp[:, t0:t0 + 2, :], ALU.mult).then_inc(un_free, 1)
                    dve.wait_ge(un_free, freed(V_CONV + j))
                    for m in range(2):
                        ins = V.tensor_scalar(conv_y[:, m, :], u_pad[:, t0 + m, 2:PADT], conv_w[2][:, t0 + m:t0 + m + 1], None, ALU.mult)
                    link(ins)
                    for tap in (1, 0):
                        for m in range(2):
                            ins = V.scalar_tensor_tensor(out=conv_y[:, m, :], in0=u_pad[:, t0 + m, tap:tap + SEQ],
                                                         scalar=conv_w[tap][:, t0 + m:t0 + m + 1], in1=conv_y[:, m, :],
                                                         op0=ALU.mult, op1=ALU.add)
                        link(ins)
                    V.tensor_tensor(zf[(Z_CONV + k) % 2][:], conv_y[:], b_gate[:, t0:t0 + 2, :], ALU.mult).then_inc(zf_ready, 1)
                    split(U_CONV_IN + j + 2)
                    z_split(Z_CONV + k, k)
                ada(8 + j)
            mod_out(0, 16, 24, 2)
            for j in range(UPD):
                split(U_CONV_OUT + j + 2)
                residual(U_CONV_OUT + j, mods[0][:, 16:24], j, acc[j])
                ada(20 + j)
            norm_stats(N_MLP0)
            mod_out(0, 24, 40, 3)
            mod_gain(0, 1)
            norm_split(H_BASE[N_MLP0], gain[:, 1, :], mods[0][:, 24:32], h_hi, h_lo)
            mod_out(0, 40, 48, 4)
            mlp(0, mods[0][:, 40:48])
            norm_stats(N_RW)
            mod_out(1, 0, 48, 5)
            mod_gain(1, 0)
            mod_gain(1, 1)
            for t in range(KT):
                ins = norm_mul(tmp, t, gain[:, 2, :])
            link(ins)
            for t in range(KT):
                ins = V.tensor_scalar(tmp[:, t, :], tmp[:, t, :], mods[1][:, t:t + 1], None, ALU.add)
            link(ins)
            V.tensor_tensor(sq[:, :, 1:SEQ], tmp[:, :, 0:SEQ - 1], tmp[:, :, 1:SEQ], ALU.subtract)
            link(V.tensor_scalar(sq[:, :, 0:1], tmp[:, :, 0:1], -1.0, None, ALU.mult))

            def mix(dst, t, which):
                c = VEC_MU + 8 * which + t
                return V.scalar_tensor_tensor(out=dst, in0=sq[:, t, :], scalar=vecT[:, c:c + 1], in1=tmp[:, t, :], op0=ALU.mult, op1=ALU.add)

            for dst, which in ((rw_r, 1), (rw_k, 4), (rw_v, 5)):
                for t in range(KT):
                    ins = mix(dst[:, t, :], t, which)
                ins.then_inc(lora_mixed, 1)
            mix_dst = ((h_hi, h_lo), (z_hi, z_lo), (h_hi, h_lo))
            mix_mu = (2, 0, 3)

            def mixes(m0, m1):
                for m in range(m0, m1 + 2):
                    if m < m1:
                        if m >= 4:
                            dve.wait_ge(mix_lo, m - 3)
                        mix(mixf[:, m % 4, :], m % KT, mix_mu[m // KT]).then_inc(mix_ready, 1)
                    if m - 2 >= m0:
                        k = m - 2
                        hi, lo = mix_dst[k // KT]
                        dve.wait_ge(mix_hi, k + 1)
                        V.tensor_tensor(lo[:, k % KT, :], mixf[:, k % 4, :], hi[:, k % KT, :].bitcast(F32), ALU.subtract).then_inc(mix_lo, 1)

            mixes(0, 2 * KT)
            dve.wait_ge(lora2_out, 8)
            for t in range(KT):
                ins = V.tensor_tensor_scan(rw_c[:, t, :], c_("resets"), rw_c[:, t, :], 0.0, ALU.mult, ALU.add)
            ins.then_inc(cum_ready, 1)
            for j in range(12):
                if j == 4:
                    dve.wait_ge(unit_done, U_RWK + 4)
                    mixes(2 * KT, 3 * KT)
                split(U_RWK + j + 2)
            dve.wait_ge(un_free, freed(V_RKV + 3))
            for j in range(4):
                for t in (2 * j, 2 * j + 1):
                    ins = V.tensor_scalar(rw_kk[:, t, :], rw_k[:, t, :], vecT[:, VEC_KK + t:VEC_KK + t + 1], None, ALU.mult)
                ins.then_inc(kk0_ready, 1)
            for j in range(4):
                dve.wait_ge(ss_done, j + 1)
                V.tensor_scalar(tmp[:, 2 * j:2 * j + 2, :], acc[j][:], 1e-24, None, ALU.max).then_inc(ss_ready, 1)
            for j in range(4):
                dve.wait_ge(ss_root, j + 1)
                ins = V.reciprocal(tmp[:, 2 * j:2 * j + 2, :], tmp[:, 2 * j:2 * j + 2, :])
            link(ins)
            link(V.tensor_tensor(rw_kk[:], rw_kk[:], tmp[:], ALU.mult))
            dve.wait_ge(lora2_out, 16)
            for t in range(KT):
                ins = V.tensor_scalar(tmp[:, t, :], rw_a[:, t, :], -1.0, vecT[:, VEC_KA + t:VEC_KA + t + 1], ALU.add, ALU.mult)
            link(ins)
            V.scalar_tensor_tensor(out=rw_k[:], in0=tmp[:], scalar=1.0, in1=rw_k[:], op0=ALU.add, op1=ALU.mult)
            link(V.tensor_tensor(rw_a[:], rw_a[:], rw_kk[:], ALU.mult))
            dve.wait_ge(unit_done, U_RWV + 4)
            V.memset(ar[:], 0.0)
            V.memset(b_bd[:], 0.0)
            V.memset(k_bd[:], 0.0)
            link(V.memset(v_bd[:], 0.0))
            dve.wait_ge(un_free, freed(V_RKV + 11))
            halves = ((0, HD), (HD, P))
            bc4 = lambda m, n: m.unsqueeze(1).to_broadcast([P, n, m.shape[-1]])
            for p in range(PAIRS):
                dve.wait_ge(exp_ready, 2 * p + 2)
                ch = lambda t, lo, hi: t[lo:hi, p, :].rearrange("p (c s) -> p c s", c=CHUNKS)
                wc = w_cum[:].rearrange("p (c s) -> p c s", c=CHUNKS)
                wi = w_inv[:].rearrange("p (c s) -> p c s", c=CHUNKS)
                V.tensor_tensor(ar[:, :, P:P + CHUNK], ch(rw_r, 0, P), wc, ALU.mult)
                for h, (lo, hi) in enumerate(halves):
                    o = CHUNK * h
                    kkh = ch(rw_kk, lo, hi)
                    V.tensor_scalar(ar[lo:hi, :, o:o + 1], kkh[:, :, 0:1], -1.0, None, ALU.mult)
                    V.scalar_tensor_tensor(out=ar[lo:hi, :, o + 1:o + CHUNK], in0=kkh[:, :, 1:CHUNK], scalar=-1.0,
                                           in1=wc[lo:hi, :, 0:CHUNK - 1], op0=ALU.mult, op1=ALU.mult)
                    V.tensor_tensor(b_bd[lo:hi, :, o:o + CHUNK], ch(rw_a, lo, hi), wi[lo:hi], ALU.mult)
                    V.tensor_tensor(k_bd[lo:hi, :, o:o + CHUNK], ch(rw_k, lo, hi), wi[lo:hi], ALU.mult)
                    ins = V.tensor_copy(v_bd[lo:hi, :, o:o + CHUNK], ch(rw_v, lo, hi))
                ins.then_inc(built, 1)
                dve.wait_ge(g_done, p + 1)
                for k in range(2):
                    ins = V.tensor_tensor(n_t[:, 2 * k:2 * k + 2, :], acc[k][:, :, 0:P], bc4(c_("before"), 2), ALU.mult)
                link(ins)
                link(V.tensor_tensor(inv_t[:], n_t[:], bc4(level_t[:, 0, :], CHUNKS), ALU.mult))
                V.tensor_tensor(inv_t[:], inv_t[:], bc4(ident, CHUNKS), ALU.add).then_inc(inv_ready, 1)
                for k in range(2):
                    V.tensor_tensor(lak_t[:, 2 * k:2 * k + 2, :], acc[2 + k][:, :, 0:P], bc4(c_("before"), 2), ALU.mult)
                    V.tensor_tensor(lrb_t[:, 2 * k:2 * k + 2, :], acc[k][:, :, P:P + CHUNK], bc4(c_("upto"), 2), ALU.mult)
                    ins = V.tensor_tensor(lrk_t[:, 2 * k:2 * k + 2, :], acc[2 + k][:, :, P:P + CHUNK], bc4(c_("upto"), 2), ALU.mult)
                ins.then_inc(masks_ready, 1)
                for j in range(1, 6):
                    V.tensor_tensor(n_m[:], n_t[:], bc4(level_t[:, j, :], CHUNKS), ALU.mult).then_inc(nm_ready, 1)
                    if j == 1:
                        dve.wait_ge(x1_out, p + 1)
                    dve.wait_ge(dx_done, 5 * p + j)
                    if j < 5:
                        V.tensor_tensor(inv_x[:], bank4(acc[1]), inv_x[:], ALU.add)
                    V.tensor_tensor(inv_t[:], bank4(acc[2]), inv_t[:], ALU.add).then_inc(inv_ready, 1)
                for c in range(CHUNKS):
                    i = CHUNKS * p + c
                    last = w_cum[:, CHUNK * c + CHUNK - 1:CHUNK * c + CHUNK]
                    if c < CHUNKS - 1:
                        k = (CHUNKS - 1) * p + c
                        if c:
                            dve.wait_ge(state_ready, k)
                            link(V.tensor_scalar(state_kept[:], state[(c - 1) % 2][:], last, None, ALU.mult))
                        dve.wait_ge(s_done, k + 1)
                        if c == 0:
                            V.tensor_scalar(state[0][:], un[0][:, 0, 0:P], last, None, ALU.mult).then_inc(state_ready, 1)
                        else:
                            V.scalar_tensor_tensor(out=state[c % 2][:], in0=un[0][:, 0, 0:P], scalar=last, in1=state_kept[:],
                                                   op0=ALU.mult, op1=ALU.add).then_inc(state_ready, 1)
                    dve.wait_ge(y_done, i + 1)
                    V.tensor_copy(y_wkv[:, p, CHUNK * c:CHUNK * (c + 1)], misc[:, 0, 0:CHUNK]).then_inc(y_out, 1)
            for t in range(KT):
                ins = V.scalar_tensor_tensor(out=rw_c[:, t, :], in0=rw_r[:, t, :], scalar=vecT[:, VEC_RK + t:VEC_RK + t + 1],
                                             in1=rw_k[:, t, :], op0=ALU.mult, op1=ALU.mult)
            ins.then_inc(rk_ready, 1)
            bonus_bank = (stat_ps, misc, un[0], un[1])
            for j in range(4):
                s2 = slice(2 * j, 2 * j + 2)
                dve.wait_ge(gn_mean_done, j + 1)
                V.tensor_tensor(y_wkv[:, s2, :], y_wkv[:, s2, :], acc[j][:], ALU.subtract).then_inc(yc_ready, 1)
            for j in range(4):
                s2 = slice(2 * j, 2 * j + 2)
                dve.wait_ge(gn_var_done, j + 1)
                V.tensor_scalar(rw_kk[:, s2, :], acc[j][:], GN_EPS, None, ALU.add).then_inc(gv_ready, 1)
            for j in range(4):
                s2 = slice(2 * j, 2 * j + 2)
                dve.wait_ge(gv_root, j + 1)
                link(V.reciprocal(rw_kk[:, s2, :], rw_kk[:, s2, :]))
                link(V.tensor_tensor(y_wkv[:, s2, :], y_wkv[:, s2, :], rw_kk[:, s2, :], ALU.mult))
                for t in (2 * j, 2 * j + 1):
                    V.tensor_scalar(y_wkv[:, t, :], y_wkv[:, t, :], vecT[:, VEC_LNW + t:VEC_LNW + t + 1], vecT[:, VEC_LNB + t:VEC_LNB + t + 1],
                                    ALU.mult, ALU.add)
                dve.wait_ge(bonus_done, j + 1)
                link(V.tensor_tensor(rw_v[:, s2, :], bonus_bank[j][:], rw_v[:, s2, :], ALU.mult))
                link(V.tensor_tensor(y_wkv[:, s2, :], y_wkv[:, s2, :], rw_v[:, s2, :], ALU.add))
                V.tensor_tensor(zf[(Z_RW + j) % 2][:], y_wkv[:, s2, :], g_wkv[:, s2, :], ALU.mult).then_inc(zf_ready, 1)
                if j:
                    z_split(Z_RW + j - 1, j - 1)
            z_split(Z_RW + 3, 3)
            for j in range(UPD):
                split(U_RWO + j + 2)
                residual(U_RWO + j, mods[1][:, 16:24], j, acc[j])
            norm_stats(N_MLP1)
            norm_split(H_BASE[N_MLP1], gain[:, 3, :], mods[1][:, 24:32], h_hi, h_lo)
            mlp(1, mods[1][:, 40:48])
            norm_stats(N_FIN1)
            for t in range(KT):
                norm_mul(x, t, vecT[:, VEC_FINAL:VEC_FINAL + KT]).then_inc(x_ready, 1)

            def rope(r, n, dst):
                dve.wait_ge(rot_done, r + 1)
                V.tensor_tensor(rope_c[:, 0:n, :], rope_in[r % 2][:, 0:n, :], bc4(c_("cos"), n), ALU.mult)
                link(V.tensor_tensor(dst, misc[:, 0:n, :], bc4(c_("sin"), n), ALU.mult))
                V.tensor_tensor(dst, dst, rope_c[:, 0:n, :], ALU.add).then_inc(rope_done, 1)

            def attention(kind, z0):
                b = HEADS * kind
                for i in range(HEADS + 6):
                    if i < HEADS:
                        lg, st = logit[i % NA], stat[i % NA]
                        dve.wait_ge(qk_done, b + i + 1)
                        if kind == 0:
                            link(V.tensor_tensor(lg[:], acc[i % 4][:], sel_bias[:], ALU.add))
                        else:
                            dve.wait_ge(sem("bias_ready"), i + 1)
                            for qt in range(QT):
                                ins = V.scalar_tensor_tensor(out=lg[:, qt, :], in0=acc[i % 4][:, qt, :], scalar=cum_q[:, qt, i:i + 1],
                                                             in1=head_bias[i % 2][:, qt, :], op0=ALU.add, op1=ALU.add)
                            link(ins)
                        V.tensor_reduce(st[:, 0:QT], lg[:], AX_X, ALU.max, negate=True).then_inc(max_ready, 1)
                    if 1 <= i <= HEADS:
                        k = i - 1
                        st = stat[k % NA]
                        dve.wait_ge(exp_done, QT * (b + k + 1))
                        link(V.reciprocal(st[:, 4:4 + QT], st[:, 2:2 + QT]))
                        for qt in range(QT):
                            ins = V.tensor_scalar(probs[k % NA][:, qt, :], probs[k % NA][:, qt, :], st[:, 4 + qt:5 + qt], None, ALU.mult)
                        ins.then_inc(p_ready, 1)
                    if i >= 7 and (i - 7) % 4 == 0:
                        j = (i - 7) // 4
                        dve.wait_ge(pv_done, b + 4 * j + 4)
                        V.tensor_copy(zf[(z0 + j) % 2][:], un[j % 2][:]).then_inc(zf_ready, 1)
                    if i >= 9 and (i - 9) % 4 == 0:
                        z_split(z0 + (i - 9) // 4, (i - 9) // 4)

            norm_stats(N_A)
            norm_split(H_BASE[N_A], vecT[:, VEC_GA:VEC_GA + KT], None, h_hi, h_lo)
            dve.wait_ge(const_b_in, 16)
            dve.wait_ge(ki_loaded, 1)
            V.tensor_scalar(wi_tok[:], un[V_A % 2][:, 1, 0:QT * IDX_HEADS].rearrange("p (a h) -> p a h", a=QT),
                            IDX_HEADS ** -0.5 * HD ** -0.5, None, ALU.mult).then_inc(un_free, 1)

            def scores(qt):
                dve.wait_ge(score_done, qt + 1)
                dst = score[:, qt, :]
                for h in range(IDX_HEADS):
                    b, o = acc[2 * (h // 4) + h % 2], h // 2 % 2
                    w = wi_tok[:, qt, h:h + 1]
                    if h == 0:
                        link(V.tensor_scalar(dst, b[:, o, :], 0.0, w, ALU.max, ALU.mult))
                    else:
                        link(V.tensor_scalar(score_t[h % 2][:], b[:, o, :], 0.0, w, ALU.max, ALU.mult))
                        ins = V.tensor_tensor(dst, dst, score_t[h % 2][:], ALU.add)
                        if h < IDX_HEADS - 1:
                            link(ins)
                        else:
                            ins.then_inc(score_used, 1)
                dve.wait_ge(score_used, qt + 1)
                link(V.tensor_tensor(dst, dst, admit[:, qt, :], ALU.add))

            def select(qt):
                w = score[:, qt, :]
                for _ in range(TOPK // 8):
                    link(V.max(top8[:], w))
                    link(V.match_replace(w, top8[:], w, TAKEN))
                link(V.tensor_scalar(sel_bias[:, qt, :], w, 0.5 * TAKEN, NEG, ALU.is_gt, ALU.mult))

            split(U_KI + 2)
            split(U_QI + 2)
            rope(ROPE_KI, 1, ki_fm[:])
            split(U_QI + 3)
            rope(ROPE_QI, 2, qi_fm[:, 0:2, :])
            split(U_KA + 2)
            rope(ROPE_QI + 1, 2, qi_fm[:, 2:4, :])
            split(U_VA + 2)
            rope(ROPE_K, 2, kA_fm[:])
            scores(0)
            split(U_QA + 2)
            scores(1)
            split(U_QA + 3)
            rope(ROPE_Q, 2, q_fm[:, 0:2, :])
            select(0)
            split(U_QA + 4)
            rope(ROPE_Q + 1, 2, q_fm[:, 2:4, :])
            select(1)
            split(U_QA + 5)
            rope(ROPE_Q + 2, 2, q_fm[:, 4:6, :])
            rope(ROPE_Q + 3, 2, q_fm[:, 6:8, :])
            attention(0, Z_A)
            for j in range(UPD):
                split(U_OA + j + 2)
                residual(U_OA + j, None, j, acc[j])
            norm_stats(N_MLP2)
            norm_split(H_BASE[N_MLP2], vecT[:, VEC_GMLP:VEC_GMLP + KT], None, h_hi, h_lo)
            mlp(2, None)
            norm_stats(N_B)
            norm_split(H_BASE[N_B], vecT[:, VEC_GKV:VEC_GKV + KT], None, h_hi, h_lo)
            norm_split(H_BASE["B_q"], vecT[:, VEC_GB:VEC_GB + KT], None, z_hi, z_lo)
            split(U_F + 2)
            dve.wait_ge(unit_done, U_F + 1)
            dve.wait_ge(bf_loaded, 16)
            V.tensor_scalar(f_z[:], un[V_B % 2][0:HEADS, 0, :], b_f[:, 0:1], None, ALU.add).then_inc(un_free, 1)
            dve.wait_ge(un_free, freed(V_B))
            V.scalar_tensor_tensor(out=f_e[:], in0=f_z[:], scalar=-1.0, in1=f_z[:], op0=ALU.mult, op1=ALU.max).then_inc(f_abs, 1)
            dve.wait_ge(f_exp, 1)
            V.tensor_scalar(f_l[:], f_l[:], 1.0, None, ALU.add).then_inc(f_one, 1)
            dve.wait_ge(f_log, 1)
            link(V.scalar_tensor_tensor(out=f_e[:], in0=f_z[:], scalar=0.0, in1=f_l[:], op0=ALU.min, op1=ALU.subtract))
            link(V.tensor_tensor_scan(f_cum[:], ones_w[0:HEADS, 0:1].to_broadcast([HEADS, SEQ]), f_e[:], 0.0, ALU.mult, ALU.add))
            V.tensor_scalar(f_neg[:], f_cum[:], -1.0, None, ALU.mult).then_inc(f_ready, 1)
            for j in range(2 * UPD):
                split(U_KB + j + 2)
                if j == UPD:
                    dve.wait_ge(cumq_ready, 1)
                    link(V.tensor_copy(cum_q[:], misc[:, 0, 0:QT * HEADS].rearrange("p (a h) -> p a h", a=QT)))
            for j in range(UPD):
                split(U_QB + j + 2)
            attention(1, Z_B)
            for j in range(UPD):
                split(U_OB + j + 2)
                residual(U_OB + j, None, j, acc[j])
            norm_stats(N_MLP3)
            norm_split(H_BASE[N_MLP3], vecT[:, VEC_GMLP + KT:VEC_GMLP + 2 * KT], None, h_hi, h_lo)
            mlp(3, None)
            norm_stats(N_OUT)
            for t in range(KT):
                norm_mul(tmp, t, vecT[:, VEC_GFIN:VEC_GFIN + KT]).then_inc(normed, 1)
            for k in range(4):
                dve.wait_ge(tp_done, 5 + k + 1)
                V.tensor_copy(out_tok[:, k // 2, 512 * (k % 2):512 * (k % 2) + 512],
                              un[(V_OUT + k) % 2][:, :, :].rearrange("p a s -> p (a s)")).then_inc(un_free, 1)

        @block.tensor
        def _(pe):
            MM = nc.tensor.matmul

            def three(out, hi_l, lo_l, hi_r, lo_r, start, stop):
                MM(out, hi_l, hi_r, start=start, stop=False, skip_group_check=True)
                MM(out, hi_l, lo_r, start=False, stop=False, skip_group_check=True)
                return MM(out, lo_l, hi_r, start=False, stop=stop, skip_group_check=True)

            def free_bank(v):
                if v >= V_CONV + 2:
                    pe.wait_ge(un_free, freed(v - 2))

            def unit(u, bank, xs, ready=None, tokens=False, first=True, last=True):
                xh, xl = xs
                wh, wl = w_hi[u % 2], w_lo[u % 2]
                pe.wait_ge(lo_made, u + 1)
                for kt in range(KT):
                    if ready is not None:
                        ready(kt)
                    for m in range(2):
                        s = first and kt == 0 and m == 0
                        if tokens:
                            q = slice(P * m, P * m + P)
                            ins = three(bank[:, m, :], xh[:, kt, q], xl[:, kt, q], wh[:, kt, :], wl[:, kt, :], s, last and kt == KT - 1)
                        else:
                            c = slice(P * m, P * m + P)
                            ins = three(bank[:, m, :], wh[:, kt, c], wl[:, kt, c], xh[:, kt, :], xl[:, kt, :], s, last and kt == KT - 1)
                ins.then_inc(unit_done, 1)

            def norm_stats(n):
                for t in range(KT):
                    pe.wait_ge(sq_ready, 8 * n + t + 1)
                    if t == 0 and n:
                        pe.wait_ge(ms_ready, n)
                    ins = MM(stat_ps[:, 0, :], mean_w, sq[:, t, :], start=(t == 0), stop=(t == KT - 1))
                ins.then_inc(stat_done, 1)

            def h_ready(base):
                return lambda kt: pe.wait_ge(h_lo_made, base + kt + 1)

            def z_ready(zc):
                return lambda kt: pe.wait_ge(z_lo_made, zc + kt // 2 + 1) if kt % 2 == 0 else None

            def mlp(m, n):
                u, v, zc = U_MLP[m], V_MLP[m], Z_MLP[m]
                for g in range(GROUPS):
                    for j in range(UPD):
                        free_bank(v + UPD * g + j)
                        unit(u + 2 * UPD * g + j, un[(v + j) % 2], (h_hi, h_lo), h_ready(H_BASE[n]) if g == 0 and j == 0 else None)
                    for j in range(UPD):
                        unit(u + 2 * UPD * g + UPD + j, acc[j], (z_hi, z_lo), z_ready(zc + UPD * g) if j == 0 else None,
                             first=(g == 0), last=(g == GROUPS - 1))

            pe.wait_ge(const_in, 32)
            pe.wait_ge(vec_loaded, 16 * VEC_DMAS)
            flat0 = un[0][:, :, :].rearrange("p a s -> p (a s)")
            for i, n in enumerate((P, P, N_VEC - 2 * P)):
                ins = nc.tensor.transpose(flat0[:, P * i:P * i + n], vec_in[0:n, i, :], ident[0:n, 0:n])
            ins.then_inc(tp_done, 1)
            pe.wait_ge(x_loaded, 16)
            for j in range(4):
                if j == 1:
                    pe.wait_ge(un_free, freed(V_VEC))
                if j >= 2:
                    pe.wait_ge(x_ready, 2 * (j - 1))
                for m in range(2):
                    for a in range(QT):
                        ins = nc.tensor.transpose(un[(V_X + j) % 2][:, m, P * a:P * a + P], x_in[:, a, P * (2 * j + m):P * (2 * j + m) + P], ident)
                ins.then_inc(tp_done, 1)

            def ada_sum(c0, c1, k):
                if k > 1:
                    pe.wait_ge(ada_summed, k - 1)
                for c in range(c0, c1):
                    ins = MM(misc[:, 0, c:c + 1], ada_acc[:, P * c:P * c + P], ones_w[:, 0:1], start=True, stop=True)
                ins.then_inc(ada_summed_pe, 1)

            norm_stats(N_CONV)
            pe.wait_ge(ada_free, 8)
            ada_sum(0, 16, 1)
            for j in range(12):
                free_bank(V_CONV + j)
                unit(U_CONV_IN + j, un[(V_CONV + j) % 2], (h_hi, h_lo), h_ready(H_BASE[N_CONV]) if j == 0 else None)
            pe.wait_ge(ada_free, 12)
            ada_sum(16, 24, 2)
            for j in range(UPD):
                unit(U_CONV_OUT + j, acc[j], (z_hi, z_lo), z_ready(Z_CONV) if j == 0 else None)
            norm_stats(N_MLP0)
            pe.wait_ge(ada_free, 20)
            ada_sum(24, 40, 3)
            pe.wait_ge(ada_free, 24)
            ada_sum(40, 48, 4)
            mlp(0, N_MLP0)
            norm_stats(N_RW)
            pe.wait_ge(ada_free, 2 * N_ADA)
            ada_sum(0, 48, 5)
            pe.wait_ge(lora_loaded, 16 * 7)
            for n, (src, c0, c1, out) in enumerate(((rw_r, 0, RD, acc[0][0:RD, 0, :]), (rw_k, RD, RD + RA, acc[1][RD:RD + RA, 0, :]),
                                                    (rw_v, RD + RA, RD + RA + P, acc[2][:, 0, :]),
                                                    (rw_v, RD + RA + P, RD + RA + RG, acc[3][0:RG - P, 0, :]))):
                pe.wait_ge(lora_mixed, min(n, 2) + 1)
                for t in range(KT):
                    ins = MM(out, lora1[:, t, c0:c1], src[:, t, :], start=(t == 0), stop=(t == KT - 1))
                if n != 2:
                    ins.then_inc(lora1_done, 1)
            for which, (rows_, w) in enumerate(((slice(0, RD), lora_w2), (slice(RD, RD + RA), lora_a2))):
                pe.wait_ge(lora1_out, 4)
                for t in range(KT):
                    if which and t % 2 == 0:
                        pe.wait_ge(lora2_out, t + 2)
                    ins = MM(acc[t // 2][:, t % 2, :], w[rows_, P * t:P * t + P], lora_h[rows_, which, :], start=True, stop=True)
                    if t % 2:
                        ins.then_inc(lora2_done, 1)

            def mix_done(m0):
                return lambda kt: pe.wait_ge(mix_lo, m0 + kt + 1)

            for j in range(12):
                free_bank(V_RKV + j)
                unit(U_RWK + j, un[(V_RKV + j) % 2], ((h_hi, h_lo), (z_hi, z_lo), (h_hi, h_lo))[j // 4],
                     mix_done(KT * (j // 4)) if j % 4 == 0 else None)
            pe.wait_ge(lora2_out, 16)
            for j in range(4):
                pe.wait_ge(kksq_ready, j + 1)
                for m in range(2):
                    ins = MM(acc[j][:, m, :], head_ones, tmp[:, 2 * j + m, :], start=True, stop=True)
                ins.then_inc(ss_done, 1)
            for t in range(KT):
                if t % 2 == 0:
                    pe.wait_ge(ss_ready, t // 2 + 1)
                MM(acc[t // 2][:, t % 2, :], lora_g2a[:, P * t:P * t + P], lora_h[:, 2, :], start=True, stop=False)
                ins = MM(acc[t // 2][:, t % 2, :], lora_g2b[:, P * t:P * t + P], lora_h[0:RG - P, 3, :], start=False, stop=True)
                if t % 2:
                    ins.then_inc(lora2_done, 1)
            pe.wait_ge(lora2_out, 20)
            pe.wait_ge(un_free, freed(V_RKV + 11))
            for p in range(PAIRS):
                pe.wait_ge(built, p + 1)
                for k, lhs in enumerate((b_bd, k_bd)):
                    for c in range(CHUNKS):
                        ins = MM(acc[2 * k + c // 2][:, c % 2, 0:P + CHUNK], lhs[:, c, :], ar[:, c, :], start=True, stop=True)
                ins.then_inc(g_done, 1)
                for src, dst in ((v_bd, stat_ps), (b_bd, misc), (k_bd, un[0])):
                    for c in range(CHUNKS):
                        ins = nc.tensor.transpose(bank4(dst)[:, c, :], src[:, c, :], ident)
                    ins.then_inc(tok_done, 1)
                pe.wait_ge(inv_ready, 6 * p + 1)
                for c in range(CHUNKS):
                    ins = nc.tensor.transpose(bank4(un[1])[:, c, :], inv_t[:, c, :], ident)
                ins.then_inc(x1_done, 1)
                pe.wait_ge(masks_ready, p + 1)
                pe.wait_ge(x1_out, p + 1)
                for j in range(1, 6):
                    pe.wait_ge(nm_ready, 5 * p + j)
                    pe.wait_ge(inv_ready, 6 * p + j)
                    for c in range(CHUNKS):
                        ins = MM(bank4(acc[0])[:, c, :], n_m[:, c, :], inv_x[:, c, :], start=True, stop=True)
                    ins.then_inc(t1_done, 1)
                    pe.wait_ge(t1_out, 5 * p + j)
                    if j < 5:
                        for c in range(CHUNKS):
                            MM(bank4(acc[1])[:, c, :], inv_t[:, c, :], t1[:, c, :], start=True, stop=True)
                    for c in range(CHUNKS):
                        ins = MM(bank4(acc[2])[:, c, :], t1[:, c, :], inv_t[:, c, :], start=True, stop=True)
                    ins.then_inc(dx_done, 1)
                pe.wait_ge(inv_ready, 6 * p + 6)
                pe.wait_ge(tok_out, 3 * p + 3)
                for c in range(CHUNKS):
                    i = CHUNKS * p + c
                    k = (CHUNKS - 1) * p + c
                    if c:
                        pe.wait_ge(state_ready, k)
                        MM(acc[3][:, 0, 0:P], ar[:, c, 0:P], state[(c - 1) % 2][:], start=True, stop=False)
                    MM(acc[3][:, 0, 0:P], lak_t[:, c, :], v_tok[:, c, :], start=(c == 0), stop=True).then_inc(rhs_done, 1)
                    pe.wait_ge(rhs_out, i + 1)
                    MM(stat_ps[:, 0, 0:P], inv_t[:, c, :], wkv_rhs[:], start=True, stop=True).then_inc(u_done, 1)
                    pe.wait_ge(u_out, i + 1)
                    if c < CHUNKS - 1:
                        MM(un[0][:, 0, 0:P], b_tok[:, c, :], wkv_u[:], start=True, stop=False)
                        MM(un[0][:, 0, 0:P], k_tok[:, c, :], v_tok[:, c, :], start=False, stop=True).then_inc(s_done, 1)
                    if i:
                        pe.wait_ge(y_out, i)
                    y = misc[:, 0, 0:CHUNK]
                    if c:
                        MM(y, state[(c - 1) % 2][:], ar[:, c, P:P + CHUNK], start=True, stop=False)
                    MM(y, wkv_u[:], lrb_t[:, c, :], start=(c == 0), stop=False)
                    MM(y, v_tok[:, c, :], lrk_t[:, c, :], start=False, stop=True).then_inc(y_done, 1)
            pe.wait_ge(y_out, CHUNKS * PAIRS)
            for j in range(4):
                for m in range(2):
                    ins = MM(acc[j][:, m, :], head_mean, y_wkv[:, 2 * j + m, :], start=True, stop=True)
                ins.then_inc(gn_mean_done, 1)
            pe.wait_ge(rk_ready, 1)
            for j, b in enumerate((stat_ps, misc, un[0], un[1])):
                for m in range(2):
                    ins = MM(b[:, m, :], head_ones, rw_c[:, 2 * j + m, :], start=True, stop=True)
                ins.then_inc(bonus_done, 1)
            for j in range(4):
                pe.wait_ge(ycsq_ready, j + 1)
                for m in range(2):
                    ins = MM(acc[j][:, m, :], head_mean, rw_kk[:, 2 * j + m, :], start=True, stop=True)
                ins.then_inc(gn_var_done, 1)
            for j in range(UPD):
                unit(U_RWO + j, acc[j], (z_hi, z_lo), z_ready(Z_RW) if j == 0 else None)
            norm_stats(N_MLP1)
            mlp(1, N_MLP1)
            norm_stats(N_FIN1)

            def rot(r, n, v):
                pe.wait_ge(un_free, freed(v))
                if r:
                    pe.wait_ge(rope_done, r)
                MM(misc[:, 0:n, :], rot_w, rope_in[r % 2][:, 0:n, :], start=True, stop=True).then_inc(rot_done, 1)

            def attention(kind, k_of, v_of):
                b = HEADS * kind
                for i in range(-2, HEADS + 1):
                    k = i + 2
                    if k < HEADS:
                        lo = HD * (k % 2)
                        if k >= 4:
                            pe.wait_ge(max_ready, b + k - 3)
                        if kind == 0:
                            pe.wait_ge(rope_done, ROPE_Q + k // 4 + 1)
                        for qt in range(QT):
                            ins = MM(acc[k % 4][:, qt, :], q_fm[lo:lo + HD, k // 2, P * qt:P * qt + P], k_of(k), start=True, stop=True)
                        ins.then_inc(qk_done, 1)
                    if 0 <= i < HEADS:
                        pe.wait_ge(p_ready, b + i + 1)
                        if i >= 2:
                            pe.wait_ge(pt_out, b + i - 1)
                        dst = (stat_ps, misc)[i % 2][:, :, :].rearrange("p a s -> p (a s)")
                        for n, (qt, st) in enumerate(((0, 0), (1, 0), (1, 1))):
                            ins = nc.tensor.transpose(dst[:, P * n:P * n + P], probs[i % NA][:, qt, P * st:P * st + P], ident)
                        ins.then_inc(pt_done, 1)
                    if i >= 1:
                        h = i - 1
                        lo = HD * (h % 2)
                        pe.wait_ge(pt_out, b + h + 1)
                        if h % 4 == 0 and h >= 8:
                            pe.wait_ge(zf_ready, (Z_A, Z_B)[kind] + h // 4 - 1)
                        o = un[h // 4 % 2][lo:lo + HD, h // 2 % 2, :]
                        pt = probs_t[h % 2]
                        MM(o[:, 0:P], v_of(h, 0), pt[:, 0, :], start=True, stop=True, skip_group_check=True)
                        MM(o[:, P:2 * P], v_of(h, 0), pt[:, 1, :], start=True, stop=False, skip_group_check=True)
                        MM(o[:, P:2 * P], v_of(h, 1), pt[:, 2, :], start=False, stop=True, skip_group_check=True).then_inc(pv_done, 1)

            norm_stats(N_A)
            h_tiles = (h_hi, h_lo)
            free_bank(V_A)
            pe.wait_ge(lo_made, U_KI + 1)
            wh, wl = w_hi[U_KI % 2], w_lo[U_KI % 2]
            bank = un[V_A % 2]
            for kt in range(KT):
                pe.wait_ge(h_lo_made, H_BASE[N_A] + kt + 1)
                three(bank[:, 0, :], wh[:, kt, 0:P], wl[:, kt, 0:P], h_hi[:, kt, :], h_lo[:, kt, :], kt == 0, kt == KT - 1)
            for a in range(QT):
                q = slice(P * a, P * a + P)
                for kt in range(KT):
                    ins = three(bank[:, 1, IDX_HEADS * a:IDX_HEADS * (a + 1)], h_hi[:, kt, q], h_lo[:, kt, q], wh[:, kt, P:KI_COLS],
                                wl[:, kt, P:KI_COLS], False, kt == KT - 1)
            ins.then_inc(unit_done, 1)

            def a_unit(k, tokens=False):
                free_bank(V_A + k)
                unit(U_KI + k, un[(V_A + k) % 2], h_tiles, tokens=tokens)

            def index_scores(qt):
                if qt == 0:
                    pe.wait_ge(rope_done, ROPE_QI + 2)
                else:
                    pe.wait_ge(score_used, qt)
                for h in range(IDX_HEADS):
                    lo = HD * (h % 2)
                    ins = MM(acc[2 * (h // 4) + h % 2][:, h // 2 % 2, :], qi_fm[lo:lo + HD, h // 2, P * qt:P * qt + P],
                             ki_fm[lo:lo + HD, 0, :], start=True, stop=True)
                ins.then_inc(score_done, 1)

            a_unit(1)
            rot(ROPE_KI, 1, V_A)
            a_unit(2)
            rot(ROPE_QI, 2, V_A + 1)
            a_unit(3)
            rot(ROPE_QI + 1, 2, V_A + 2)
            a_unit(4, tokens=True)
            rot(ROPE_K, 2, V_A + 3)
            index_scores(0)
            a_unit(5)
            index_scores(1)
            a_unit(6)
            rot(ROPE_Q, 2, V_A + 5)
            a_unit(7)
            rot(ROPE_Q + 1, 2, V_A + 6)
            a_unit(8)
            rot(ROPE_Q + 2, 2, V_A + 7)
            rot(ROPE_Q + 3, 2, V_A + 8)
            pe.wait_ge(kdup_ready, KV_HEADS)
            pe.wait_ge(score_used, 2)
            group = HEADS // KV_HEADS
            attention(0, lambda h: k_dup[HD * (h % 2):HD * (h % 2) + HD, h // group, :],
                      lambda h, s: vA_tok[:, s, HD * (h // group):HD * (h // group) + HD])
            for j in range(UPD):
                unit(U_OA + j, acc[j], (z_hi, z_lo), z_ready(Z_A) if j == 0 else None)
            norm_stats(N_MLP2)
            mlp(2, N_MLP2)
            norm_stats(N_B)
            free_bank(V_B)
            pe.wait_ge(lo_made, U_F + 1)
            wh, wl = w_hi[U_F % 2], w_lo[U_F % 2]
            for kt in range(KT):
                pe.wait_ge(h_lo_made, H_BASE[N_B] + kt + 1)
                ins = three(un[V_B % 2][:, 0, :], wh[:, kt, 0:P], wl[:, kt, 0:P], h_hi[:, kt, :], h_lo[:, kt, :], kt == 0, kt == KT - 1)
            ins.then_inc(unit_done, 1)
            for j in range(UPD):
                free_bank(V_B + 1 + j)
                unit(U_KB + j, un[(V_B + 1 + j) % 2], h_tiles)
            pe.wait_ge(f_ready, 1)
            for a in range(QT):
                ins = nc.tensor.transpose(misc[:, 0, HEADS * a:HEADS * (a + 1)], f_cum[:, P * a:P * a + P], ident[0:HEADS, 0:HEADS])
            ins.then_inc(cumq_ready, 1)
            for r in range(8):
                if r >= 4:
                    pe.wait_ge(cumk_ready, r - 3)
                for m in range(2):
                    ins = MM(acc[r % 4][:, m, :], ident[0:HEADS, 2 * r + m:2 * r + m + 1].to_broadcast([HEADS, P]), f_neg[:], start=True, stop=True)
                ins.then_inc(f_bcast, 1)
            for j in range(UPD):
                free_bank(V_B + 5 + j)
                unit(U_VB + j, un[(V_B + 5 + j) % 2], h_tiles, tokens=True)
            for j in range(UPD):
                free_bank(V_B + 9 + j)
                unit(U_QB + j, un[(V_B + 9 + j) % 2], (z_hi, z_lo), h_ready(H_BASE["B_q"]) if j == 0 else None)
            pe.wait_ge(un_free, freed(V_B + 12))
            attention(1, lambda h: kB_fm[HD * (h % 2):HD * (h % 2) + HD, h // 2, :], lambda h, s: vB_tok[:, s, HD * h:HD * h + HD])
            for j in range(UPD):
                unit(U_OB + j, acc[j], (z_hi, z_lo), z_ready(Z_B) if j == 0 else None)
            norm_stats(N_MLP3)
            mlp(3, N_MLP3)
            norm_stats(N_OUT)
            pe.wait_ge(normed, 64 + KT)
            for k in range(4):
                free_bank(V_OUT + k)
                for n in range(4):
                    t = 4 * (k % 2) + n
                    ins = nc.tensor.transpose(bank4(un[(V_OUT + k) % 2])[:, n, :], tmp[:, t, P * (k // 2):P * (k // 2) + P], ident)
                ins.then_inc(tp_done, 1)


INPUTS = ("x", "c", "norm_g", "final_g", "ada_w", "ada_b", "conv_w_in", "conv_w", "conv_w_out", "rw_mu", "rw_w_rkv", "rw_w_o",
          "rw_w0", "rw_w1", "rw_w2", "rw_a0", "rw_a1", "rw_a2", "rw_g1", "rw_g2", "rw_k_k", "rw_k_a", "rw_r_k", "rw_ln_w",
          "rw_ln_b", "mlp_w1", "mlp_w2", "g_attn_a_2", "w_in_a_2", "w_o_a_2", "g_kv_2", "w_kv_b_2", "b_f_2", "g_attn_b_2",
          "w_q_b_2", "w_o_b_2", "g_mlp_2", "w_up_2", "w_down_2", "g_final_2")


def kernel(**inputs):
    import concourse.bacc as bacc
    from concourse.bass_utils import run_bass_kernel_spmd

    nc = bacc.Bacc("TRN2", target_bir_lowering=False, num_devices=1)
    arrays = {f"in_{n}": np.ascontiguousarray(inputs[n]) for n in INPUTS}
    arrays["in_const_table"] = constant_table()
    aps = {n[3:]: nc.dram_tensor(n, a.shape, mybir.dt.from_np(a.dtype), kind="ExternalInput").ap() for n, a in arrays.items()}
    out = nc.dram_tensor("out_x", (1, SEQ, D), F32, kind="ExternalOutput").ap()
    build(nc, aps, out)
    return run_bass_kernel_spmd(nc, [arrays], core_ids=[0]).results[0]["out_x"]
```

```python
from contextlib import ExitStack

import concourse.bass as bass
import numpy as np
from concourse import mybir

ALU = mybir.AluOpType
ACT = mybir.ActivationFunctionType
F32 = mybir.dt.float32
F32R = mybir.dt.float32r
AX_X = mybir.AxisListType.X

P = 128
SEQ = 256
D = 1024
KT = D // P
QT = SEQ // P
FF = 4 * D
GROUPS = FF // D
HD = 64
HEADS = D // HD
PAIRS = HEADS // 2
CHUNK = 64
CHUNKS = SEQ // CHUNK
UC = 256
UPD = D // UC
KV_HEADS = 4
IDX_HEADS = 8
TOPK = min(256, SEQ // 4)
RD, RA, RG = 64, 64, 160
DECAY = float(np.exp(-0.5))
NORM_EPS = 1e-6
GN_EPS = 64e-5
NEG = -1e30
TAKEN = -3e38

VEC_ADA_B, VEC_NORM_G, VEC_CONV_W, VEC_MU = 0, 96, 128, 152
VEC_W0, VEC_A0, VEC_KK, VEC_KA, VEC_RK, VEC_LNW, VEC_LNB = 200, 208, 216, 224, 232, 240, 248
VEC_C, VEC_FINAL, VEC_GA, VEC_GKV, VEC_GB, VEC_GMLP, VEC_GFIN = 256, 264, 272, 280, 288, 296, 312
N_VEC = 320

CONST_PARTS = ((("ident", P), ("mean", P), ("ones", P), ("rot", P)),
               (("head_ones", P), ("head_mean", P), ("level_t", 6 * P), ("before", P), ("upto", CHUNK), ("resets", SEQ)),
               (("cos", SEQ), ("sin", SEQ), ("admit", QT * SEQ), ("causal", QT * SEQ)))
CONST_COLS, CONST_AT = {}, [0]
for _part in CONST_PARTS:
    _at = CONST_AT[-1]
    for _name, _n in _part:
        CONST_COLS[_name] = (_at, _at + _n)
        _at += _n
    CONST_AT.append(_at)
N_CONST = CONST_AT[-1]


def constant_table():
    t = np.zeros((P, N_CONST), np.float32)

    def put(name, a):
        lo, hi = CONST_COLS[name]
        t[:, lo:hi] = np.asarray(a, np.float32).reshape(P, hi - lo)

    i = np.arange(P)
    same_head = (i[:, None] // HD) == (i[None, :] // HD)
    put("ident", np.eye(P))
    put("mean", np.full((P, P), 1.0 / D))
    put("ones", np.ones((P, P)))
    put("head_ones", same_head)
    put("head_mean", same_head / HD)
    rot = np.zeros((P, P))
    for m in range(P):
        d = m % HD
        rot[m + HD // 2 if d < HD // 2 else m - HD // 2, m] = -1.0 if d < HD // 2 else 1.0
    put("rot", rot)
    s, q = i[:, None], i[None, :]
    levels = [same_head & (s >> (j + 1) == q >> (j + 1)) & ((q >> j) & 1 == 1) & ((s >> j) & 1 == 0) for j in range(6)]
    put("level_t", np.stack(levels, 1))
    put("before", same_head & (s < q))
    put("upto", (i[:, None] % CHUNK) <= np.arange(CHUNK)[None, :])
    pos = np.arange(SEQ)
    put("resets", np.broadcast_to(pos % CHUNK != 0, (P, SEQ)))
    inv = np.float32(1.0) / (np.float32(10000.0) ** (np.arange(0, HD, 2, dtype=np.float32) / np.float32(HD)))
    ang = inv.astype(np.float32)[:, None] * pos.astype(np.float32)[None, :]
    put("cos", np.tile(np.cos(ang), (4, 1)))
    put("sin", np.tile(np.sin(ang), (4, 1)))
    tok = np.arange(QT)[None, :, None] * P + i[:, None, None]
    put("admit", np.where(pos[None, None, :] < (tok // CHUNK + 1) * CHUNK, 0.0, NEG))
    put("causal", np.where(pos[None, None, :] <= tok, 0.0, NEG))
    return t


def build(nc, A, out):
    with ExitStack() as ctx:
        sems = {}

        def sem(name):
            if name not in sems:
                sems[name] = ctx.enter_context(nc.semaphore(name))
            return sems[name]

        base = (nc.sbuf_base + 63) // 64 * 64
        top = [base]

        def here(nbytes):
            off = top[0]
            top[0] += (nbytes + 63) // 64 * 64
            return off

        def at(name, shape, off, dt=F32):
            return nc.alloc_sbuf_tensor_at(name, shape, dt, offset=off)

        def new(name, shape, dt=F32):
            return at(name, shape, here(4 * int(np.prod(shape[1:]))), dt)

        FM = [P, KT, SEQ]
        FMB = 4 * KT * SEQ
        NSTAGE = 4
        stage = [new(f"stage{i}", [P, KT, UC]) for i in range(NSTAGE)]
        w_hi = [new(f"w_hi{i}", [P, KT, UC], F32R) for i in range(2)]
        w_lo = [new(f"w_lo{i}", [P, KT, UC], F32R) for i in range(2)]
        x = new("x", FM)
        act_off = [here(FMB) for _ in range(4)]
        h_hi, h_lo, z_hi, z_lo = (at(n, FM, o, F32R) for n, o in zip(("h_hi", "h_lo", "z_hi", "z_lo"), act_off))
        tmp_off = top[0]
        tmp = new("tmp", FM)
        sq = new("sq", FM)
        r_off = [here(FMB) for _ in range(6)]
        scr_off = here(26 * 1024)
        part_cols = [CONST_AT[i + 1] - CONST_AT[i] for i in range(3)]
        const_off = [here(4 * part_cols[0])]
        const_off += [here(4 * max(part_cols[1:]))] * 2
        const = [at(f"const{i}", [P, n], o) for i, (n, o) in enumerate(zip(part_cols, const_off))]
        vecT = new("vecT", [P, N_VEC])
        mods = [new(f"mod{i}", [P, 48]) for i in range(2)]
        gain = new("gain", [P, 4, KT])
        small = new("small", [P, 64])
        rstd = new("rstd", [P, 3, SEQ])

        def c_(name):
            lo, hi = CONST_COLS[name]
            i = max(i for i in range(3) if CONST_AT[i] <= lo)
            return const[i][:, lo - CONST_AT[i]:hi - CONST_AT[i]]

        ident, mean_w, ones_w, head_ones, head_mean, rot_w = (c_(n) for n in ("ident", "mean", "ones", "head_ones", "head_mean", "rot"))
        level_t = c_("level_t").rearrange("p (j q) -> p j q", j=6)
        admit = c_("admit").rearrange("p (a s) -> p a s", a=QT)
        causal = c_("causal").rearrange("p (a s) -> p a s", a=QT)

        x_in = at("x_in", [P, QT, D], scr_off)
        vec_in = at("vec_in", [P, 3, P], scr_off + 8192)
        ada_acc = at("ada_acc", [P, 6 * D], r_off[0])
        ada_first = [at(f"ada_first{i}", [P, KT, UC], o) for i, o in enumerate(act_off + [tmp_off] + r_off[3:6])]
        ada_dve = ada_first[6]
        ada_pool = [ada_first[5], ada_first[7]]
        c_silu = small[:, 0:8]
        b_gate = at("b_gate", FM, scr_off + 16 * 1024)
        PADT = SEQ + 2
        u_pad = at("u_pad", [P, KT, PADT], scr_off)
        conv_y = at("conv_y", [P, 2, SEQ], scr_off + 8320)
        zf = [at(f"zf{i}", [P, 2, SEQ], scr_off + 12 * 1024 + 2048 * i) for i in range(2)]
        relu_b = [at(f"relu{i}", [P, 2, SEQ], scr_off + 16 * 1024 + 2048 * i) for i in range(2)]
        RW = [at(f"rw{i}", FM, r_off[i]) for i in range(6)]
        rw_r, rw_k, rw_v, rw_c, rw_a, rw_kk = RW
        lora1 = at("lora1", [P, KT, RD + RA + RG], scr_off)
        lora_w2 = at("lora_w2", [P, D], scr_off + 9216)
        lora_a2 = lora_w2
        lora_g2a = at("lora_g2a", [P, D], scr_off + 13312)
        lora_g2b = at("lora_g2b", [32, D], scr_off + 17408)
        lora_h = at("lora_h", [P, 4, SEQ], scr_off + 21504)
        mixf = at("mixf", [P, 4, SEQ], r_off[5])
        BD = [P, CHUNKS, P]
        next_at = [0, 0]

        def pair_new(name, shape, dt=F32):
            off = act_off[0] + next_at[0]
            next_at[0] += 4 * int(np.prod(shape[1:]))
            assert next_at[0] <= 4 * FMB
            return at(name, shape, off)

        def scratch_new(name, shape):
            off = scr_off + next_at[1]
            next_at[1] += 4 * int(np.prod(shape[1:]))
            assert next_at[1] <= 26 * 1024
            return at(name, shape, off)

        b_tok, k_tok, v_tok, inv_t, lak_t = ([pair_new(f"{n}{i}", BD) for i in range(2)] for n in ("b_tok", "k_tok", "v_tok", "inv_t", "lak_t"))
        lrb_t, lrk_t = ([pair_new(f"{n}{i}", [P, CHUNKS, CHUNK]) for i in range(2)] for n in ("lrb_t", "lrk_t"))
        n_t, inv_x, t1 = (pair_new(n, BD) for n in ("n_t", "inv_x", "t1"))
        ar = [scratch_new(f"ar{i}", [P, CHUNKS, P + CHUNK]) for i in range(2)]
        b_bd, k_bd, v_bd = (scratch_new(n, BD) for n in ("b_bd", "k_bd", "v_bd"))
        w_cum, w_inv = (scratch_new(n, [P, SEQ]) for n in ("w_cum", "w_inv"))
        n_m = [scratch_new(f"n_m{i}", BD) for i in range(2)]
        state = [scratch_new(f"state{i}", [P, P]) for i in range(2)]
        state_kept, wkv_rhs, wkv_u = (scratch_new(n, [P, P]) for n in ("state_kept", "wkv_rhs", "wkv_u"))
        w_end = scratch_new("w_end", [P, PAIRS, CHUNKS])
        y_wkv, g_wkv = tmp, sq
        q_fm = at("q_fm", FM, r_off[0])
        kA_fm = at("kA_fm", [P, 2, SEQ], r_off[1])
        k_dup = at("k_dup", [P, KV_HEADS, SEQ], r_off[1] + 2048)
        qi_fm = at("qi_fm", [P, 4, SEQ], r_off[2])
        ki_fm = at("ki_fm", [P, 1, SEQ], r_off[2] + 4096)
        vA_tok = at("vA_tok", [P, QT, 256], r_off[2] + 5120)
        kB_fm = at("kB_fm", FM, r_off[1])
        vB_tok = at("vB_tok", [P, QT, D], r_off[2])
        rope_in = [at(f"rope_in{i}", [P, 2, SEQ], r_off[3] + 2048 * i) for i in range(2)]
        rope_c = at("rope_c", [P, 2, SEQ], r_off[3] + 4096)
        sel_bias = at("sel_bias", [P, QT, SEQ], r_off[3] + 6144)
        score = at("score", [P, QT, SEQ], r_off[4])
        score_t = [at(f"score_t{i}", [P, SEQ], r_off[4] + 2048 + 1024 * i) for i in range(2)]
        top8 = at("top8", [P, 8], r_off[4] + 4096)
        wi_tok = at("wi_tok", [P, QT, IDX_HEADS], r_off[4] + 4160)
        cum_k = at("cum_k", [P, HEADS, SEQ], r_off[3])
        f_z = at("f_z", [HEADS, SEQ], scr_off + 10 * 1024)
        f_e = at("f_e", [HEADS, SEQ], scr_off + 11 * 1024)
        f_l = at("f_l", [HEADS, SEQ], scr_off + 16 * 1024)
        f_cum = at("f_cum", [HEADS, SEQ], scr_off + 17 * 1024)
        f_neg = at("f_neg", [HEADS, SEQ], scr_off + 18 * 1024)
        b_f = at("b_f", [HEADS, 1], scr_off + 24 * 1024)
        cum_q = at("cum_q", [P, QT, HEADS], scr_off + 24 * 1024 + 64)
        head_bias = [at(f"head_bias{i}", [P, QT, SEQ], scr_off + 18 * 1024 + 1024 + 2048 * i) for i in range(2)]
        NA = 3
        logit = [at(f"logit{i}", [P, QT, SEQ], r_off[5] + 2048 * i) for i in range(NA)]
        probs = [at(f"probs{i}", [P, QT, SEQ], scr_off + 2048 * i) for i in range(NA)]
        probs_t = [at(f"probs_t{i}", [P, 3, P], scr_off + 6144 + 1536 * i) for i in range(2)]
        stat = [at(f"stat{i}", [P, 8], scr_off + 9344 + 64 * i) for i in range(NA)]
        out_tok = at("out_tok", [P, QT, D], scr_off)
        assert top[0] <= nc.sbuf_usable_end, (top[0], nc.sbuf_usable_end)

        acc = [ctx.enter_context(nc.psum_tensor(f"acc{i}", [P, 2, SEQ], F32)) for i in range(4)]
        un = [ctx.enter_context(nc.psum_tensor(f"un{i}", [P, 2, SEQ], F32)) for i in range(2)]
        stat_ps = ctx.enter_context(nc.psum_tensor("stat_ps", [P, 2, SEQ], F32))
        misc = ctx.enter_context(nc.psum_tensor("misc", [P, 2, SEQ], F32))

        def bank4(b):
            return b[:, :, :].rearrange("p a s -> p (a s)").rearrange("p (c q) -> p c q", c=CHUNKS)

        units = []

        def cols(w, c0, n=UC, r0=0):
            return [(0, n, w[r0:r0 + D, c0:c0 + n].rearrange("(t p) n -> p t n", p=P))]

        def add(sources):
            units.append(sources)
            return len(units) - 1

        def add_dense(w, n):
            first = len(units)
            for j in range(n // UC):
                add(cols(w, j * UC))
            return first

        def add_mlp(w1, w2):
            first = len(units)
            for g in range(GROUPS):
                for j in range(UPD):
                    add(cols(w1, g * D + j * UC))
                for j in range(UPD):
                    add(cols(w2, j * UC, r0=g * D))
            return first

        w_in_a, w_kv = A["w_in_a_2"][0], A["w_kv_b_2"]
        U_CONV_IN = add_dense(A["conv_w_in"][0], 3 * D)
        U_CONV_OUT = add_dense(A["conv_w_out"][0], D)
        U_MLP = [add_mlp(A["mlp_w1"][0], A["mlp_w2"][0])]
        U_RWK = add_dense(A["rw_w_rkv"][0, 1], D)
        U_RWR = add_dense(A["rw_w_rkv"][0, 0], D)
        U_RWV = add_dense(A["rw_w_rkv"][0, 2], D)
        U_RWO = add_dense(A["rw_w_o"][0], D)
        U_MLP.append(add_mlp(A["mlp_w1"][1], A["mlp_w2"][1]))
        A_K, A_V, A_QI, A_KI = D, D + 256, D + 512, D + 1024
        KI_COLS = HD + HD + IDX_HEADS
        U_KI = add([(0, HD, cols(w_in_a, A_KI, HD)[0][2]), (HD, KI_COLS, cols(w_in_a, A_KI, HD + IDX_HEADS)[0][2])])
        U_QI = add(cols(w_in_a, A_QI))
        add(cols(w_in_a, A_QI + UC))
        U_KA = add(cols(w_in_a, A_K))
        U_VA = add(cols(w_in_a, A_V))
        U_QA = len(units)
        for j in range(UPD):
            add(cols(w_in_a, j * UC))
        U_OA = add_dense(A["w_o_a_2"][0], D)
        U_MLP.append(add_mlp(A["w_up_2"][0], A["w_down_2"][0]))
        U_F = add([(0, HEADS, cols(w_kv, 2 * D, HEADS)[0][2]), (HEADS, P, cols(w_kv, 0, P - HEADS)[0][2])])
        U_KB = len(units)
        for j in range(2 * UPD):
            add(cols(w_kv, j * UC))
        U_VB = U_KB + UPD
        U_QB = add_dense(A["w_q_b_2"][0], D)
        U_OB = add_dense(A["w_o_b_2"][0], D)
        U_MLP.append(add_mlp(A["w_up_2"][1], A["w_down_2"][1]))
        NU = len(units)

        def unit_cols(u):
            return max(hi for _, hi, _ in units[u])

        V_VEC, V_X, V_CONV = 0, 1, 5
        V_MLP = [17]
        V_RKV = V_MLP[0] + 16
        V_MLP.append(V_RKV + 12)
        V_A = V_MLP[1] + 16
        V_MLP.append(V_A + 9)
        V_B = V_MLP[2] + 16
        V_MLP.append(V_B + 13)
        V_OUT = V_MLP[3] + 16
        Z_CONV, Z_MLP0, Z_RW, Z_MLP1, Z_A, Z_MLP2, Z_B, Z_MLP3 = 0, 4, 20, 24, 40, 44, 60, 64
        Z_MLP = [Z_MLP0, Z_MLP1, Z_MLP2, Z_MLP3]
        N_CONV, N_MLP0, N_RW, N_MLP1, N_FIN1, N_A, N_MLP2, N_B, N_MLP3, N_OUT = range(10)
        N_MLP = [N_MLP0, N_MLP1, N_MLP2, N_MLP3]
        H_BASE = {N_CONV: 0, N_MLP0: 8, N_MLP1: 16, N_A: 24, N_MLP2: 32, N_B: 40, "B_q": 48, N_MLP3: 56}
        ROPE_KI, ROPE_QI, ROPE_K, ROPE_Q, N_ROPE = 0, 1, 3, 4, 8

        const_in, const_b_in, x_loaded, vec_loaded, lora_loaded, bf_loaded = (sem(n) for n in ("const_in", "const_b_in", "x_loaded", "vec_loaded", "lora_loaded", "bf_loaded"))
        landed = [sem(f"unit_landed{i}") for i in range(NSTAGE)]
        hi_made, lo_made, unit_done, un_free = (sem(n) for n in ("hi_made", "lo_made", "unit_done", "un_free"))
        VEC_DMAS = 19

        def freed(v):
            return v + 1 if v < V_X else v - 3

        N_ADA = 6 * D // UC
        ADA_FIRST = 8
        ADA_DVE = (0, 1, 3, 4, 6, 7) + tuple(range(9, 20, 2)) + tuple(range(N_ADA + 2, 2 * N_ADA, 3))
        ADA_POOL = tuple(a for a in range(2 * N_ADA) if a not in ADA_DVE)

        def ada_cols(a):
            return cols(A["ada_w"][a // N_ADA], a % N_ADA * UC)[0][2]

        def ada_count(units_of, a_end):
            return sum(a < a_end for a in units_of)

        WKV_LEVELS = range(1, 6)
        wkv_prepare = [("gram", 0, 0), ("gram", 0, 1), ("tok", 0, 0), ("tok", 0, 1), ("x1", 0, 0), ("x1", 0, 1)]
        for j in WKV_LEVELS:
            wkv_prepare += [("t1", j, 0), ("t1", j, 1), ("dx", j, 0), ("dx", j, 1)]
        wkv_chain = [(step, c, c // 2) for c in range(CHUNKS) for step in ("rhs", "u", "sy")]
        WKV_STEPS = []
        for n, step in enumerate(wkv_prepare):
            WKV_STEPS.append(step)
            if n < 6 or n % 2 and n < 18:
                WKV_STEPS.append(wkv_chain.pop(0))
        assert not wkv_chain

        def wkv_steps(p):
            for step, j, h in WKV_STEPS:
                chain_step = step in ("rhs", "u", "sy")
                if 0 <= p - chain_step < PAIRS:
                    yield step, p - chain_step, j, h

        block = ctx.enter_context(nc.Block())

        @block.sync
        def _(sp):
            for i in range(2):
                sp.dma_start(const[i][:], A["const_table"][:, CONST_AT[i]:CONST_AT[i + 1]]).then_inc(const_in, 16)
            sp.dma_start(x_in[:], A["x"][0].rearrange("(a p) d -> p a d", p=P)).then_inc(x_loaded, 16)

            def rows(tile, r0, ap, n):
                sp.dma_start(vec_in[r0:r0 + n, tile, :], ap).then_inc(vec_loaded, 16)

            flat = lambda ap, n: ap.rearrange("(r q) -> r q", q=P)
            rows(0, 0, flat(A["ada_b"][0], 48), 48)
            rows(0, 48, flat(A["ada_b"][1], 48), 48)
            rows(0, 96, A["norm_g"].rearrange("a b (r q) -> (a b r) q", q=P), 32)
            rows(1, 0, A["conv_w"][0].rearrange("a (r q) -> (a r) q", q=P), 24)
            rows(1, 24, A["rw_mu"][0].rearrange("a (r q) -> (a r) q", q=P), 48)
            for r0, name in ((72, "rw_w0"), (80, "rw_a0"), (88, "rw_k_k"), (96, "rw_k_a"), (112, "rw_ln_w"), (120, "rw_ln_b")):
                rows(1, r0, flat(A[name][0], 8), 8)
            rows(1, 104, A["rw_r_k"][0].rearrange("(r a) d -> r (a d)", a=2), 8)
            rows(2, 0, flat(A["c"][0], 8), 8)
            rows(2, 8, flat(A["final_g"], 8), 8)
            rows(2, 16, flat(A["g_attn_a_2"][0], 8), 8)
            rows(2, 24, flat(A["g_kv_2"], 8), 8)
            rows(2, 32, flat(A["g_attn_b_2"][0], 8), 8)
            rows(2, 40, A["g_mlp_2"].rearrange("a (r q) -> (a r) q", q=P), 16)
            rows(2, 56, flat(A["g_final_2"], 8), 8)

            for a in range(ADA_FIRST):
                sp.dma_start(ada_first[a][:], ada_cols(a)).then_inc(sem(f"ada_first_landed{a}"), 16)

            ada_at = [U_CONV_IN + NSTAGE] + [U_CONV_IN + 2 * k + 8 for k in range(5)] + [U_MLP[0] + 1] +\
                [U_MLP[0] + 8 * g + d + 7 for g in range(GROUPS) for d in (UPD, 2 * UPD - 1)][:-1]

            def load_unit(u):
                if u >= NSTAGE:
                    sp.wait_ge(lo_made, u - NSTAGE + 1)
                for lo, hi, src in units[u]:
                    sp.dma_start(stage[u % NSTAGE][:, :, lo:hi], src).then_inc(landed[u % NSTAGE], 32 // len(units[u]))

            for u in range(NU):
                if u == U_RWK + NSTAGE:
                    sp.wait_ge(sem("x_ready"), 8 * N_RW + 8)
                    sp.dma_start(lora1[:, :, 0:RD], A["rw_w1"][0].rearrange("(t p) n -> p t n", p=P)).then_inc(lora_loaded, 16)
                    sp.dma_start(lora1[:, :, RD:RD + RA], A["rw_a1"][0].rearrange("(t p) n -> p t n", p=P)).then_inc(lora_loaded, 16)
                    sp.dma_start(lora1[:, :, RD + RA:], A["rw_g1"][0].rearrange("(t p) n -> p t n", p=P)).then_inc(lora_loaded, 16)
                    sp.dma_start(lora_w2[0:RD, :], A["rw_w2"][0]).then_inc(lora_loaded, 16)
                    sp.dma_start(lora_w2[RD:RD + RA, :], A["rw_a2"][0]).then_inc(lora_loaded, 16)
                    sp.dma_start(lora_g2a[:, :], A["rw_g2"][0, 0:P, :]).then_inc(lora_loaded, 16)
                    sp.dma_start(lora_g2b[:, :], A["rw_g2"][0, P:RG, :]).then_inc(lora_loaded, 16)
                if u == U_MLP[1] + UPD:
                    sp.wait_ge(sem("x_ready"), 8 * N_MLP1 + 8)
                    sp.dma_start(const[2][:], A["const_table"][:, CONST_AT[2]:]).then_inc(const_b_in, 16)
                if u == U_F:
                    sp.wait_ge(sem("x_ready"), 8 * N_MLP2 + 8)
                    sp.dma_start(b_f[:], A["b_f_2"].rearrange("(h a) -> h a", a=1)).then_inc(bf_loaded, 16)
                if u in ada_at:
                    k = ada_at.index(u) + ADA_FIRST - 2
                    sp.wait_ge(sem("ada_dve_done"), k)
                    sp.dma_start(ada_dve[:], ada_cols(ADA_DVE[k])).then_inc(sem("ada_dve_landed"), 16)
                load_unit(u)
            out_v = out[0].rearrange("(a p) d -> p a d", p=P)
            sp.wait_ge(un_free, freed(V_OUT + 3))
            sp.dma_start(out_v, out_tok[:]).then_inc(sem("stored"), 16)
            sp.wait_ge(sem("stored"), 16)

        ada_first_landed = [sem(f"ada_first_landed{a}") for a in range(ADA_FIRST)]
        ada_pool_landed = [sem(f"ada_pool_landed{i}") for i in range(2)]
        ada_dve_landed, ada_dve_done, ada_pool_done, ada_summed = (sem(n) for n in ("ada_dve_landed", "ada_dve_done", "ada_pool_done", "ada_summed"))

        @block.gpsimd
        def _(pool):
            G = nc.gpsimd
            chain = sem("pool_chain")
            count = [0]

            def link(ins):
                count[0] += 1
                ins.then_inc(chain, 1)
                pool.wait_ge(chain, count[0])

            n_first = ada_count(ADA_POOL, ADA_FIRST)

            def load_ada(k):
                pool.dma_start(ada_pool[k % 2][:], ada_cols(ADA_POOL[k])).then_inc(ada_pool_landed[k % 2], 16)

            pool.wait_ge(sem("silu_ready"), 1)
            for k, a in enumerate(ADA_POOL):
                if k < n_first:
                    pool.wait_ge(ada_first_landed[a], 16)
                    w = ada_first[a]
                else:
                    if a >= N_ADA > ADA_POOL[k - 1]:
                        pool.wait_ge(ada_summed, 4)
                    pool.wait_ge(ada_pool_landed[k % 2], 16 * ((k - n_first) // 2 + 1))
                    w = ada_pool[k % 2]
                link(G.tensor_tensor(w[:], w[:], c_silu.unsqueeze(2).to_broadcast([P, KT, UC]), ALU.mult))
                link(G.tensor_tensor(w[:, 0:4, :], w[:, 0:4, :], w[:, 4:8, :], ALU.add))
                link(G.tensor_tensor(w[:, 0:2, :], w[:, 0:2, :], w[:, 2:4, :], ALU.add))
                G.tensor_tensor(ada_acc[:, a % N_ADA * UC:(a % N_ADA + 1) * UC], w[:, 0, :], w[:, 1, :], ALU.add).then_inc(ada_pool_done, 1)
                if k == n_first - 1:
                    pool.wait_ge(ada_pool_done, n_first)
                    pool.wait_ge(ada_dve_done, ada_count(ADA_DVE, ADA_FIRST))
                    load_ada(n_first)
                    load_ada(n_first + 1)
                elif n_first <= k and k + 2 < len(ADA_POOL):
                    pool.wait_ge(ada_pool_done, k + 1)
                    load_ada(k + 2)

            pool.wait_ge(sem("lora2_done"), 12)
            for m in (b_bd, k_bd, v_bd, ar[0], ar[1]):
                ins = G.memset(m[:], 0.0)
            ins.then_inc(sem("bd_zeroed"), 1)
            pool.wait_ge(sem("bd_zeroed"), 1)
            pool.wait_ge(sem("rw_ready"), 1)
            pool.wait_ge(un_free, freed(V_RKV + 7))
            wc = w_cum[:].rearrange("p (c s) -> p c s", c=CHUNKS)
            wi = w_inv[:].rearrange("p (c s) -> p c s", c=CHUNKS)

            def in_chunks(m, p, lo, hi):
                return m[lo:hi, p, :].rearrange("p (c s) -> p c s", c=CHUNKS)

            def build_bk(p):
                pool.wait_ge(sem("exp_ready"), 2 * p + 2)
                if p:
                    pool.wait_ge(sem("nm_ready"), 4 * p - 2)
                if p:
                    pool.wait_ge(sem("tok_done"), 3 * p)
                for h, (lo, hi) in enumerate(((0, HD), (HD, P))):
                    o = CHUNK * h
                    G.tensor_tensor(b_bd[lo:hi, :, o:o + CHUNK], in_chunks(rw_a, p, lo, hi), wi[lo:hi], ALU.mult)
                    link(G.tensor_tensor(k_bd[lo:hi, :, o:o + CHUNK], in_chunks(rw_k, p, lo, hi), wi[lo:hi], ALU.mult))

            def build_ar(p):
                if p >= 2:
                    pool.wait_ge(sem("y_done"), CHUNKS * (p - 1))
                if p:
                    pool.wait_ge(sem("nm_ready"), 4 * p)
                m = ar[p % 2]
                for h, (lo, hi) in enumerate(((0, HD), (HD, P))):
                    o = CHUNK * h
                    nkk = in_chunks(rw_kk, p, lo, hi)
                    G.tensor_copy(m[lo:hi, :, o:o + 1], nkk[:, :, 0:1])
                    link(G.tensor_tensor(m[lo:hi, :, o + 1:o + CHUNK], nkk[:, :, 1:CHUNK], wc[lo:hi, :, 0:CHUNK - 1], ALU.mult))
                G.tensor_tensor(m[:, :, P:P + CHUNK], in_chunks(rw_r, p, 0, P), wc, ALU.mult).then_inc(sem("built"), 1)

            build_bk(0)
            build_ar(0)
            for p in range(PAIRS):
                for j in WKV_LEVELS[1:]:
                    if j == 2:
                        pool.wait_ge(sem("inv_ready"), 12 * p + 2)
                    else:
                        pool.wait_ge(sem("t1_done"), 10 * p + 2 * (j - 2))
                    G.tensor_tensor(n_m[(j - 1) % 2][:], n_t[:], level_t[:, j, :].unsqueeze(1).to_broadcast([P, CHUNKS, P]), ALU.mult)\
                        .then_inc(sem("nm_ready"), 1)
                    if j == 3 and p + 1 < PAIRS:
                        build_bk(p + 1)
                if p + 1 < PAIRS:
                    build_ar(p + 1)

            for i in range(HEADS):
                if i == 0:
                    pool.wait_ge(const_b_in, 16)
                    pool.wait_ge(sem("cumk_ready"), 8)
                if i >= 2:
                    pool.wait_ge(sem("max_ready"), HEADS + i - 1)
                nc.gpsimd.tensor_tensor(head_bias[i % 2][:], causal, cum_k[:, i, :].unsqueeze(1).to_broadcast([P, QT, SEQ]), ALU.add)\
                    .then_inc(sem("bias_ready"), 1)

        tp_done, x_ready = sem("tp_done"), sem("x_ready")
        sq_ready, stat_done, ms_ready, std_ready = (sem(n) for n in ("sq_ready", "stat_done", "ms_ready", "std_ready"))
        normed, h_hi_made, h_lo_made = (sem(n) for n in ("normed", "h_hi_made", "h_lo_made"))
        zf_ready, z_hi_made, z_lo_made, relu_ready = (sem(n) for n in ("zf_ready", "z_hi_made", "z_lo_made", "relu_ready"))
        lora_mixed, lora1_done, lora1_out, lora2_done, lora2_out = (sem(n) for n in ("lora_mixed", "lora1_done", "lora1_out", "lora2_done", "lora2_out"))
        mix_ready, mix_hi, mix_lo = (sem(n) for n in ("mix_ready", "mix_hi", "mix_lo"))
        kk0_ready, kksq_ready, ss_done, ss_ready, ss_root = (sem(n) for n in ("kk0_ready", "kksq_ready", "ss_done", "ss_ready", "ss_root"))
        cum_ready, exp_ready, built = (sem(n) for n in ("cum_ready", "exp_ready", "built"))
        g_done, tok_done, tok_out, inv_ready, lak_ready, v_built, end_ready = (
            sem(n) for n in ("g_done", "tok_done", "tok_out", "inv_ready", "lak_ready", "v_built", "end_ready"))
        x1_done, x1_out, nm_ready, t1_done, t1_out, dx_done = (sem(n) for n in ("x1_done", "x1_out", "nm_ready", "t1_done", "t1_out", "dx_done"))
        rhs_done, rhs_out, u_done, u_out, y_done, y_out, s_done, state_ready = (
            sem(n) for n in ("rhs_done", "rhs_out", "u_done", "u_out", "y_done", "y_out", "s_done", "state_ready"))
        rk_ready, gn_mean_done, yc_ready, ycsq_ready, gn_var_done, gv_ready, gv_root, bonus_done = (
            sem(n) for n in ("rk_ready", "gn_mean_done", "yc_ready", "ycsq_ready", "gn_var_done", "gv_ready", "gv_root", "bonus_done"))
        rot_done, rope_done, ki_loaded, kdup_ready = (sem(n) for n in ("rot_done", "rope_done", "ki_loaded", "kdup_ready"))
        score_done, score_used = sem("score_done"), sem("score_used")
        f_abs, f_exp, f_one, f_log, f_ready, f_bcast, cumk_ready, cumq_ready = (
            sem(n) for n in ("f_abs", "f_exp", "f_one", "f_log", "f_ready", "f_bcast", "cumk_ready", "cumq_ready"))
        qk_done, max_ready, exp_done, p_ready, pt_done, pt_out, pv_done = (
            sem(n) for n in ("qk_done", "max_ready", "exp_done", "p_ready", "pt_done", "pt_out", "pv_done"))
        silu_e, silu_ready, ada_summed_pe = sem("silu_e"), sem("silu_ready"), sem("ada_summed_pe")

        @block.scalar
        def _(act):
            A_ = nc.scalar.activation

            def split(u):
                if u >= NU:
                    return
                n = unit_cols(u)
                act.wait_ge(landed[u % NSTAGE], 32 * (u // NSTAGE + 1))
                if u >= 2:
                    act.wait_ge(unit_done, u - 1)
                A_(w_hi[u % 2][:, :, 0:n], stage[u % NSTAGE][:, :, 0:n], ACT.Copy).then_inc(hi_made, 1)

            def norm_stats(n):
                for t in range(KT):
                    act.wait_ge(x_ready, 8 * n + t + 1)
                    if t == 0 and n:
                        act.wait_ge(stat_done, n)
                    A_(sq[:, t, :], x[:, t, :], ACT.Square).then_inc(sq_ready, 1)
                act.wait_ge(ms_ready, n + 1)
                A_(rstd[:, 1, :], rstd[:, 0, :], ACT.Sqrt).then_inc(std_ready, 1)

            def norm_split(base, hi, shift):
                for t in range(KT):
                    act.wait_ge(normed, base + t + 1)
                    if shift is None:
                        A_(hi[:, t, :], tmp[:, t, :], ACT.Copy).then_inc(h_hi_made, 1)
                    else:
                        A_(hi[:, t, :], tmp[:, t, :], ACT.Identity, bias=shift[:, t:t + 1]).then_inc(h_hi_made, 1)

            def z_split(zc, j):
                act.wait_ge(zf_ready, zc + 1)
                A_(z_hi[:, 2 * j:2 * j + 2, :], zf[zc % 2][:], ACT.Copy).then_inc(z_hi_made, 1)

            def evac(u, v, dst, scale=1.0):
                act.wait_ge(unit_done, u + 1)
                A_(dst, un[v % 2][:], ACT.Copy, scale=scale).then_inc(un_free, 1)

            def mlp(m):
                u, v, zc = U_MLP[m], V_MLP[m], Z_MLP[m]
                for g in range(GROUPS):
                    for j in range(UPD):
                        uu = u + 2 * UPD * g + j
                        act.wait_ge(unit_done, uu + 1)
                        A_(relu_b[j % 2][:], un[(v + j) % 2][:], ACT.Relu).then_inc(relu_ready, 1)
                        if j < UPD - 1:
                            split(uu + 2)
                            z_split(zc + UPD * g + j, j)
                        else:
                            z_split(zc + UPD * g + j, j)
                            split(uu + 2)
                    for j in range(UPD):
                        split(u + 2 * UPD * g + UPD + j + 2)

            act.wait_ge(un_free, freed(V_VEC))
            A_(small[:, 8:16], vecT[:, VEC_C:VEC_C + KT], ACT.Exp, scale=-1.0).then_inc(silu_e, 1)
            norm_stats(N_CONV)
            split(0)
            split(1)
            norm_split(H_BASE[N_CONV], h_hi, mods[0][:, 0:8])
            for j in range(12):
                if j < 8:
                    dst = (b_gate if j < 4 else tmp)[:, 2 * (j % 4):2 * (j % 4) + 2, :]
                    evac(U_CONV_IN + j, V_CONV + j, dst)
                split(U_CONV_IN + j + 2)
                if j >= 8:
                    z_split(Z_CONV + j - 8, j - 8)
            for j in range(UPD):
                split(U_CONV_OUT + j + 2)
            norm_stats(N_MLP0)
            norm_split(H_BASE[N_MLP0], h_hi, mods[0][:, 24:32])
            mlp(0)
            norm_stats(N_RW)
            mix_dst = (h_hi, z_hi, h_hi)

            def mix_split(m):
                act.wait_ge(mix_ready, m + 1)
                A_(mix_dst[m // KT][:, m % KT, :], mixf[:, m % 4, :], ACT.Copy).then_inc(mix_hi, 1)

            for m in range(2 * KT):
                mix_split(m)
            act.wait_ge(lora1_done, 1)
            A_(lora_h[0:RD, 0, :], acc[0][0:RD, 0, :], ACT.Tanh).then_inc(lora1_out, 1)
            act.wait_ge(lora1_done, 2)
            A_(lora_h[RD:RD + RA, 1, :], acc[1][RD:RD + RA, 0, :], ACT.Copy).then_inc(lora1_out, 1)
            act.wait_ge(lora1_done, 3)
            A_(lora_h[:, 2, :], acc[2][:, 0, :], ACT.Sigmoid).then_inc(lora1_out, 1)
            A_(lora_h[0:RG - P, 3, :], acc[3][0:RG - P, 0, :], ACT.Sigmoid).then_inc(lora1_out, 1)
            for which, (dst, vec) in enumerate(((rw_c, VEC_W0), (rw_a, VEC_A0))):
                for t in range(KT):
                    if t % 2 == 0:
                        act.wait_ge(lora2_done, 4 * which + t // 2 + 1)
                    A_(dst[:, t, :], acc[t // 2][:, t % 2, :], ACT.Sigmoid, bias=vecT[:, vec + t:vec + t + 1]).then_inc(lora2_out, 1)
            for j in range(12):
                dst = (rw_k, rw_r, rw_v)[j // 4]
                evac(U_RWK + j, V_RKV + j, dst[:, 2 * (j % 4):2 * (j % 4) + 2, :])
                split(U_RWK + j + 2)
                if j == 3:
                    for m in range(2 * KT, 3 * KT):
                        mix_split(m)
                if j == 4:
                    for k in range(4):
                        act.wait_ge(kk0_ready, k + 1)
                        A_(tmp[:, 2 * k:2 * k + 2, :], rw_kk[:, 2 * k:2 * k + 2, :], ACT.Square).then_inc(kksq_ready, 1)
                if j == 6:
                    for k in range(4):
                        act.wait_ge(ss_ready, k + 1)
                        A_(tmp[:, 2 * k:2 * k + 2, :], tmp[:, 2 * k:2 * k + 2, :], ACT.Sqrt).then_inc(ss_root, 1)
                if j == 7:
                    for k in range(4):
                        act.wait_ge(lora2_done, 8 + k + 1)
                        A_(g_wkv[:, 2 * k:2 * k + 2, :], acc[k][:], ACT.Copy).then_inc(lora2_out, 1)
                    act.wait_ge(cum_ready, 1)
                    A_(w_end[:], rw_c[:].rearrange("p t (c s) -> p t c s", c=CHUNKS)[:, :, :, CHUNK - 1], ACT.Exp, scale=-DECAY).then_inc(end_ready, 1)

            def wkv_build(p):
                if p:
                    act.wait_ge(built, p)
                A_(w_cum[:], rw_c[:, p, :], ACT.Exp, scale=-DECAY).then_inc(exp_ready, 1)
                A_(w_inv[:], rw_c[:, p, :], ACT.Exp, scale=DECAY).then_inc(exp_ready, 1)
                if p:
                    act.wait_ge(tok_done, 3 * p - 2)
                else:
                    act.wait_ge(sem("bd_zeroed"), 1)
                v = rw_v[:, p, :].rearrange("p (c s) -> p c s", c=CHUNKS)
                A_(v_bd[0:HD, :, 0:CHUNK], v[0:HD], ACT.Copy)
                A_(v_bd[HD:P, :, CHUNK:P], v[HD:P], ACT.Copy).then_inc(v_built, 1)

            wkv_build(0)
            for slot in range(PAIRS + 1):
                for step, p, j, h in wkv_steps(slot):
                    half = slice(2 * h, 2 * h + 2)
                    if step == "tok":
                        for n, (dst, src) in ((0, (v_tok, un[0])), (1, (b_tok, un[1]))) if h == 0 else ((2, (k_tok, un[0])),):
                            act.wait_ge(tok_done, 3 * p + n + 1)
                            A_(dst[p % 2][:], bank4(src), ACT.Copy).then_inc(tok_out, 1)
                    elif step == "x1":
                        act.wait_ge(x1_done, 2 * p + h + 1)
                        A_(inv_x[:, half, :], bank4(acc[h])[:, 0:2, :], ACT.Copy).then_inc(x1_out, 1)
                        if h == 1 and p + 1 < PAIRS:
                            wkv_build(p + 1)
                    elif step == "t1":
                        act.wait_ge(t1_done, 10 * p + 2 * (j - 1) + h + 1)
                        A_(t1[:, half, :], bank4(acc[h])[:, 0:2, :], ACT.Copy).then_inc(t1_out, 1)
                    elif step == "rhs":
                        act.wait_ge(rhs_done, CHUNKS * p + j + 1)
                        A_(wkv_rhs[:], stat_ps[:, 0, 0:P], ACT.Copy).then_inc(rhs_out, 1)
                    elif step == "u":
                        act.wait_ge(u_done, CHUNKS * p + j + 1)
                        A_(wkv_u[:], stat_ps[:, 0, 0:P], ACT.Copy).then_inc(u_out, 1)
            for j in range(4):
                act.wait_ge(yc_ready, j + 1)
                A_(rw_kk[:, 2 * j:2 * j + 2, :], y_wkv[:, 2 * j:2 * j + 2, :], ACT.Square).then_inc(ycsq_ready, 1)
            for j in range(4):
                act.wait_ge(gv_ready, j + 1)
                A_(rw_kk[:, 2 * j:2 * j + 2, :], rw_kk[:, 2 * j:2 * j + 2, :], ACT.Sqrt).then_inc(gv_root, 1)
            for j in range(4):
                z_split(Z_RW + j, j)
            for j in range(UPD):
                split(U_RWO + j + 2)
            norm_stats(N_MLP1)
            norm_split(H_BASE[N_MLP1], h_hi, mods[1][:, 24:32])
            mlp(1)
            norm_stats(N_FIN1)

            def attention(kind, z0):
                b = HEADS * kind
                for i in range(HEADS + 6):
                    if i < HEADS:
                        act.wait_ge(max_ready, b + i + 1)
                        if b + i >= NA:
                            act.wait_ge(pt_done, b + i - NA + 1)
                        for qt in range(QT):
                            A_(probs[i % NA][:, qt, :], logit[i % NA][:, qt, :], ACT.Exp, bias=stat[i % NA][:, qt:qt + 1],
                               accum_out=stat[i % NA][:, 2 + qt:3 + qt]).then_inc(exp_done, 1)
                    if 2 <= i < HEADS + 2:
                        k = i - 2
                        act.wait_ge(pt_done, b + k + 1)
                        if b + k >= 2:
                            act.wait_ge(pv_done, b + k - 1)
                        A_(probs_t[k % 2][:], (stat_ps, misc)[k % 2][:, :, :].rearrange("p a s -> p (a s)")[:, 0:3 * P]
                           .rearrange("p (c q) -> p c q", c=3), ACT.Copy).then_inc(pt_out, 1)
                    if i >= 9 and (i - 9) % 4 == 0:
                        z_split(z0 + (i - 9) // 4, (i - 9) // 4)

            norm_stats(N_A)
            norm_split(H_BASE[N_A], h_hi, None)

            def rope_load(u, v, r, n, scale=1.0, signal=None):
                act.wait_ge(unit_done, u + 1)
                if r >= 2:
                    act.wait_ge(rope_done, r - 1)
                A_(rope_in[r % 2][:, 0:n, :], un[v % 2][:, 0:n, :], ACT.Copy, scale=scale).then_inc(signal or un_free, 1)

            rope_load(U_KI, V_A, ROPE_KI, 1, signal=ki_loaded)
            split(U_KI + 2)
            act.wait_ge(un_free, freed(V_A))
            for j in range(2):
                rope_load(U_QI + j, V_A + 1 + j, ROPE_QI + j, 2)
                split(U_QI + j + 2)
            rope_load(U_KA, V_A + 3, ROPE_K, 2)
            split(U_KA + 2)
            evac(U_VA, V_A + 4, vA_tok[:])
            split(U_VA + 2)
            act.wait_ge(rope_done, ROPE_K + 1)
            for j in range(KV_HEADS):
                src = kA_fm[HD * (j % 2):HD * (j % 2) + HD, j // 2, :]
                A_(k_dup[0:HD, j, :], src, ACT.Copy)
                A_(k_dup[HD:P, j, :], src, ACT.Copy).then_inc(kdup_ready, 1)
            for j in range(UPD):
                rope_load(U_QA + j, V_A + 5 + j, ROPE_Q + j, 2, scale=HD ** -0.5)
                split(U_QA + j + 2)
            attention(0, Z_A)
            for j in range(UPD):
                split(U_OA + j + 2)
            norm_stats(N_MLP2)
            norm_split(H_BASE[N_MLP2], h_hi, None)
            mlp(2)
            norm_stats(N_B)
            norm_split(H_BASE[N_B], h_hi, None)
            norm_split(H_BASE["B_q"], z_hi, None)
            split(U_F + 2)
            act.wait_ge(f_abs, 1)
            A_(f_l[:], f_e[:], ACT.Exp, scale=-1.0).then_inc(f_exp, 1)
            act.wait_ge(f_one, 1)
            A_(f_l[:], f_l[:], ACT.Ln).then_inc(f_log, 1)
            for j in range(UPD):
                evac(U_KB + j, V_B + 1 + j, kB_fm[:, 2 * j:2 * j + 2, :])
                split(U_KB + j + 2)
            for r in range(8):
                act.wait_ge(f_bcast, r + 1)
                A_(cum_k[:, 2 * r:2 * r + 2, :], acc[r % 4][:], ACT.Copy).then_inc(cumk_ready, 1)
            for j in range(UPD):
                evac(U_VB + j, V_B + 5 + j, vB_tok[:, :, UC * j:UC * (j + 1)])
                split(U_VB + j + 2)
            for j in range(UPD):
                evac(U_QB + j, V_B + 9 + j, q_fm[:, 2 * j:2 * j + 2, :], scale=HD ** -0.5)
                split(U_QB + j + 2)
            attention(1, Z_B)
            for j in range(UPD):
                split(U_OB + j + 2)
            norm_stats(N_MLP3)
            norm_split(H_BASE[N_MLP3], h_hi, None)
            mlp(3)
            norm_stats(N_OUT)

        @block.vector
        def _(dve):
            V = nc.vector
            chain = sem("dve_chain")
            count = [0]

            def link(ins):
                count[0] += 1
                ins.then_inc(chain, 1)
                dve.wait_ge(chain, count[0])

            def split(u):
                if u >= NU:
                    return
                n = unit_cols(u)
                dve.wait_ge(hi_made, u + 1)
                V.tensor_tensor(w_lo[u % 2][:, :, 0:n], stage[u % NSTAGE][:, :, 0:n], w_hi[u % 2][:, :, 0:n].bitcast(F32),
                                ALU.subtract).then_inc(lo_made, 1)

            def norm_stats(n):
                dve.wait_ge(stat_done, n + 1)
                V.tensor_scalar(rstd[:, 0, :], stat_ps[:, 0, :], NORM_EPS, None, ALU.add).then_inc(ms_ready, 1)
                dve.wait_ge(std_ready, n + 1)
                link(V.reciprocal(rstd[:, 2, :], rstd[:, 1, :]))
                link(V.tensor_tensor(rstd[:, 1, :], rstd[:, 2, :], rstd[:, 2, :], ALU.mult))
                link(V.tensor_tensor(rstd[:, 1, :], rstd[:, 1, :], rstd[:, 0, :], ALU.mult))
                link(V.tensor_scalar(rstd[:, 1, :], rstd[:, 1, :], -0.5, 1.5, ALU.mult, ALU.add))
                link(V.tensor_tensor(rstd[:, 2, :], rstd[:, 2, :], rstd[:, 1, :], ALU.mult))

            def norm_mul(dst, t, g):
                return V.scalar_tensor_tensor(out=dst[:, t, :], in0=x[:, t, :], scalar=g[:, t:t + 1], in1=rstd[:, 2, :],
                                              op0=ALU.mult, op1=ALU.mult)

            def norm_split(base, g, shift, hi, lo):
                for t in range(KT + 2):
                    if t < KT:
                        norm_mul(tmp, t, g).then_inc(normed, 1)
                    if t >= 2:
                        k = t - 2
                        dve.wait_ge(h_hi_made, base + k + 1)
                        if shift is None:
                            ins = V.tensor_tensor(lo[:, k, :], tmp[:, k, :], hi[:, k, :].bitcast(F32), ALU.subtract)
                        else:
                            ins = V.scalar_tensor_tensor(out=lo[:, k, :], in0=tmp[:, k, :], scalar=shift[:, k:k + 1],
                                                         in1=hi[:, k, :].bitcast(F32), op0=ALU.add, op1=ALU.subtract)
                        ins.then_inc(h_lo_made, 1)

            def z_split(zc, j):
                dve.wait_ge(z_hi_made, zc + 1)
                V.tensor_tensor(z_lo[:, 2 * j:2 * j + 2, :], zf[zc % 2][:], z_hi[:, 2 * j:2 * j + 2, :].bitcast(F32),
                                ALU.subtract).then_inc(z_lo_made, 1)

            def residual(u, gate, j, b):
                dve.wait_ge(unit_done, u + 1)
                for m in range(2):
                    t = 2 * j + m
                    if gate is None:
                        ins = V.tensor_tensor(x[:, t, :], b[:, m, :], x[:, t, :], ALU.add)
                    else:
                        ins = V.scalar_tensor_tensor(out=x[:, t, :], in0=b[:, m, :], scalar=gate[:, t:t + 1], in1=x[:, t, :],
                                                     op0=ALU.mult, op1=ALU.add)
                    ins.then_inc(x_ready, 1)

            def mlp(m, gate):
                u, v, zc = U_MLP[m], V_MLP[m], Z_MLP[m]
                for g in range(GROUPS):
                    for j in range(UPD):
                        uu = u + 2 * UPD * g + j
                        k = zc + UPD * g + j
                        dve.wait_ge(relu_ready, 4 * GROUPS * m + UPD * g + j + 1)
                        V.scalar_tensor_tensor(out=zf[k % 2][:], in0=un[(v + j) % 2][:], scalar=0.0, in1=relu_b[j % 2][:],
                                               op0=ALU.max, op1=ALU.mult).then_inc(zf_ready, 1)
                        dve.wait_ge(zf_ready, k + 1)
                        V.engine_nop().then_inc(un_free, 1)
                        if j < UPD - 1:
                            split(uu + 2)
                            z_split(k, j)
                        else:
                            z_split(k, j)
                            split(uu + 2)
                    for j in range(UPD):
                        split(u + 2 * UPD * g + UPD + j + 2)
                        if m == 0 and j in (0, UPD - 1):
                            ada()
                        if g == GROUPS - 1:
                            residual(u + 2 * UPD * g + UPD + j, gate, j, acc[j])

            dve.wait_ge(tp_done, 1)
            V.tensor_copy(vecT[:], un[0][:, :, :].rearrange("p a s -> p (a s)")[:, 0:N_VEC]).then_inc(un_free, 1)
            for j in range(4):
                dve.wait_ge(tp_done, 2 + j)
                V.tensor_copy(x[:, 2 * j:2 * j + 2, :], un[(V_X + j) % 2][:]).then_inc(x_ready, 2)
            dve.wait_ge(silu_e, 1)
            link(V.tensor_scalar(small[:, 16:24], small[:, 8:16], 1.0, None, ALU.add))
            link(V.reciprocal(small[:, 24:32], small[:, 16:24]))
            V.tensor_tensor(c_silu, vecT[:, VEC_C:VEC_C + KT], small[:, 24:32], ALU.mult).then_inc(silu_ready, 1)
            dve.wait_ge(silu_ready, 1)
            norm_stats(N_CONV)

            ada_done = [0]

            def ada():
                k = ada_done[0]
                ada_done[0] += 1
                a = ADA_DVE[k]
                if a < ADA_FIRST:
                    dve.wait_ge(ada_first_landed[a], 16)
                    w = ada_first[a]
                else:
                    dve.wait_ge(ada_dve_landed, 16 * (k + 1 - ada_count(ADA_DVE, ADA_FIRST)))
                    w = ada_dve
                    if a >= N_ADA > ADA_DVE[k - 1]:
                        dve.wait_ge(ada_summed, 4)
                dst = ada_acc[:, a % N_ADA * UC:(a % N_ADA + 1) * UC]
                link(V.tensor_scalar(dst, w[:, 0, :], c_silu[:, 0:1], None, ALU.mult))
                for t in range(1, KT):
                    ins = V.scalar_tensor_tensor(out=dst, in0=w[:, t, :], scalar=c_silu[:, t:t + 1], in1=dst, op0=ALU.mult, op1=ALU.add)
                    if t < KT - 1:
                        link(ins)
                ins.then_inc(ada_dve_done, 1)

            def mod_out(layer, c0, c1, k):
                dve.wait_ge(ada_summed_pe, k)
                V.tensor_tensor(mods[layer][:, c0:c1], misc[:, 0, c0:c1], vecT[:, VEC_ADA_B + 48 * layer + c0:VEC_ADA_B + 48 * layer + c1],
                                ALU.add).then_inc(ada_summed, 1)
                dve.wait_ge(ada_summed, k)

            def mod_gain(layer, sub):
                link(V.scalar_tensor_tensor(out=gain[:, 2 * layer + sub, :], in0=mods[layer][:, 24 * sub + 8:24 * sub + 16], scalar=1.0,
                                            in1=vecT[:, VEC_NORM_G + 8 * (2 * layer + sub):VEC_NORM_G + 8 * (2 * layer + sub) + 8],
                                            op0=ALU.add, op1=ALU.mult))

            for _ in range(ada_count(ADA_DVE, ADA_FIRST)):
                ada()
            split(0)
            split(1)
            mod_out(0, 0, 16, 1)
            mod_gain(0, 0)
            norm_split(H_BASE[N_CONV], gain[:, 0, :], mods[0][:, 0:8], h_hi, h_lo)
            link(V.memset(u_pad[:, :, 0:2], 0.0))
            conv_w = [vecT[:, VEC_CONV_W + 8 * k:VEC_CONV_W + 8 * k + 8] for k in range(3)]
            for j in range(12):
                if j < 8:
                    split(U_CONV_IN + j + 2)
                else:
                    k = j - 8
                    t0 = 2 * k
                    dve.wait_ge(unit_done, U_CONV_IN + j + 1)
                    dve.wait_ge(un_free, freed(V_CONV + 7))
                    V.tensor_tensor(u_pad[:, t0:t0 + 2, 2:PADT], un[(V_CONV + j) % 2][:], tmp[:, t0:t0 + 2, :], ALU.mult).then_inc(un_free, 1)
                    dve.wait_ge(un_free, freed(V_CONV + j))
                    for m in range(2):
                        ins = V.tensor_scalar(conv_y[:, m, :], u_pad[:, t0 + m, 2:PADT], conv_w[2][:, t0 + m:t0 + m + 1], None, ALU.mult)
                    link(ins)
                    for tap in (1, 0):
                        for m in range(2):
                            ins = V.scalar_tensor_tensor(out=conv_y[:, m, :], in0=u_pad[:, t0 + m, tap:tap + SEQ],
                                                         scalar=conv_w[tap][:, t0 + m:t0 + m + 1], in1=conv_y[:, m, :],
                                                         op0=ALU.mult, op1=ALU.add)
                        link(ins)
                    V.tensor_tensor(zf[(Z_CONV + k) % 2][:], conv_y[:], b_gate[:, t0:t0 + 2, :], ALU.mult).then_inc(zf_ready, 1)
                    split(U_CONV_IN + j + 2)
                    z_split(Z_CONV + k, k)
                if j % 2:
                    ada()
            mod_out(0, 16, 24, 2)
            for j in range(UPD):
                split(U_CONV_OUT + j + 2)
                residual(U_CONV_OUT + j, mods[0][:, 16:24], j, acc[j])
            norm_stats(N_MLP0)
            mod_out(0, 24, 40, 3)
            mod_gain(0, 1)
            norm_split(H_BASE[N_MLP0], gain[:, 1, :], mods[0][:, 24:32], h_hi, h_lo)
            mod_out(0, 40, 48, 4)
            mlp(0, mods[0][:, 40:48])
            norm_stats(N_RW)
            mod_out(1, 0, 48, 5)
            mod_gain(1, 0)
            mod_gain(1, 1)
            for t in range(KT):
                ins = norm_mul(tmp, t, gain[:, 2, :])
            link(ins)
            for t in range(KT):
                ins = V.tensor_scalar(tmp[:, t, :], tmp[:, t, :], mods[1][:, t:t + 1], None, ALU.add)
            link(ins)
            V.tensor_tensor(sq[:, :, 1:SEQ], tmp[:, :, 0:SEQ - 1], tmp[:, :, 1:SEQ], ALU.subtract)
            link(V.tensor_scalar(sq[:, :, 0:1], tmp[:, :, 0:1], -1.0, None, ALU.mult))

            def mix(dst, t, which):
                c = VEC_MU + 8 * which + t
                return V.scalar_tensor_tensor(out=dst, in0=sq[:, t, :], scalar=vecT[:, c:c + 1], in1=tmp[:, t, :], op0=ALU.mult, op1=ALU.add)

            for dst, which in ((rw_r, 1), (rw_k, 4), (rw_v, 5)):
                for t in range(KT):
                    ins = mix(dst[:, t, :], t, which)
                ins.then_inc(lora_mixed, 1)
            mix_dst = ((h_hi, h_lo), (z_hi, z_lo), (h_hi, h_lo))
            mix_mu = (2, 0, 3)

            def mixes(m0, m1):
                for m in range(m0, m1 + 2):
                    if m < m1:
                        if m >= 4:
                            dve.wait_ge(mix_lo, m - 3)
                        mix(mixf[:, m % 4, :], m % KT, mix_mu[m // KT]).then_inc(mix_ready, 1)
                    if m - 2 >= m0:
                        k = m - 2
                        hi, lo = mix_dst[k // KT]
                        dve.wait_ge(mix_hi, k + 1)
                        V.tensor_tensor(lo[:, k % KT, :], mixf[:, k % 4, :], hi[:, k % KT, :].bitcast(F32), ALU.subtract).then_inc(mix_lo, 1)

            mixes(0, 2 * KT)
            dve.wait_ge(lora2_out, 8)
            for t in range(KT):
                ins = V.tensor_tensor_scan(rw_c[:, t, :], c_("resets"), rw_c[:, t, :], 0.0, ALU.mult, ALU.add)
            ins.then_inc(cum_ready, 1)
            for j in range(12):
                if j == 4:
                    dve.wait_ge(unit_done, U_RWK + 4)
                    mixes(2 * KT, 3 * KT)
                split(U_RWK + j + 2)
                if j == 4:
                    dve.wait_ge(un_free, freed(V_RKV + 3))
                    dve.wait_ge(mix_lo, 3 * KT)
                    for k in range(4):
                        for t in (2 * k, 2 * k + 1):
                            ins = V.tensor_scalar(rw_kk[:, t, :], rw_k[:, t, :], vecT[:, VEC_KK + t:VEC_KK + t + 1], None, ALU.mult)
                        ins.then_inc(kk0_ready, 1)
                if j == 6:
                    for k in range(4):
                        dve.wait_ge(ss_done, k + 1)
                        V.tensor_scalar(tmp[:, 2 * k:2 * k + 2, :], acc[k][:], 1e-24, None, ALU.max).then_inc(ss_ready, 1)
                if j == 7:
                    for k in range(4):
                        s2 = slice(2 * k, 2 * k + 2)
                        dve.wait_ge(ss_root, k + 1)
                        ins = V.reciprocal(tmp[:, s2, :], tmp[:, s2, :])
                    link(ins)
                    link(V.scalar_tensor_tensor(out=rw_kk[:], in0=rw_kk[:], scalar=-1.0, in1=tmp[:], op0=ALU.mult, op1=ALU.mult))
                if j == 8:
                    dve.wait_ge(lora2_out, 16)
                    for t in range(KT):
                        ins = V.tensor_scalar(tmp[:, t, :], rw_a[:, t, :], -1.0, vecT[:, VEC_KA + t:VEC_KA + t + 1], ALU.add, ALU.mult)
                    link(ins)
                    V.scalar_tensor_tensor(out=rw_k[:], in0=tmp[:], scalar=1.0, in1=rw_k[:], op0=ALU.add, op1=ALU.mult)
                    V.scalar_tensor_tensor(out=rw_a[:], in0=rw_a[:], scalar=-1.0, in1=rw_kk[:], op0=ALU.mult, op1=ALU.mult).then_inc(sem("rw_ready"), 1)
            dve.wait_ge(unit_done, U_RWV + 4)
            dve.wait_ge(end_ready, 1)
            bc4 = lambda m, n: m.unsqueeze(1).to_broadcast([P, n, m.shape[-1]])
            for slot in range(PAIRS + 1):
                for step, p, j, h in wkv_steps(slot):
                    half = slice(2 * h, 2 * h + 2)
                    xt = inv_t[p % 2]
                    if step == "gram":
                        dve.wait_ge(g_done, 2 * p + h + 1)
                        raw_n, raw_k = acc[h][:, :, 0:P], acc[2 + h]
                        V.tensor_tensor(xt[:, half, :], raw_n, bc4(level_t[:, 0, :], 2), ALU.mult)
                        V.tensor_tensor(n_t[:, half, :], raw_n, bc4(c_("before"), 2), ALU.mult)
                        link(V.tensor_tensor(n_m[0][:, half, :], raw_n, bc4(level_t[:, 1, :], 2), ALU.mult))
                        V.tensor_tensor(xt[:, half, :], xt[:, half, :], bc4(ident, 2), ALU.add).then_inc(inv_ready, 1)
                        V.tensor_tensor(lak_t[p % 2][:, half, :], raw_k[:, :, 0:P], bc4(c_("before"), 2), ALU.mult)
                        V.tensor_tensor(lrb_t[p % 2][:, half, :], raw_k[:, :, P:P + CHUNK], bc4(c_("upto"), 2), ALU.mult)
                        V.tensor_tensor(lrk_t[p % 2][:, half, :], raw_k[:, :, P + CHUNK:P + 2 * CHUNK], bc4(c_("upto"), 2), ALU.mult).then_inc(lak_ready, 1)
                    elif step == "dx":
                        dve.wait_ge(dx_done, 10 * p + 2 * (j - 1) + h + 1)
                        if j < WKV_LEVELS[-1]:
                            V.tensor_tensor(inv_x[:, half, :], bank4(acc[2 + h])[:, 0:2, :], inv_x[:, half, :], ALU.add)
                        V.tensor_tensor(xt[:, half, :], bank4(un[h])[:, 0:2, :], xt[:, half, :], ALU.add).then_inc(inv_ready, 1)
                    elif step == "sy":
                        c = j
                        last = w_end[:, p, c:c + 1]
                        if c < CHUNKS - 1:
                            k = (CHUNKS - 1) * p + c
                            if c:
                                dve.wait_ge(state_ready, k)
                                link(V.tensor_scalar(state_kept[:], state[(c - 1) % 2][:], last, None, ALU.mult))
                            dve.wait_ge(s_done, k + 1)
                            if c == 0:
                                V.tensor_scalar(state[0][:], stat_ps[:, 0, 0:P], last, None, ALU.mult).then_inc(state_ready, 1)
                            else:
                                V.scalar_tensor_tensor(out=state[c % 2][:], in0=stat_ps[:, 0, 0:P], scalar=last, in1=state_kept[:],
                                                       op0=ALU.mult, op1=ALU.add).then_inc(state_ready, 1)
                        dve.wait_ge(y_done, CHUNKS * p + c + 1)
                        V.tensor_copy(y_wkv[:, p, CHUNK * c:CHUNK * (c + 1)], misc[:, 0, 0:CHUNK]).then_inc(y_out, 1)
            for t in range(KT):
                ins = V.scalar_tensor_tensor(out=rw_c[:, t, :], in0=rw_r[:, t, :], scalar=vecT[:, VEC_RK + t:VEC_RK + t + 1],
                                             in1=rw_k[:, t, :], op0=ALU.mult, op1=ALU.mult)
            ins.then_inc(rk_ready, 1)
            bonus_bank = (stat_ps, misc, un[0], un[1])
            for j in range(4):
                s2 = slice(2 * j, 2 * j + 2)
                dve.wait_ge(gn_mean_done, j + 1)
                V.tensor_tensor(y_wkv[:, s2, :], y_wkv[:, s2, :], acc[j][:], ALU.subtract).then_inc(yc_ready, 1)
            for j in range(4):
                s2 = slice(2 * j, 2 * j + 2)
                dve.wait_ge(gn_var_done, j + 1)
                V.tensor_scalar(rw_kk[:, s2, :], acc[j][:], GN_EPS, None, ALU.add).then_inc(gv_ready, 1)
            for j in range(4):
                s2 = slice(2 * j, 2 * j + 2)
                dve.wait_ge(gv_root, j + 1)
                link(V.reciprocal(rw_kk[:, s2, :], rw_kk[:, s2, :]))
                link(V.tensor_tensor(y_wkv[:, s2, :], y_wkv[:, s2, :], rw_kk[:, s2, :], ALU.mult))
                for t in (2 * j, 2 * j + 1):
                    V.tensor_scalar(y_wkv[:, t, :], y_wkv[:, t, :], vecT[:, VEC_LNW + t:VEC_LNW + t + 1], vecT[:, VEC_LNB + t:VEC_LNB + t + 1],
                                    ALU.mult, ALU.add)
                dve.wait_ge(bonus_done, j + 1)
                link(V.tensor_tensor(rw_v[:, s2, :], bonus_bank[j][:], rw_v[:, s2, :], ALU.mult))
                link(V.tensor_tensor(y_wkv[:, s2, :], y_wkv[:, s2, :], rw_v[:, s2, :], ALU.add))
                V.tensor_tensor(zf[(Z_RW + j) % 2][:], y_wkv[:, s2, :], g_wkv[:, s2, :], ALU.mult).then_inc(zf_ready, 1)
                if j:
                    z_split(Z_RW + j - 1, j - 1)
            z_split(Z_RW + 3, 3)
            for j in range(UPD):
                split(U_RWO + j + 2)
                residual(U_RWO + j, mods[1][:, 16:24], j, acc[j])
            norm_stats(N_MLP1)
            norm_split(H_BASE[N_MLP1], gain[:, 3, :], mods[1][:, 24:32], h_hi, h_lo)
            mlp(1, mods[1][:, 40:48])
            norm_stats(N_FIN1)
            for t in range(KT):
                norm_mul(x, t, vecT[:, VEC_FINAL:VEC_FINAL + KT]).then_inc(x_ready, 1)

            def rope(r, n, dst):
                dve.wait_ge(rot_done, r + 1)
                V.tensor_tensor(rope_c[:, 0:n, :], rope_in[r % 2][:, 0:n, :], bc4(c_("cos"), n), ALU.mult)
                link(V.tensor_tensor(dst, misc[:, 0:n, :], bc4(c_("sin"), n), ALU.mult))
                V.tensor_tensor(dst, dst, rope_c[:, 0:n, :], ALU.add).then_inc(rope_done, 1)

            def attention(kind, z0):
                b = HEADS * kind
                for i in range(HEADS + 6):
                    if i < HEADS:
                        lg, st = logit[i % NA], stat[i % NA]
                        dve.wait_ge(qk_done, b + i + 1)
                        if kind == 0:
                            link(V.tensor_tensor(lg[:], acc[i % 4][:], sel_bias[:], ALU.add))
                        else:
                            dve.wait_ge(sem("bias_ready"), i + 1)
                            for qt in range(QT):
                                ins = V.scalar_tensor_tensor(out=lg[:, qt, :], in0=acc[i % 4][:, qt, :], scalar=cum_q[:, qt, i:i + 1],
                                                             in1=head_bias[i % 2][:, qt, :], op0=ALU.add, op1=ALU.add)
                            link(ins)
                        V.tensor_reduce(st[:, 0:QT], lg[:], AX_X, ALU.max, negate=True).then_inc(max_ready, 1)
                    if 1 <= i <= HEADS:
                        k = i - 1
                        st = stat[k % NA]
                        dve.wait_ge(exp_done, QT * (b + k + 1))
                        link(V.reciprocal(st[:, 4:4 + QT], st[:, 2:2 + QT]))
                        for qt in range(QT):
                            ins = V.tensor_scalar(probs[k % NA][:, qt, :], probs[k % NA][:, qt, :], st[:, 4 + qt:5 + qt], None, ALU.mult)
                        ins.then_inc(p_ready, 1)
                    if i >= 7 and (i - 7) % 4 == 0:
                        j = (i - 7) // 4
                        dve.wait_ge(pv_done, b + 4 * j + 4)
                        V.tensor_copy(zf[(z0 + j) % 2][:], un[j % 2][:]).then_inc(zf_ready, 1)
                    if i >= 9 and (i - 9) % 4 == 0:
                        z_split(z0 + (i - 9) // 4, (i - 9) // 4)

            norm_stats(N_A)
            norm_split(H_BASE[N_A], vecT[:, VEC_GA:VEC_GA + KT], None, h_hi, h_lo)
            dve.wait_ge(const_b_in, 16)
            dve.wait_ge(ki_loaded, 1)
            V.tensor_scalar(wi_tok[:], un[V_A % 2][:, 1, 0:QT * IDX_HEADS].rearrange("p (a h) -> p a h", a=QT),
                            IDX_HEADS ** -0.5 * HD ** -0.5, None, ALU.mult).then_inc(un_free, 1)

            def scores(qt):
                dve.wait_ge(score_done, qt + 1)
                dst = score[:, qt, :]
                for h in range(IDX_HEADS):
                    b, o = acc[2 * (h // 4) + h % 2], h // 2 % 2
                    w = wi_tok[:, qt, h:h + 1]
                    if h == 0:
                        link(V.tensor_scalar(dst, b[:, o, :], 0.0, w, ALU.max, ALU.mult))
                    else:
                        link(V.tensor_scalar(score_t[h % 2][:], b[:, o, :], 0.0, w, ALU.max, ALU.mult))
                        ins = V.tensor_tensor(dst, dst, score_t[h % 2][:], ALU.add)
                        if h < IDX_HEADS - 1:
                            link(ins)
                        else:
                            ins.then_inc(score_used, 1)
                dve.wait_ge(score_used, qt + 1)
                link(V.tensor_tensor(dst, dst, admit[:, qt, :], ALU.add))

            def select(qt):
                w = score[:, qt, :]
                for _ in range(TOPK // 8):
                    link(V.max(top8[:], w))
                    link(V.match_replace(w, top8[:], w, TAKEN))
                link(V.tensor_scalar(sel_bias[:, qt, :], w, 0.5 * TAKEN, NEG, ALU.is_gt, ALU.mult))

            split(U_KI + 2)
            split(U_QI + 2)
            rope(ROPE_KI, 1, ki_fm[:])
            split(U_QI + 3)
            rope(ROPE_QI, 2, qi_fm[:, 0:2, :])
            split(U_KA + 2)
            rope(ROPE_QI + 1, 2, qi_fm[:, 2:4, :])
            split(U_VA + 2)
            rope(ROPE_K, 2, kA_fm[:])
            scores(0)
            split(U_QA + 2)
            scores(1)
            split(U_QA + 3)
            rope(ROPE_Q, 2, q_fm[:, 0:2, :])
            select(0)
            split(U_QA + 4)
            rope(ROPE_Q + 1, 2, q_fm[:, 2:4, :])
            select(1)
            split(U_QA + 5)
            rope(ROPE_Q + 2, 2, q_fm[:, 4:6, :])
            rope(ROPE_Q + 3, 2, q_fm[:, 6:8, :])
            attention(0, Z_A)
            for j in range(UPD):
                split(U_OA + j + 2)
                residual(U_OA + j, None, j, acc[j])
            norm_stats(N_MLP2)
            norm_split(H_BASE[N_MLP2], vecT[:, VEC_GMLP:VEC_GMLP + KT], None, h_hi, h_lo)
            mlp(2, None)
            norm_stats(N_B)
            norm_split(H_BASE[N_B], vecT[:, VEC_GKV:VEC_GKV + KT], None, h_hi, h_lo)
            norm_split(H_BASE["B_q"], vecT[:, VEC_GB:VEC_GB + KT], None, z_hi, z_lo)
            split(U_F + 2)
            dve.wait_ge(unit_done, U_F + 1)
            dve.wait_ge(bf_loaded, 16)
            V.tensor_scalar(f_z[:], un[V_B % 2][0:HEADS, 0, :], b_f[:, 0:1], None, ALU.add).then_inc(un_free, 1)
            dve.wait_ge(un_free, freed(V_B))
            V.scalar_tensor_tensor(out=f_e[:], in0=f_z[:], scalar=-1.0, in1=f_z[:], op0=ALU.mult, op1=ALU.max).then_inc(f_abs, 1)
            dve.wait_ge(f_exp, 1)
            V.tensor_scalar(f_l[:], f_l[:], 1.0, None, ALU.add).then_inc(f_one, 1)
            dve.wait_ge(f_log, 1)
            link(V.scalar_tensor_tensor(out=f_e[:], in0=f_z[:], scalar=0.0, in1=f_l[:], op0=ALU.min, op1=ALU.subtract))
            link(V.tensor_tensor_scan(f_cum[:], ones_w[0:HEADS, 0:1].to_broadcast([HEADS, SEQ]), f_e[:], 0.0, ALU.mult, ALU.add))
            V.tensor_scalar(f_neg[:], f_cum[:], -1.0, None, ALU.mult).then_inc(f_ready, 1)
            for j in range(2 * UPD):
                split(U_KB + j + 2)
                if j == UPD:
                    dve.wait_ge(cumq_ready, 1)
                    link(V.tensor_copy(cum_q[:], misc[:, 0, 0:QT * HEADS].rearrange("p (a h) -> p a h", a=QT)))
            for j in range(UPD):
                split(U_QB + j + 2)
            attention(1, Z_B)
            for j in range(UPD):
                split(U_OB + j + 2)
                residual(U_OB + j, None, j, acc[j])
            norm_stats(N_MLP3)
            norm_split(H_BASE[N_MLP3], vecT[:, VEC_GMLP + KT:VEC_GMLP + 2 * KT], None, h_hi, h_lo)
            mlp(3, None)
            norm_stats(N_OUT)
            for t in range(KT):
                norm_mul(tmp, t, vecT[:, VEC_GFIN:VEC_GFIN + KT]).then_inc(normed, 1)
            for k in range(4):
                dve.wait_ge(tp_done, 5 + k + 1)
                V.tensor_copy(out_tok[:, k // 2, 512 * (k % 2):512 * (k % 2) + 512],
                              un[(V_OUT + k) % 2][:, :, :].rearrange("p a s -> p (a s)")).then_inc(un_free, 1)

        @block.tensor
        def _(pe):
            MM = nc.tensor.matmul

            def three(out, hi_l, lo_l, hi_r, lo_r, start, stop):
                MM(out, hi_l, hi_r, start=start, stop=False, skip_group_check=True)
                MM(out, hi_l, lo_r, start=False, stop=False, skip_group_check=True)
                return MM(out, lo_l, hi_r, start=False, stop=stop, skip_group_check=True)

            def free_bank(v):
                if v >= V_CONV + 2:
                    pe.wait_ge(un_free, freed(v - 2))

            def unit(u, bank, xs, ready=None, tokens=False, first=True, last=True):
                xh, xl = xs
                wh, wl = w_hi[u % 2], w_lo[u % 2]
                pe.wait_ge(lo_made, u + 1)
                for kt in range(KT):
                    if ready is not None:
                        ready(kt)
                    for m in range(2):
                        s = first and kt == 0 and m == 0
                        if tokens:
                            q = slice(P * m, P * m + P)
                            ins = three(bank[:, m, :], xh[:, kt, q], xl[:, kt, q], wh[:, kt, :], wl[:, kt, :], s, last and kt == KT - 1)
                        else:
                            c = slice(P * m, P * m + P)
                            ins = three(bank[:, m, :], wh[:, kt, c], wl[:, kt, c], xh[:, kt, :], xl[:, kt, :], s, last and kt == KT - 1)
                ins.then_inc(unit_done, 1)

            def norm_stats(n):
                for t in range(KT):
                    pe.wait_ge(sq_ready, 8 * n + t + 1)
                    if t == 0 and n:
                        pe.wait_ge(ms_ready, n)
                    ins = MM(stat_ps[:, 0, :], mean_w, sq[:, t, :], start=(t == 0), stop=(t == KT - 1))
                ins.then_inc(stat_done, 1)

            def h_ready(base):
                return lambda kt: pe.wait_ge(h_lo_made, base + kt + 1)

            def z_ready(zc):
                return lambda kt: pe.wait_ge(z_lo_made, zc + kt // 2 + 1) if kt % 2 == 0 else None

            def mlp(m, n):
                u, v, zc = U_MLP[m], V_MLP[m], Z_MLP[m]
                for g in range(GROUPS):
                    for j in range(UPD):
                        free_bank(v + UPD * g + j)
                        unit(u + 2 * UPD * g + j, un[(v + j) % 2], (h_hi, h_lo), h_ready(H_BASE[n]) if g == 0 and j == 0 else None)
                    for j in range(UPD):
                        unit(u + 2 * UPD * g + UPD + j, acc[j], (z_hi, z_lo), z_ready(zc + UPD * g) if j == 0 else None,
                             first=(g == 0), last=(g == GROUPS - 1))

            pe.wait_ge(const_in, 32)
            pe.wait_ge(vec_loaded, 16 * VEC_DMAS)
            flat0 = un[0][:, :, :].rearrange("p a s -> p (a s)")
            for i, n in enumerate((P, P, N_VEC - 2 * P)):
                ins = nc.tensor.transpose(flat0[:, P * i:P * i + n], vec_in[0:n, i, :], ident[0:n, 0:n])
            ins.then_inc(tp_done, 1)
            pe.wait_ge(x_loaded, 16)
            for j in range(4):
                if j == 1:
                    pe.wait_ge(un_free, freed(V_VEC))
                if j >= 2:
                    pe.wait_ge(x_ready, 2 * (j - 1))
                for m in range(2):
                    for a in range(QT):
                        ins = nc.tensor.transpose(un[(V_X + j) % 2][:, m, P * a:P * a + P], x_in[:, a, P * (2 * j + m):P * (2 * j + m) + P], ident)
                ins.then_inc(tp_done, 1)

            def ada_sum(c0, c1, k):
                if k > 1:
                    pe.wait_ge(ada_summed, k - 1)
                a_end = (N_ADA if k == 5 else 0) + c1 * P // UC
                pe.wait_ge(ada_dve_done, ada_count(ADA_DVE, a_end))
                pe.wait_ge(ada_pool_done, ada_count(ADA_POOL, a_end))
                for c in range(c0, c1):
                    ins = MM(misc[:, 0, c:c + 1], ada_acc[:, P * c:P * c + P], ones_w[:, 0:1], start=True, stop=True)
                ins.then_inc(ada_summed_pe, 1)

            norm_stats(N_CONV)
            ada_sum(0, 16, 1)
            for j in range(12):
                free_bank(V_CONV + j)
                unit(U_CONV_IN + j, un[(V_CONV + j) % 2], (h_hi, h_lo), h_ready(H_BASE[N_CONV]) if j == 0 else None)
            ada_sum(16, 24, 2)
            for j in range(UPD):
                unit(U_CONV_OUT + j, acc[j], (z_hi, z_lo), z_ready(Z_CONV) if j == 0 else None)
            norm_stats(N_MLP0)
            ada_sum(24, 40, 3)
            ada_sum(40, 48, 4)
            mlp(0, N_MLP0)
            norm_stats(N_RW)
            ada_sum(0, 48, 5)
            pe.wait_ge(lora_loaded, 16 * 7)
            for n, (src, c0, c1, out) in enumerate(((rw_r, 0, RD, acc[0][0:RD, 0, :]), (rw_k, RD, RD + RA, acc[1][RD:RD + RA, 0, :]),
                                                    (rw_v, RD + RA, RD + RA + P, acc[2][:, 0, :]),
                                                    (rw_v, RD + RA + P, RD + RA + RG, acc[3][0:RG - P, 0, :]))):
                pe.wait_ge(lora_mixed, min(n, 2) + 1)
                for t in range(KT):
                    ins = MM(out, lora1[:, t, c0:c1], src[:, t, :], start=(t == 0), stop=(t == KT - 1))
                if n != 2:
                    ins.then_inc(lora1_done, 1)
            for which, (rows_, w) in enumerate(((slice(0, RD), lora_w2), (slice(RD, RD + RA), lora_a2))):
                pe.wait_ge(lora1_out, 4)
                for t in range(KT):
                    if which and t % 2 == 0:
                        pe.wait_ge(lora2_out, t + 2)
                    ins = MM(acc[t // 2][:, t % 2, :], w[rows_, P * t:P * t + P], lora_h[rows_, which, :], start=True, stop=True)
                    if t % 2:
                        ins.then_inc(lora2_done, 1)

            def mix_done(m0):
                return lambda kt: pe.wait_ge(mix_lo, m0 + kt + 1)

            for j in range(12):
                free_bank(V_RKV + j)
                unit(U_RWK + j, un[(V_RKV + j) % 2], ((h_hi, h_lo), (z_hi, z_lo), (h_hi, h_lo))[j // 4],
                     mix_done(KT * (j // 4)) if j % 4 == 0 else None)
                if j == 5:
                    pe.wait_ge(lora2_out, 16)
                    for k in range(4):
                        pe.wait_ge(kksq_ready, k + 1)
                        for m in range(2):
                            ins = MM(acc[k][:, m, :], head_ones, tmp[:, 2 * k + m, :], start=True, stop=True)
                        ins.then_inc(ss_done, 1)
                if j == 7:
                    for t in range(KT):
                        if t % 2 == 0:
                            pe.wait_ge(ss_ready, t // 2 + 1)
                        MM(acc[t // 2][:, t % 2, :], lora_g2a[:, P * t:P * t + P], lora_h[:, 2, :], start=True, stop=False)
                        ins = MM(acc[t // 2][:, t % 2, :], lora_g2b[:, P * t:P * t + P], lora_h[0:RG - P, 3, :], start=False, stop=True)
                        if t % 2:
                            ins.then_inc(lora2_done, 1)
            pe.wait_ge(lora2_out, 20)
            pe.wait_ge(un_free, freed(V_RKV + 11))
            for slot in range(PAIRS + 1):
                for step, p, j, h in wkv_steps(slot):
                    half = (2 * h, 2 * h + 1)
                    xt = inv_t[p % 2]
                    if step == "gram":
                        pe.wait_ge(built, p + 1)
                        for c in half:
                            a_, r_ = ar[p % 2][:, c, 0:P], ar[p % 2][:, c, P:P + CHUNK]
                            MM(acc[h][:, c % 2, 0:P], b_bd[:, c, :], a_, start=True, stop=True)
                            MM(acc[2 + h][:, c % 2, P:P + CHUNK], b_bd[:, c, :], r_, start=True, stop=True)
                            MM(acc[2 + h][:, c % 2, 0:P], k_bd[:, c, :], a_, start=True, stop=True)
                            ins = MM(acc[2 + h][:, c % 2, P + CHUNK:P + 2 * CHUNK], k_bd[:, c, :], r_, start=True, stop=True)
                        ins.then_inc(g_done, 1)
                    elif step == "tok":
                        if h == 0:
                            pe.wait_ge(v_built, p + 1)
                            if p:
                                pe.wait_ge(inv_ready, 12 * p)
                        else:
                            pe.wait_ge(tok_out, 3 * p + 1)
                        for src, dst in ((v_bd, un[0]), (b_bd, un[1])) if h == 0 else ((k_bd, un[0]),):
                            for c in range(CHUNKS):
                                ins = nc.tensor.transpose(bank4(dst)[:, c, :], src[:, c, :], ident)
                            ins.then_inc(tok_done, 1)
                    elif step == "x1":
                        pe.wait_ge(inv_ready, 12 * p + h + 1)
                        for c in half:
                            ins = nc.tensor.transpose(bank4(acc[h])[:, c % 2, :], xt[:, c, :], ident)
                        ins.then_inc(x1_done, 1)
                    elif step == "t1":
                        if j == 1:
                            pe.wait_ge(x1_out, 2 * p + h + 1)
                        else:
                            pe.wait_ge(nm_ready, 4 * p + j - 1)
                            pe.wait_ge(inv_ready, 12 * p + 2 * (j - 1) + h + 1)
                        for c in half:
                            ins = MM(bank4(acc[h])[:, c % 2, :], n_m[(j - 1) % 2][:, c, :], inv_x[:, c, :], start=True, stop=True)
                        ins.then_inc(t1_done, 1)
                    elif step == "dx":
                        if j == 1:
                            pe.wait_ge(lak_ready, 2 * p + h + 1)
                            pe.wait_ge(tok_out, 3 * p + 3)
                        pe.wait_ge(t1_out, 10 * p + 2 * (j - 1) + h + 1)
                        for c in half:
                            if j < WKV_LEVELS[-1]:
                                MM(bank4(acc[2 + h])[:, c % 2, :], xt[:, c, :], t1[:, c, :], start=True, stop=True)
                            ins = MM(bank4(un[h])[:, c % 2, :], t1[:, c, :], xt[:, c, :], start=True, stop=True)
                        ins.then_inc(dx_done, 1)
                    else:
                        c, i, q = j, CHUNKS * p + j, p % 2
                        before = state[(c - 1) % 2]
                        if step == "rhs":
                            out_ = stat_ps[:, 0, 0:P]
                            if c:
                                pe.wait_ge(state_ready, (CHUNKS - 1) * p + c)
                                MM(out_, ar[q][:, c, 0:P], before[:], start=True, stop=False)
                            MM(out_, lak_t[q][:, c, :], v_tok[q][:, c, :], start=(c == 0), stop=True).then_inc(rhs_done, 1)
                        elif step == "u":
                            pe.wait_ge(rhs_out, i + 1)
                            pe.wait_ge(inv_ready, 12 * p + 11 + h)
                            MM(stat_ps[:, 0, 0:P], xt[:, c, :], wkv_rhs[:], start=True, stop=True).then_inc(u_done, 1)
                        else:
                            pe.wait_ge(u_out, i + 1)
                            if c < CHUNKS - 1:
                                MM(stat_ps[:, 0, 0:P], b_tok[q][:, c, :], wkv_u[:], start=True, stop=False)
                                MM(stat_ps[:, 0, 0:P], k_tok[q][:, c, :], v_tok[q][:, c, :], start=False, stop=True).then_inc(s_done, 1)
                            if i:
                                pe.wait_ge(y_out, i)
                            y = misc[:, 0, 0:CHUNK]
                            if c:
                                MM(y, before[:], ar[q][:, c, P:P + CHUNK], start=True, stop=False)
                            MM(y, wkv_u[:], lrb_t[q][:, c, :], start=(c == 0), stop=False)
                            MM(y, v_tok[q][:, c, :], lrk_t[q][:, c, :], start=False, stop=True).then_inc(y_done, 1)
            pe.wait_ge(y_out, CHUNKS * PAIRS)
            for j in range(4):
                for m in range(2):
                    ins = MM(acc[j][:, m, :], head_mean, y_wkv[:, 2 * j + m, :], start=True, stop=True)
                ins.then_inc(gn_mean_done, 1)
            pe.wait_ge(rk_ready, 1)
            for j, b in enumerate((stat_ps, misc, un[0], un[1])):
                for m in range(2):
                    ins = MM(b[:, m, :], head_ones, rw_c[:, 2 * j + m, :], start=True, stop=True)
                ins.then_inc(bonus_done, 1)
            for j in range(4):
                pe.wait_ge(ycsq_ready, j + 1)
                for m in range(2):
                    ins = MM(acc[j][:, m, :], head_mean, rw_kk[:, 2 * j + m, :], start=True, stop=True)
                ins.then_inc(gn_var_done, 1)
            for j in range(UPD):
                unit(U_RWO + j, acc[j], (z_hi, z_lo), z_ready(Z_RW) if j == 0 else None)
            norm_stats(N_MLP1)
            mlp(1, N_MLP1)
            norm_stats(N_FIN1)

            def rot(r, n, v):
                pe.wait_ge(un_free, freed(v))
                if r:
                    pe.wait_ge(rope_done, r)
                MM(misc[:, 0:n, :], rot_w, rope_in[r % 2][:, 0:n, :], start=True, stop=True).then_inc(rot_done, 1)

            def attention(kind, k_of, v_of):
                b = HEADS * kind
                for i in range(-2, HEADS + 1):
                    k = i + 2
                    if k < HEADS:
                        lo = HD * (k % 2)
                        if k >= 4:
                            pe.wait_ge(max_ready, b + k - 3)
                        if kind == 0:
                            pe.wait_ge(rope_done, ROPE_Q + k // 4 + 1)
                        for qt in range(QT):
                            ins = MM(acc[k % 4][:, qt, :], q_fm[lo:lo + HD, k // 2, P * qt:P * qt + P], k_of(k), start=True, stop=True)
                        ins.then_inc(qk_done, 1)
                    if 0 <= i < HEADS:
                        pe.wait_ge(p_ready, b + i + 1)
                        if i >= 2:
                            pe.wait_ge(pt_out, b + i - 1)
                        dst = (stat_ps, misc)[i % 2][:, :, :].rearrange("p a s -> p (a s)")
                        for n, (qt, st) in enumerate(((0, 0), (1, 0), (1, 1))):
                            ins = nc.tensor.transpose(dst[:, P * n:P * n + P], probs[i % NA][:, qt, P * st:P * st + P], ident)
                        ins.then_inc(pt_done, 1)
                    if i >= 1:
                        h = i - 1
                        lo = HD * (h % 2)
                        pe.wait_ge(pt_out, b + h + 1)
                        if h % 4 == 0 and h >= 8:
                            pe.wait_ge(zf_ready, (Z_A, Z_B)[kind] + h // 4 - 1)
                        o = un[h // 4 % 2][lo:lo + HD, h // 2 % 2, :]
                        pt = probs_t[h % 2]
                        MM(o[:, 0:P], v_of(h, 0), pt[:, 0, :], start=True, stop=True, skip_group_check=True)
                        MM(o[:, P:2 * P], v_of(h, 0), pt[:, 1, :], start=True, stop=False, skip_group_check=True)
                        MM(o[:, P:2 * P], v_of(h, 1), pt[:, 2, :], start=False, stop=True, skip_group_check=True).then_inc(pv_done, 1)

            norm_stats(N_A)
            h_tiles = (h_hi, h_lo)
            free_bank(V_A)
            pe.wait_ge(lo_made, U_KI + 1)
            wh, wl = w_hi[U_KI % 2], w_lo[U_KI % 2]
            bank = un[V_A % 2]
            for kt in range(KT):
                pe.wait_ge(h_lo_made, H_BASE[N_A] + kt + 1)
                three(bank[:, 0, :], wh[:, kt, 0:P], wl[:, kt, 0:P], h_hi[:, kt, :], h_lo[:, kt, :], kt == 0, kt == KT - 1)
            for a in range(QT):
                q = slice(P * a, P * a + P)
                for kt in range(KT):
                    ins = three(bank[:, 1, IDX_HEADS * a:IDX_HEADS * (a + 1)], h_hi[:, kt, q], h_lo[:, kt, q], wh[:, kt, P:KI_COLS],
                                wl[:, kt, P:KI_COLS], False, kt == KT - 1)
            ins.then_inc(unit_done, 1)

            def a_unit(k, tokens=False):
                free_bank(V_A + k)
                unit(U_KI + k, un[(V_A + k) % 2], h_tiles, tokens=tokens)

            def index_scores(qt):
                if qt == 0:
                    pe.wait_ge(rope_done, ROPE_QI + 2)
                else:
                    pe.wait_ge(score_used, qt)
                for h in range(IDX_HEADS):
                    lo = HD * (h % 2)
                    ins = MM(acc[2 * (h // 4) + h % 2][:, h // 2 % 2, :], qi_fm[lo:lo + HD, h // 2, P * qt:P * qt + P],
                             ki_fm[lo:lo + HD, 0, :], start=True, stop=True)
                ins.then_inc(score_done, 1)

            a_unit(1)
            rot(ROPE_KI, 1, V_A)
            a_unit(2)
            rot(ROPE_QI, 2, V_A + 1)
            a_unit(3)
            rot(ROPE_QI + 1, 2, V_A + 2)
            a_unit(4, tokens=True)
            rot(ROPE_K, 2, V_A + 3)
            index_scores(0)
            a_unit(5)
            index_scores(1)
            a_unit(6)
            rot(ROPE_Q, 2, V_A + 5)
            a_unit(7)
            rot(ROPE_Q + 1, 2, V_A + 6)
            a_unit(8)
            rot(ROPE_Q + 2, 2, V_A + 7)
            rot(ROPE_Q + 3, 2, V_A + 8)
            pe.wait_ge(kdup_ready, KV_HEADS)
            pe.wait_ge(score_used, 2)
            group = HEADS // KV_HEADS
            attention(0, lambda h: k_dup[HD * (h % 2):HD * (h % 2) + HD, h // group, :],
                      lambda h, s: vA_tok[:, s, HD * (h // group):HD * (h // group) + HD])
            for j in range(UPD):
                unit(U_OA + j, acc[j], (z_hi, z_lo), z_ready(Z_A) if j == 0 else None)
            norm_stats(N_MLP2)
            mlp(2, N_MLP2)
            norm_stats(N_B)
            free_bank(V_B)
            pe.wait_ge(lo_made, U_F + 1)
            wh, wl = w_hi[U_F % 2], w_lo[U_F % 2]
            for kt in range(KT):
                pe.wait_ge(h_lo_made, H_BASE[N_B] + kt + 1)
                ins = three(un[V_B % 2][:, 0, :], wh[:, kt, 0:P], wl[:, kt, 0:P], h_hi[:, kt, :], h_lo[:, kt, :], kt == 0, kt == KT - 1)
            ins.then_inc(unit_done, 1)
            for j in range(UPD):
                free_bank(V_B + 1 + j)
                unit(U_KB + j, un[(V_B + 1 + j) % 2], h_tiles)
            pe.wait_ge(f_ready, 1)
            for a in range(QT):
                ins = nc.tensor.transpose(misc[:, 0, HEADS * a:HEADS * (a + 1)], f_cum[:, P * a:P * a + P], ident[0:HEADS, 0:HEADS])
            ins.then_inc(cumq_ready, 1)
            for r in range(8):
                if r >= 4:
                    pe.wait_ge(cumk_ready, r - 3)
                for m in range(2):
                    ins = MM(acc[r % 4][:, m, :], ident[0:HEADS, 2 * r + m:2 * r + m + 1].to_broadcast([HEADS, P]), f_neg[:], start=True, stop=True)
                ins.then_inc(f_bcast, 1)
            for j in range(UPD):
                free_bank(V_B + 5 + j)
                unit(U_VB + j, un[(V_B + 5 + j) % 2], h_tiles, tokens=True)
            for j in range(UPD):
                free_bank(V_B + 9 + j)
                unit(U_QB + j, un[(V_B + 9 + j) % 2], (z_hi, z_lo), h_ready(H_BASE["B_q"]) if j == 0 else None)
            pe.wait_ge(un_free, freed(V_B + 12))
            attention(1, lambda h: kB_fm[HD * (h % 2):HD * (h % 2) + HD, h // 2, :], lambda h, s: vB_tok[:, s, HD * h:HD * h + HD])
            for j in range(UPD):
                unit(U_OB + j, acc[j], (z_hi, z_lo), z_ready(Z_B) if j == 0 else None)
            norm_stats(N_MLP3)
            mlp(3, N_MLP3)
            norm_stats(N_OUT)
            pe.wait_ge(normed, 64 + KT)
            for k in range(4):
                free_bank(V_OUT + k)
                for n in range(4):
                    t = 4 * (k % 2) + n
                    ins = nc.tensor.transpose(bank4(un[(V_OUT + k) % 2])[:, n, :], tmp[:, t, P * (k // 2):P * (k // 2) + P], ident)
                ins.then_inc(tp_done, 1)


INPUTS = ("x", "c", "norm_g", "final_g", "ada_w", "ada_b", "conv_w_in", "conv_w", "conv_w_out", "rw_mu", "rw_w_rkv", "rw_w_o",
          "rw_w0", "rw_w1", "rw_w2", "rw_a0", "rw_a1", "rw_a2", "rw_g1", "rw_g2", "rw_k_k", "rw_k_a", "rw_r_k", "rw_ln_w",
          "rw_ln_b", "mlp_w1", "mlp_w2", "g_attn_a_2", "w_in_a_2", "w_o_a_2", "g_kv_2", "w_kv_b_2", "b_f_2", "g_attn_b_2",
          "w_q_b_2", "w_o_b_2", "g_mlp_2", "w_up_2", "w_down_2", "g_final_2")


def kernel(**inputs):
    import concourse.bacc as bacc
    from concourse.bass_utils import run_bass_kernel_spmd

    nc = bacc.Bacc("TRN2", target_bir_lowering=False, num_devices=1)
    arrays = {f"in_{n}": np.ascontiguousarray(inputs[n]) for n in INPUTS}
    arrays["in_const_table"] = constant_table()
    aps = {n[3:]: nc.dram_tensor(n, a.shape, mybir.dt.from_np(a.dtype), kind="ExternalInput").ap() for n, a in arrays.items()}
    out = nc.dram_tensor("out_x", (1, SEQ, D), F32, kind="ExternalOutput").ap()
    build(nc, aps, out)
    return run_bass_kernel_spmd(nc, [arrays], core_ids=[0]).results[0]["out_x"]
```

```python
from contextlib import ExitStack

import concourse.bass as bass
import numpy as np
from concourse import mybir

ALU = mybir.AluOpType
ACT = mybir.ActivationFunctionType
F32 = mybir.dt.float32
F32R = mybir.dt.float32r
AX_X = mybir.AxisListType.X

P = 128
SEQ = 256
D = 1024
KT = D // P
QT = SEQ // P
FF = 4 * D
GROUPS = FF // D
HD = 64
HEADS = D // HD
PAIRS = HEADS // 2
CHUNK = 64
CHUNKS = SEQ // CHUNK
UC = 256
UPD = D // UC
KV_HEADS = 4
IDX_HEADS = 8
TOPK = min(256, SEQ // 4)
RD, RA, RG = 64, 64, 160
DECAY = float(np.exp(-0.5))
NORM_EPS = 1e-6
GN_EPS = 64e-5
NEG = -1e30
TAKEN = -3e38

VEC_ADA_B, VEC_NORM_G, VEC_CONV_W, VEC_MU = 0, 96, 128, 152
VEC_W0, VEC_A0, VEC_KK, VEC_KA, VEC_RK, VEC_LNW, VEC_LNB = 200, 208, 216, 224, 232, 240, 248
VEC_C, VEC_FINAL, VEC_GA, VEC_GKV, VEC_GB, VEC_GMLP, VEC_GFIN = 256, 264, 272, 280, 288, 296, 312
N_VEC = 320

CONST_PARTS = ((("ident", P), ("mean", P), ("ones", P), ("rot", P)),
               (("head_ones", P), ("head_mean", P), ("level_t", 6 * P), ("before", P), ("upto", CHUNK), ("resets", SEQ)),
               (("cos", SEQ), ("sin", SEQ), ("admit", P + SEQ), ("causal", P + SEQ)))
CONST_COLS, CONST_AT = {}, [0]
for _part in CONST_PARTS:
    _at = CONST_AT[-1]
    for _name, _n in _part:
        CONST_COLS[_name] = (_at, _at + _n)
        _at += _n
    CONST_AT.append(_at)
N_CONST = CONST_AT[-1]


def constant_table():
    t = np.zeros((P, N_CONST), np.float32)

    def put(name, a):
        lo, hi = CONST_COLS[name]
        t[:, lo:hi] = np.asarray(a, np.float32).reshape(P, hi - lo)

    i = np.arange(P)
    same_head = (i[:, None] // HD) == (i[None, :] // HD)
    put("ident", np.eye(P))
    put("mean", np.full((P, P), 1.0 / D))
    put("ones", np.ones((P, P)))
    put("head_ones", same_head)
    put("head_mean", same_head / HD)
    rot = np.zeros((P, P))
    for m in range(P):
        d = m % HD
        rot[m + HD // 2 if d < HD // 2 else m - HD // 2, m] = -1.0 if d < HD // 2 else 1.0
    put("rot", rot)
    s, q = i[:, None], i[None, :]
    levels = [same_head & (s >> (j + 1) == q >> (j + 1)) & ((q >> j) & 1 == 1) & ((s >> j) & 1 == 0) for j in range(6)]
    put("level_t", np.stack(levels, 1))
    put("before", same_head & (s < q))
    put("upto", (i[:, None] % CHUNK) <= np.arange(CHUNK)[None, :])
    pos = np.arange(SEQ)
    put("resets", np.broadcast_to(pos % CHUNK != 0, (P, SEQ)))
    inv = np.float32(1.0) / (np.float32(10000.0) ** (np.arange(0, HD, 2, dtype=np.float32) / np.float32(HD)))
    ang = inv.astype(np.float32)[:, None] * pos.astype(np.float32)[None, :]
    put("cos", np.tile(np.cos(ang), (4, 1)))
    put("sin", np.tile(np.sin(ang), (4, 1)))
    tok = np.arange(QT)[None, :, None] * P + i[:, None, None]
    packed = lambda a: np.concatenate([a[:, 0, 0:P], a[:, 1, :]], 1)
    put("admit", packed(np.where(pos[None, None, :] < (tok // CHUNK + 1) * CHUNK, 0.0, NEG)))
    put("causal", packed(np.where(pos[None, None, :] <= tok, 0.0, NEG)))
    return t


def build(nc, A, out):
    with ExitStack() as ctx:
        sems = {}

        def sem(name):
            if name not in sems:
                sems[name] = ctx.enter_context(nc.semaphore(name))
            return sems[name]

        base = (nc.sbuf_base + 63) // 64 * 64
        top = [base]

        def here(nbytes):
            off = top[0]
            top[0] += (nbytes + 63) // 64 * 64
            return off

        def at(name, shape, off, dt=F32):
            return nc.alloc_sbuf_tensor_at(name, shape, dt, offset=off)

        def new(name, shape, dt=F32):
            return at(name, shape, here(4 * int(np.prod(shape[1:]))), dt)

        FM = [P, KT, SEQ]
        FMB = 4 * KT * SEQ
        NSTAGE = 4
        stage = [new(f"stage{i}", [P, KT, UC]) for i in range(NSTAGE)]
        w_hi = [new(f"w_hi{i}", [P, KT, UC], F32R) for i in range(2)]
        w_lo = [new(f"w_lo{i}", [P, KT, UC], F32R) for i in range(2)]
        x = new("x", FM)
        act_off = [here(FMB) for _ in range(4)]
        h_hi, h_lo, z_hi, z_lo = (at(n, FM, o, F32R) for n, o in zip(("h_hi", "h_lo", "z_hi", "z_lo"), act_off))
        tmp_off = top[0]
        tmp = new("tmp", FM)
        sq = new("sq", FM)
        r_off = [here(FMB) for _ in range(6)]
        scr_off = here(26 * 1024)
        part_cols = [CONST_AT[i + 1] - CONST_AT[i] for i in range(3)]
        const_off = [here(4 * part_cols[0])]
        const_off += [here(4 * max(part_cols[1:]))] * 2
        const = [at(f"const{i}", [P, n], o) for i, (n, o) in enumerate(zip(part_cols, const_off))]
        vecT = new("vecT", [P, N_VEC])
        mods = [new(f"mod{i}", [P, 48]) for i in range(2)]
        gain = new("gain", [P, 4, KT])
        small = new("small", [P, 64])
        rstd = new("rstd", [P, 3, SEQ])

        def c_(name):
            lo, hi = CONST_COLS[name]
            i = max(i for i in range(3) if CONST_AT[i] <= lo)
            return const[i][:, lo - CONST_AT[i]:hi - CONST_AT[i]]

        ident, mean_w, ones_w, head_ones, head_mean, rot_w = (c_(n) for n in ("ident", "mean", "ones", "head_ones", "head_mean", "rot"))
        level_t = c_("level_t").rearrange("p (j q) -> p j q", j=6)
        admit, causal = c_("admit"), c_("causal")
        PACK = P + SEQ
        KEYS = (P, SEQ)
        QUERY = (slice(0, P), slice(P, PACK))

        x_in = at("x_in", [P, QT, D], scr_off)
        vec_in = at("vec_in", [P, 3, P], scr_off + 8192)
        ada_acc = at("ada_acc", [P, 6 * D], r_off[0])
        ada_first = [at(f"ada_first{i}", [P, KT, UC], o) for i, o in enumerate(act_off + [tmp_off] + r_off[3:6])]
        ada_dve = ada_first[6]
        ada_pool = [ada_first[5], ada_first[7]]
        c_silu = small[:, 0:8]
        eps_norm, eps_group = small[:, 32:33], small[:, 33:34]
        b_gate = at("b_gate", FM, scr_off + 16 * 1024)
        PADT = SEQ + 2
        u_pad = at("u_pad", [P, KT, PADT], scr_off)
        conv_y = at("conv_y", [P, 2, SEQ], scr_off + 8320)
        zf = [at(f"zf{i}", [P, 2, SEQ], scr_off + 12 * 1024 + 2048 * i) for i in range(2)]
        relu_b = [at(f"relu{i}", [P, 2, SEQ], scr_off + 16 * 1024 + 2048 * i) for i in range(2)]
        RW = [at(f"rw{i}", FM, r_off[i]) for i in range(6)]
        rw_r, rw_k, rw_v, rw_c, rw_a, rw_kk = RW
        lora1 = at("lora1", [P, KT, RD + RA + RG], scr_off)
        lora_w2 = at("lora_w2", [P, D], scr_off + 9216)
        lora_a2 = lora_w2
        lora_g2a = at("lora_g2a", [P, D], scr_off + 14336)
        lora_g2b = at("lora_g2b", [32, D], scr_off + 18432)
        lora_h = at("lora_h", [P, 4, SEQ], scr_off + 22528)
        lora_in_w, lora_in_a, lora_in_g = rw_c, rw_a, rw_v
        mixf = at("mixf", [P, 4, SEQ], r_off[5])
        BD = [P, CHUNKS, P]
        next_at = [0, 0]

        def pair_new(name, shape, dt=F32):
            off = act_off[0] + next_at[0]
            next_at[0] += 4 * int(np.prod(shape[1:]))
            assert next_at[0] <= 4 * FMB
            return at(name, shape, off)

        def scratch_new(name, shape):
            off = scr_off + next_at[1]
            next_at[1] += 4 * int(np.prod(shape[1:]))
            assert next_at[1] <= 26 * 1024
            return at(name, shape, off)

        b_tok, k_tok, v_tok, inv_t, lak_t = ([pair_new(f"{n}{i}", BD) for i in range(2)] for n in ("b_tok", "k_tok", "v_tok", "inv_t", "lak_t"))
        lrb_t, lrk_t = ([pair_new(f"{n}{i}", [P, CHUNKS, CHUNK]) for i in range(2)] for n in ("lrb_t", "lrk_t"))
        n_t, inv_x, t1 = (pair_new(n, BD) for n in ("n_t", "inv_x", "t1"))
        ar = [scratch_new(f"ar{i}", [P, CHUNKS, P + CHUNK]) for i in range(2)]
        b_bd, k_bd, v_bd = (scratch_new(n, BD) for n in ("b_bd", "k_bd", "v_bd"))
        w_cum, w_inv = (scratch_new(n, [P, SEQ]) for n in ("w_cum", "w_inv"))
        n_m = [scratch_new(f"n_m{i}", BD) for i in range(2)]
        state = [scratch_new(f"state{i}", [P, P]) for i in range(2)]
        state_kept, wkv_rhs, wkv_u = (scratch_new(n, [P, P]) for n in ("state_kept", "wkv_rhs", "wkv_u"))
        w_end = scratch_new("w_end", [P, PAIRS, CHUNKS])
        y_wkv, g_wkv = tmp, sq
        q_fm = at("q_fm", FM, r_off[0])
        kA_fm = at("kA_fm", [P, 2, SEQ], r_off[1])
        k_dup = at("k_dup", [P, KV_HEADS, SEQ], r_off[1] + 2048)
        qi_fm = at("qi_fm", [P, 4, SEQ], r_off[2])
        ki_fm = at("ki_fm", [P, 1, SEQ], r_off[2] + 4096)
        vA_tok = at("vA_tok", [P, QT, 256], r_off[2] + 5120)
        kB_fm = at("kB_fm", FM, r_off[1])
        vB_tok = at("vB_tok", [P, QT, D], r_off[2])
        rope_in = [at(f"rope_in{i}", [P, 2, SEQ], r_off[3] + 2048 * i) for i in range(2)]
        rope_c = at("rope_c", [P, 2, SEQ], r_off[3] + 4096)
        sel_bias = at("sel_bias", [P, PACK], r_off[3] + 6144)
        score = at("score", [P, PACK], r_off[4])
        score_r = [at(f"score_r{i}", [P, 2, SEQ], r_off[4] + 2048 + 2048 * i) for i in range(2)]
        top8 = at("top8", [P, QT, 8], r_off[4] + 6144)
        wi_tok = at("wi_tok", [P, QT, IDX_HEADS], r_off[4] + 6208)
        cum_k = at("cum_k", [P, HEADS, SEQ], r_off[3])
        f_z = at("f_z", [HEADS, SEQ], scr_off + 10 * 1024)
        f_e = at("f_e", [HEADS, SEQ], scr_off + 11 * 1024)
        f_l = at("f_l", [HEADS, SEQ], scr_off + 16 * 1024)
        f_cum = at("f_cum", [HEADS, SEQ], scr_off + 17 * 1024)
        f_neg = at("f_neg", [HEADS, SEQ], scr_off + 18 * 1024)
        b_f = at("b_f", [HEADS, 1], scr_off + 24 * 1024)
        cum_q = at("cum_q", [P, QT, HEADS], scr_off + 24 * 1024 + 64)
        head_bias = [at(f"head_bias{i}", [P, PACK], scr_off + 18 * 1024 + 1024 + 2048 * i) for i in range(2)]
        NA = 4
        logit = [at(f"logit{i}", [P, PACK], r_off[5] + 2048 * i) for i in range(NA)]
        probs = [at(f"probs{i}", [P, PACK], scr_off + 2048 * i) for i in range(NA)]
        probs_t = [at(f"probs_t{i}", [P, 3, P], scr_off + 8192 + 1536 * i) for i in range(2)]
        stat = [at(f"stat{i}", [P, 8], scr_off + 11264 + 64 * i) for i in range(NA)]
        out_tok = at("out_tok", [P, QT, D], scr_off)
        assert top[0] <= nc.sbuf_usable_end, (top[0], nc.sbuf_usable_end)

        acc = [ctx.enter_context(nc.psum_tensor(f"acc{i}", [P, 2, SEQ], F32)) for i in range(4)]
        un = [ctx.enter_context(nc.psum_tensor(f"un{i}", [P, 2, SEQ], F32)) for i in range(2)]
        stat_ps = ctx.enter_context(nc.psum_tensor("stat_ps", [P, 2, SEQ], F32))
        misc = ctx.enter_context(nc.psum_tensor("misc", [P, 2, SEQ], F32))

        GN_GROUPS = ((0, 2), (2, 4), (4, 6), (6, 7), (7, 8))
        gn_bank, bonus_bank = (acc[0], acc[1], acc[2], acc[3], misc), (un[0], un[1], un[0], un[1])
        GROUP_PE = {0: (("mean", 0), ("mean", 1)), 1: (("bonus", 0), ("bonus", 1)), 2: (("mean", 2), ("mean", 3), ("var", 0)), 3: (("var", 1),),
                    4: (("bonus", 2), ("var", 2)), 5: (("var", 3),), 6: (("bonus", 3),)}
        GROUP_ACT = {0: (("square", 0),), 1: (("square", 1),), 3: (("square", 2), ("root", 0), ("square", 3)), 4: (("shift", 0), ("root", 1)),
                     5: (("shift", 1),), 6: (("root", 2),), 7: (("root", 3), ("shift", 2)), 8: (("shift", 3),)}
        GROUP_DVE = {0: (("center", 0), ("center", 1)), 1: (("bonus", 0), ("bonus", 1)), 2: (("center", 2), ("center", 3)), 4: (("scale", 0),),
                     5: (("bonus", 2), ("scale", 1)), 8: (("bonus", 3), ("scale", 2)), 10: (("scale", 3),)}
        GROUP_POOL = (("weigh", 0), ("weigh", 1), ("gate", 0), ("weigh", 2), ("weigh", 3), ("gate", 1), ("add", 0), ("gate", 2), ("add", 1),
                      ("gate", 3), ("add", 2), ("add", 3), ("weigh", 4))

        def flat(b):
            return b[:, :, :].rearrange("p a s -> p (a s)")

        def bank4(b):
            return b[:, :, :].rearrange("p a s -> p (a s)").rearrange("p (c q) -> p c q", c=CHUNKS)

        units = []

        def cols(w, c0, n=UC, r0=0):
            return [(0, n, w[r0:r0 + D, c0:c0 + n].rearrange("(t p) n -> p t n", p=P))]

        def add(sources):
            units.append(sources)
            return len(units) - 1

        def add_dense(w, n):
            first = len(units)
            for j in range(n // UC):
                add(cols(w, j * UC))
            return first

        def add_mlp(w1, w2):
            first = len(units)
            for g in range(GROUPS):
                for j in range(UPD):
                    add(cols(w1, g * D + j * UC))
                for j in range(UPD):
                    add(cols(w2, j * UC, r0=g * D))
            return first

        w_in_a, w_kv = A["w_in_a_2"][0], A["w_kv_b_2"]
        U_CONV_IN = add_dense(A["conv_w_in"][0], 3 * D)
        U_CONV_OUT = add_dense(A["conv_w_out"][0], D)
        U_MLP = [add_mlp(A["mlp_w1"][0], A["mlp_w2"][0])]
        U_RWK = add_dense(A["rw_w_rkv"][0, 1], D)
        U_RWR = add_dense(A["rw_w_rkv"][0, 0], D)
        U_RWV = add_dense(A["rw_w_rkv"][0, 2], D)
        U_RWO = add_dense(A["rw_w_o"][0], D)
        U_MLP.append(add_mlp(A["mlp_w1"][1], A["mlp_w2"][1]))
        A_K, A_V, A_QI, A_KI = D, D + 256, D + 512, D + 1024
        KI_COLS = HD + HD + IDX_HEADS
        U_KI = add([(0, HD, cols(w_in_a, A_KI, HD)[0][2]), (HD, KI_COLS, cols(w_in_a, A_KI, HD + IDX_HEADS)[0][2])])
        U_QI = add(cols(w_in_a, A_QI))
        add(cols(w_in_a, A_QI + UC))
        U_KA = add(cols(w_in_a, A_K))
        U_VA = add(cols(w_in_a, A_V))
        U_QA = len(units)
        for j in range(UPD):
            add(cols(w_in_a, j * UC))
        U_OA = add_dense(A["w_o_a_2"][0], D)
        U_MLP.append(add_mlp(A["w_up_2"][0], A["w_down_2"][0]))
        U_F = add([(0, HEADS, cols(w_kv, 2 * D, HEADS)[0][2]), (HEADS, P, cols(w_kv, 0, P - HEADS)[0][2])])
        U_KB = len(units)
        for j in range(2 * UPD):
            add(cols(w_kv, j * UC))
        U_VB = U_KB + UPD
        U_QB = add_dense(A["w_q_b_2"][0], D)
        U_OB = add_dense(A["w_o_b_2"][0], D)
        U_MLP.append(add_mlp(A["w_up_2"][1], A["w_down_2"][1]))
        NU = len(units)

        W_HALF = (slice(0, KT // 2), slice(KT // 2, KT))

        def unit_cols(u):
            return max(hi for _, hi, _ in units[u])

        V_VEC, V_X, V_CONV = 0, 1, 5
        V_MLP = [17]
        V_RKV = V_MLP[0] + 16
        V_MLP.append(V_RKV + 12)
        V_A = V_MLP[1] + 16
        V_MLP.append(V_A + 9)
        V_B = V_MLP[2] + 16
        V_MLP.append(V_B + 13)
        V_OUT = V_MLP[3] + 16
        Z_CONV, Z_MLP0, Z_RW, Z_MLP1, Z_A, Z_MLP2, Z_B, Z_MLP3 = 0, 4, 20, 24, 40, 44, 60, 64

        def zf_count(zc):
            return zc + 1 - (UPD if zc >= Z_RW else 0)
        Z_MLP = [Z_MLP0, Z_MLP1, Z_MLP2, Z_MLP3]
        N_CONV, N_MLP0, N_RW, N_MLP1, N_FIN1, N_A, N_MLP2, N_B, N_MLP3, N_OUT = range(10)
        N_MLP = [N_MLP0, N_MLP1, N_MLP2, N_MLP3]
        H_BASE = {N_CONV: 0, N_MLP0: 8, N_MLP1: 16, N_A: 24, N_MLP2: 32, N_B: 40, "B_q": 48, N_MLP3: 56}
        ROPE_USE = (0, 1, 2, 3, 5, 6, 7, 8)
        ROPE_KI, ROPE_QI, ROPE_K, ROPE_Q, N_ROPE = 0, 1, 3, 4, 8

        const_in, const_b_in, x_loaded, vec_loaded, lora_loaded, bf_loaded = (sem(n) for n in ("const_in", "const_b_in", "x_loaded", "vec_loaded", "lora_loaded", "bf_loaded"))
        landed = [sem(f"unit_landed{i}") for i in range(NSTAGE)]
        hi_made, lo_made, unit_done, un_free = (sem(n) for n in ("hi_made", "lo_made", "unit_done", "un_free"))
        VEC_DMAS = 19

        def freed(v):
            return v + 1 if v < V_X else v - 3

        N_ADA = 6 * D // UC
        ADA_FIRST = 8
        ADA_DVE = (0, 1, 3, 4, 6, 7) + tuple(range(9, 20, 2)) + tuple(range(N_ADA + 2, 2 * N_ADA, 3))
        ADA_POOL = tuple(a for a in range(2 * N_ADA) if a not in ADA_DVE)

        def ada_cols(a):
            return cols(A["ada_w"][a // N_ADA], a % N_ADA * UC)[0][2]

        def ada_count(units_of, a_end):
            return sum(a < a_end for a in units_of)

        WKV_LEVELS = range(1, 6)
        wkv_prepare = [("gram", 0, 0), ("gram", 0, 1), ("tok", 0, 0), ("tok", 0, 1), ("x1", 0, 0), ("x1", 0, 1)]
        for j in WKV_LEVELS:
            wkv_prepare += [("t1", j, 0), ("t1", j, 1), ("dx", j, 0), ("dx", j, 1)]
        WKV_CHAIN_AFTER = (0, 1, 2, 4, 6, 8, 10, 12, 14, 16, 18, 20)
        wkv_chain = [(step, c, c // 2) for c in range(CHUNKS) for step in ("rhs", "u", "sy")]
        WKV_STEPS = []
        for n, step in enumerate(wkv_prepare):
            WKV_STEPS.append(step)
            WKV_STEPS += [c for c, after in zip(wkv_chain, WKV_CHAIN_AFTER) if after == n]

        def joined(m, j):
            return m.rearrange("p (b two s) -> p b two s", two=2, s=1 << j)

        def early(m, j):
            return joined(m, j)[:, :, 0, :]

        def late(m, j):
            return joined(m, j)[:, :, 1, :]

        def wkv_steps(p):
            for step, j, h in WKV_STEPS:
                chain_step = step in ("rhs", "u", "sy")
                if 0 <= p - chain_step < PAIRS:
                    yield step, p - chain_step, j, h

        block = ctx.enter_context(nc.Block())

        @block.sync
        def _(sp):
            for i in range(2):
                sp.dma_start(const[i][:], A["const_table"][:, CONST_AT[i]:CONST_AT[i + 1]]).then_inc(const_in, 16)
            sp.dma_start(x_in[:], A["x"][0].rearrange("(a p) d -> p a d", p=P)).then_inc(x_loaded, 16)

            def rows(tile, r0, ap, n):
                sp.dma_start(vec_in[r0:r0 + n, tile, :], ap).then_inc(vec_loaded, 16)

            as_rows = lambda ap, n: ap.rearrange("(r q) -> r q", q=P)
            rows(0, 0, as_rows(A["ada_b"][0], 48), 48)
            rows(0, 48, as_rows(A["ada_b"][1], 48), 48)
            rows(0, 96, A["norm_g"].rearrange("a b (r q) -> (a b r) q", q=P), 32)
            rows(1, 0, A["conv_w"][0].rearrange("a (r q) -> (a r) q", q=P), 24)
            rows(1, 24, A["rw_mu"][0].rearrange("a (r q) -> (a r) q", q=P), 48)
            for r0, name in ((72, "rw_w0"), (80, "rw_a0"), (88, "rw_k_k"), (96, "rw_k_a"), (112, "rw_ln_w"), (120, "rw_ln_b")):
                rows(1, r0, as_rows(A[name][0], 8), 8)
            rows(1, 104, A["rw_r_k"][0].rearrange("(r a) d -> r (a d)", a=2), 8)
            rows(2, 0, as_rows(A["c"][0], 8), 8)
            rows(2, 8, as_rows(A["final_g"], 8), 8)
            rows(2, 16, as_rows(A["g_attn_a_2"][0], 8), 8)
            rows(2, 24, as_rows(A["g_kv_2"], 8), 8)
            rows(2, 32, as_rows(A["g_attn_b_2"][0], 8), 8)
            rows(2, 40, A["g_mlp_2"].rearrange("a (r q) -> (a r) q", q=P), 16)
            rows(2, 56, as_rows(A["g_final_2"], 8), 8)

            for a in range(ADA_FIRST):
                sp.dma_start(ada_first[a][:], ada_cols(a)).then_inc(sem(f"ada_first_landed{a}"), 16)

            ada_at = [U_CONV_IN + NSTAGE] + [U_CONV_IN + 2 * k + 8 for k in range(5)] + [U_MLP[0] + 1] +\
                [U_MLP[0] + 8 * g + d + 7 for g in range(GROUPS) for d in (UPD, UPD + 2)][:-1]

            def load_unit(u):
                if u >= NSTAGE:
                    sp.wait_ge(lo_made, 2 * (u - NSTAGE + 1))
                for lo, hi, src in units[u]:
                    sp.dma_start(stage[u % NSTAGE][:, :, lo:hi], src).then_inc(landed[u % NSTAGE], 32 // len(units[u]))

            for u in range(NU):
                if u == U_RWK + NSTAGE:
                    sp.wait_ge(sem("x_ready"), 8 * N_RW + 8)
                    sp.dma_start(lora1[:, :, 0:RD], A["rw_w1"][0].rearrange("(t p) n -> p t n", p=P)).then_inc(lora_loaded, 16)
                    sp.dma_start(lora1[:, :, RD:RD + RA], A["rw_a1"][0].rearrange("(t p) n -> p t n", p=P)).then_inc(lora_loaded, 16)
                    sp.dma_start(lora1[:, :, RD + RA:], A["rw_g1"][0].rearrange("(t p) n -> p t n", p=P)).then_inc(lora_loaded, 16)
                    sp.dma_start(lora_w2[0:RD, :], A["rw_w2"][0]).then_inc(lora_loaded, 16)
                    sp.dma_start(lora_w2[RD:RD + RA, :], A["rw_a2"][0]).then_inc(lora_loaded, 16)
                    sp.dma_start(lora_g2a[:, :], A["rw_g2"][0, 0:P, :]).then_inc(lora_loaded, 16)
                    sp.dma_start(lora_g2b[:, :], A["rw_g2"][0, P:RG, :]).then_inc(lora_loaded, 16)
                if u == U_MLP[1] + UPD:
                    sp.wait_ge(sem("x_ready"), 8 * N_MLP1 + 8)
                    sp.dma_start(const[2][:], A["const_table"][:, CONST_AT[2]:]).then_inc(const_b_in, 16)
                if u == U_F:
                    sp.wait_ge(sem("x_ready"), 8 * N_MLP2 + 8)
                    sp.dma_start(b_f[:], A["b_f_2"].rearrange("(h a) -> h a", a=1)).then_inc(bf_loaded, 16)
                if u in ada_at:
                    k = ada_at.index(u) + ADA_FIRST - 2
                    sp.wait_ge(sem("ada_dve_done"), k)
                    sp.dma_start(ada_dve[:], ada_cols(ADA_DVE[k])).then_inc(sem("ada_dve_landed"), 16)
                load_unit(u)
            out_v = out[0].rearrange("(a p) d -> p a d", p=P)
            sp.wait_ge(un_free, freed(V_OUT + 3))
            sp.dma_start(out_v, out_tok[:]).then_inc(sem("stored"), 16)
            sp.wait_ge(sem("stored"), 16)

        tp_done, x_ready = sem("tp_done"), sem("x_ready")
        sq_ready, stat_done, log_done, ms_ready, root_ready = (sem(n) for n in ("sq_ready", "stat_done", "log_done", "ms_ready", "root_ready"))
        normed, h_hi_made, h_lo_made = (sem(n) for n in ("normed", "h_hi_made", "h_lo_made"))
        zf_ready, z_hi_made, z_lo_made, relu_ready = (sem(n) for n in ("zf_ready", "z_hi_made", "z_lo_made", "relu_ready"))
        lora_mixed, lora1_done, lora1_out, lora2_done, lora2_out = (sem(n) for n in ("lora_mixed", "lora1_done", "lora1_out", "lora2_done", "lora2_out"))
        hs_normed, hs_shifted, xx_ready, mix_ready, mix_hi, mix_lo = (
            sem(n) for n in ("hs_normed", "hs_shifted", "xx_ready", "mix_ready", "mix_hi", "mix_lo"))
        kk0_ready, kksq_ready, ss_done, ss_ready, ss_root = (sem(n) for n in ("kk0_ready", "kksq_ready", "ss_done", "ss_ready", "ss_root"))
        cum_ready, exp_ready, built = (sem(n) for n in ("cum_ready", "exp_ready", "built"))
        g_done, tok_done, tok_out, inv_ready, lak_ready, v_built, end_ready = (
            sem(n) for n in ("g_done", "tok_done", "tok_out", "inv_ready", "lak_ready", "v_built", "end_ready"))
        x1_done, x1_out, nm_ready, t1_done, t1_out, dx_done = (sem(n) for n in ("x1_done", "x1_out", "nm_ready", "t1_done", "t1_out", "dx_done"))
        rhs_done, rhs_out, u_done, u_out, y_done, y_out, s_done, state_ready = (
            sem(n) for n in ("rhs_done", "rhs_out", "u_done", "u_out", "y_done", "y_out", "s_done", "state_ready"))
        rk_ready, gn_mean_done, yc_ready, ycsq_ready, gn_var_done, gv_root, bonus_done, bonus_ready, bonus_shifted, bonus_gated, weighed, scaled, group_done, last_done = (
            sem(n) for n in ("rk_ready", "gn_mean_done", "yc_ready", "ycsq_ready", "gn_var_done", "gv_root", "bonus_done", "bonus_ready", "bonus_shifted",
                             "bonus_gated", "weighed", "scaled", "group_done", "last_done"))
        rot_done, rope_done, ki_loaded, cos_done, kdup_ready = (sem(n) for n in ("rot_done", "rope_done", "ki_loaded", "cos_done", "kdup_ready"))
        score_done, score_relu, score_used = sem("score_done"), sem("score_relu"), sem("score_used")
        f_abs, f_exp, f_one, f_log, f_ready, f_bcast, cumk_ready, cumq_ready = (
            sem(n) for n in ("f_abs", "f_exp", "f_one", "f_log", "f_ready", "f_bcast", "cumk_ready", "cumq_ready"))
        qk_done, max_ready, exp_done, sum_ready, p0_ready, p1_ready, pt_done, pt_out, pv_done = (
            sem(n) for n in ("qk_done", "max_ready", "exp_done", "sum_ready", "p0_ready", "p1_ready", "pt_done", "pt_out", "pv_done"))
        silu_e, silu_ready, ada_summed_pe = sem("silu_e"), sem("silu_ready"), sem("ada_summed_pe")

        ada_first_landed = [sem(f"ada_first_landed{a}") for a in range(ADA_FIRST)]
        ada_pool_landed = [sem(f"ada_pool_landed{i}") for i in range(2)]
        ada_dve_landed, ada_dve_done, ada_pool_done, ada_summed = (sem(n) for n in ("ada_dve_landed", "ada_dve_done", "ada_pool_done", "ada_summed"))

        @block.gpsimd
        def _(pool):
            G = nc.gpsimd
            chain = sem("pool_chain")
            count = [0]

            def link(ins):
                count[0] += 1
                ins.then_inc(chain, 1)
                pool.wait_ge(chain, count[0])

            n_first = ada_count(ADA_POOL, ADA_FIRST)

            def load_ada(k):
                pool.dma_start(ada_pool[k % 2][:], ada_cols(ADA_POOL[k])).then_inc(ada_pool_landed[k % 2], 16)

            pool.wait_ge(sem("silu_ready"), 1)
            for k, a in enumerate(ADA_POOL):
                if k < n_first:
                    pool.wait_ge(ada_first_landed[a], 16)
                    w = ada_first[a]
                else:
                    if a >= N_ADA > ADA_POOL[k - 1]:
                        pool.wait_ge(ada_summed, 4)
                    pool.wait_ge(ada_pool_landed[k % 2], 16 * ((k - n_first) // 2 + 1))
                    w = ada_pool[k % 2]
                link(G.tensor_tensor(w[:], w[:], c_silu.unsqueeze(2).to_broadcast([P, KT, UC]), ALU.mult))
                link(G.tensor_tensor(w[:, 0:4, :], w[:, 0:4, :], w[:, 4:8, :], ALU.add))
                link(G.tensor_tensor(w[:, 0:2, :], w[:, 0:2, :], w[:, 2:4, :], ALU.add))
                G.tensor_tensor(ada_acc[:, a % N_ADA * UC:(a % N_ADA + 1) * UC], w[:, 0, :], w[:, 1, :], ALU.add).then_inc(ada_pool_done, 1)
                if k == n_first - 1:
                    pool.wait_ge(ada_pool_done, n_first)
                    pool.wait_ge(ada_dve_done, ada_count(ADA_DVE, ADA_FIRST))
                    load_ada(n_first)
                    load_ada(n_first + 1)
                elif n_first <= k and k + 2 < len(ADA_POOL):
                    pool.wait_ge(ada_pool_done, k + 1)
                    load_ada(k + 2)

            pool.wait_ge(sem("xx_ready"), KT)
            for dst, which in ((lora_in_w, 1), (lora_in_a, 4), (lora_in_g, 5)):
                mu = vecT[:, VEC_MU + 8 * which:VEC_MU + 8 * which + 8].unsqueeze(2).to_broadcast([P, KT, SEQ])
                if dst is lora_in_g:
                    pool.wait_ge(sem("ada_summed_pe"), 6)
                link(G.tensor_tensor(dst[:], sq[:], mu, ALU.mult))
                G.tensor_tensor(dst[:], dst[:], tmp[:], ALU.add).then_inc(sem("lora_mixed"), 1)

            pool.wait_ge(sem("lora2_done"), 8)
            for m in (b_bd, k_bd, v_bd, ar[0], ar[1]):
                ins = G.memset(m[:], 0.0)
            ins.then_inc(sem("bd_zeroed"), 1)
            pool.wait_ge(sem("bd_zeroed"), 1)
            pool.wait_ge(sem("rw_ready"), 1)
            pool.wait_ge(un_free, freed(V_RKV + 7))
            wc = w_cum[:].rearrange("p (c s) -> p c s", c=CHUNKS)
            wi = w_inv[:].rearrange("p (c s) -> p c s", c=CHUNKS)

            def in_chunks(m, p, lo, hi):
                return m[lo:hi, p, :].rearrange("p (c s) -> p c s", c=CHUNKS)

            def build_bk(p):
                pool.wait_ge(sem("exp_ready"), 2 * p + 2)
                if p:
                    pool.wait_ge(sem("nm_ready"), 4 * p - 2)
                if p:
                    pool.wait_ge(sem("tok_done"), 3 * p)
                for h, (lo, hi) in enumerate(((0, HD), (HD, P))):
                    o = CHUNK * h
                    G.tensor_tensor(b_bd[lo:hi, :, o:o + CHUNK], in_chunks(rw_a, p, lo, hi), wi[lo:hi], ALU.mult)
                    link(G.tensor_tensor(k_bd[lo:hi, :, o:o + CHUNK], in_chunks(rw_k, p, lo, hi), wi[lo:hi], ALU.mult))

            def build_ar(p):
                if p >= 2:
                    pool.wait_ge(sem("y_done"), CHUNKS * (p - 1))
                if p:
                    pool.wait_ge(sem("nm_ready"), 4 * p)
                m = ar[p % 2]
                for h, (lo, hi) in enumerate(((0, HD), (HD, P))):
                    o = CHUNK * h
                    nkk = in_chunks(rw_kk, p, lo, hi)
                    G.tensor_copy(m[lo:hi, :, o:o + 1], nkk[:, :, 0:1])
                    link(G.tensor_tensor(m[lo:hi, :, o + 1:o + CHUNK], nkk[:, :, 1:CHUNK], wc[lo:hi, :, 0:CHUNK - 1], ALU.mult))
                G.tensor_tensor(m[:, :, P:P + CHUNK], in_chunks(rw_r, p, 0, P), wc, ALU.mult).then_inc(sem("built"), 1)

            def gate_products(p):
                spread = lambda vec: vecT[:, vec + p:vec + p + 1].to_broadcast([P, SEQ])
                link(G.tensor_tensor(rw_c[:, p, :], rw_r[:, p, :], rw_k[:, p, :], ALU.mult))
                G.tensor_tensor(rw_c[:, p, :], rw_c[:, p, :], spread(VEC_RK), ALU.mult).then_inc(rk_ready, 1)
                G.tensor_tensor(rw_k[:, p, :], g_wkv[:, p, :], spread(VEC_LNW), ALU.mult).then_inc(sem("gate_weighed"), 1)

            pool.wait_ge(sem("lora2_out"), 20)
            build_bk(0)
            build_ar(0)
            for p in range(PAIRS):
                for j in WKV_LEVELS[1:]:
                    if j == 2:
                        pool.wait_ge(sem("inv_ready"), 12 * p + 2)
                    else:
                        pool.wait_ge(sem("t1_done"), 10 * p + 2 * (j - 2))
                    G.tensor_tensor(n_m[(j - 1) % 2][:], n_t[:], level_t[:, j, :].unsqueeze(1).to_broadcast([P, CHUNKS, P]), ALU.mult)\
                        .then_inc(sem("nm_ready"), 1)
                    if j == 3 and p + 1 < PAIRS:
                        build_bk(p + 1)
                if p + 1 < PAIRS:
                    build_ar(p + 1)
                gate_products(p)

            pool.wait_ge(sem("gate_weighed"), PAIRS)
            for step, j in GROUP_POOL:
                if step == "weigh":
                    pool.wait_ge(yc_ready, j + 1)
                    t = slice(*GN_GROUPS[j])
                    G.tensor_tensor(rw_k[:, t, :], y_wkv[:, t, :], rw_k[:, t, :], ALU.mult).then_inc(weighed, 1)
                elif step == "gate":
                    pool.wait_ge(bonus_shifted, j + 1)
                    t = slice(2 * j, 2 * j + 2)
                    G.tensor_tensor(rw_v[:, t, :], rw_v[:, t, :], g_wkv[:, t, :], ALU.mult).then_inc(bonus_gated, 1)
                else:
                    pool.wait_ge(scaled, j + 1)
                    pool.wait_ge(bonus_gated, GN_GROUPS[j][0] // 2 + 1)
                    t = slice(*GN_GROUPS[j])
                    G.tensor_tensor(rw_k[:, t, :], rw_k[:, t, :], rw_v[:, t, :], ALU.add).then_inc(group_done, 1)

            pool.wait_ge(const_b_in, 16)
            for r in range(N_ROPE):
                n = 1 if r == ROPE_KI else 2
                if r == ROPE_KI:
                    pool.wait_ge(sem("ki_loaded"), 1)
                else:
                    pool.wait_ge(un_free, freed(V_A + ROPE_USE[r]))
                if r:
                    pool.wait_ge(sem("rope_done"), r)
                G.tensor_tensor(rope_c[:, 0:n, :], rope_in[r % 2][:, 0:n, :], c_("cos").unsqueeze(1).to_broadcast([P, n, SEQ]), ALU.mult)\
                    .then_inc(sem("cos_done"), 1)

            for i in range(HEADS):
                if i == 0:
                    pool.wait_ge(sem("cumk_ready"), 8)
                if i >= 2:
                    pool.wait_ge(sem("max_ready"), HEADS + i - 1)
                for qt in range(QT):
                    ins = G.tensor_tensor(head_bias[i % 2][:, QUERY[qt]], causal[:, QUERY[qt]], cum_k[:, i, 0:KEYS[qt]], ALU.add)
                ins.then_inc(sem("bias_ready"), 1)

        @block.scalar
        def _(act):
            A_ = nc.scalar.activation

            def split_half(u, s):
                if u >= NU:
                    return
                n = unit_cols(u)
                if s == 0:
                    act.wait_ge(landed[u % NSTAGE], 32 * (u // NSTAGE + 1))
                    if u >= 2:
                        act.wait_ge(unit_done, u - 1)
                half = W_HALF[s]
                A_(w_hi[u % 2][:, half, 0:n], stage[u % NSTAGE][:, half, 0:n], ACT.Copy).then_inc(hi_made, 1)

            def split(u):
                split_half(u, 0)
                split_half(u, 1)

            chain = sem("act_chain")
            count = [0]

            def link(ins):
                count[0] += 1
                ins.then_inc(chain, 1)
                act.wait_ge(chain, count[0])

            def load_tables(set_id):
                act.add_instruction(mybir.InstLoadActFuncSet(name=nc.get_next_instruction_name(), engine=mybir.EngineType.Activation,
                                                             ins=[], outs=[], act_func_set_id=set_id))

            def square(n, t):
                act.wait_ge(x_ready, 8 * n + t + 1)
                if t == 0 and n:
                    act.wait_ge(stat_done, n)
                A_(sq[:, t, :], x[:, t, :], ACT.Square).then_inc(sq_ready, 1)

            def last_splits(u, n):
                for j in range(UPD):
                    if j < UPD - 1:
                        split(u + j + 2)
                    square(n, 2 * j)
                    square(n, 2 * j + 1)
                split(u + UPD + 1)
                norm_root(n)

            def norm_stats(n):
                for t in range(KT):
                    square(n, t)
                norm_root(n)

            def norm_root(n):
                act.wait_ge(stat_done, n + 1)
                A_(rstd[:, 1, :], stat_ps[:, 0, :], ACT.Ln, bias=eps_norm).then_inc(log_done, 1)
                act.wait_ge(log_done, n + 1)
                A_(rstd[:, 2, :], rstd[:, 1, :], ACT.Exp, scale=-0.5).then_inc(root_ready, 1)

            def norm_split(base, hi, shift):
                for t in range(KT):
                    act.wait_ge(normed, base + t + 1)
                    if shift is None:
                        A_(hi[:, t, :], tmp[:, t, :], ACT.Copy).then_inc(h_hi_made, 1)
                    else:
                        A_(hi[:, t, :], tmp[:, t, :], ACT.Identity, bias=shift[:, t:t + 1]).then_inc(h_hi_made, 1)

            def z_split(zc, j):
                act.wait_ge(zf_ready, zf_count(zc))
                A_(z_hi[:, 2 * j:2 * j + 2, :], zf[zc % 2][:], ACT.Copy).then_inc(z_hi_made, 1)

            def evac(u, v, dst, scale=1.0):
                act.wait_ge(unit_done, u + 1)
                A_(dst, un[v % 2][:], ACT.Copy, scale=scale).then_inc(un_free, 1)

            def mlp(m, n_next):
                u, v, zc = U_MLP[m], V_MLP[m], Z_MLP[m]
                for g in range(GROUPS):
                    for j in range(UPD):
                        uu = u + 2 * UPD * g + j
                        act.wait_ge(unit_done, uu + 1)
                        A_(relu_b[j % 2][:], un[(v + j) % 2][:], ACT.Relu).then_inc(relu_ready, 1)
                        if j < UPD - 1:
                            split(uu + 2)
                            z_split(zc + UPD * g + j, j)
                        else:
                            split_half(uu + 2, 0)
                            z_split(zc + UPD * g + j, j)
                            split_half(uu + 2, 1)
                    if g < GROUPS - 1:
                        for j in range(UPD):
                            split(u + 2 * UPD * g + UPD + j + 2)
                    else:
                        last_splits(u + 2 * UPD * g + UPD, n_next)

            load_tables(6)
            act.wait_ge(un_free, freed(V_VEC))
            A_(small[:, 8:16], vecT[:, VEC_C:VEC_C + KT], ACT.Exp, scale=-1.0).then_inc(silu_e, 1)
            norm_stats(N_CONV)
            split(0)
            split(1)
            norm_split(H_BASE[N_CONV], h_hi, mods[0][:, 0:8])
            for j in range(12):
                if j < 8:
                    dst = (b_gate if j < 4 else tmp)[:, 2 * (j % 4):2 * (j % 4) + 2, :]
                    evac(U_CONV_IN + j, V_CONV + j, dst)
                split(U_CONV_IN + j + 2)
                if j >= 8:
                    z_split(Z_CONV + j - 8, j - 8)
            last_splits(U_CONV_OUT, N_MLP0)
            norm_split(H_BASE[N_MLP0], h_hi, mods[0][:, 24:32])
            mlp(0, N_RW)
            mix_dst = (h_hi, z_hi, h_hi)

            def mix_split(m):
                act.wait_ge(mix_ready, m + 1)
                A_(mix_dst[m // KT][:, m % KT, :], mixf[:, m % 4, :], ACT.Copy).then_inc(mix_hi, 1)

            for t in range(KT + 2):
                if t < KT:
                    act.wait_ge(hs_normed, t + 1)
                    A_(tmp[:, t, :], tmp[:, t, :], ACT.Identity, bias=mods[1][:, t:t + 1]).then_inc(hs_shifted, 1)
                if t >= 2:
                    mix_split(t - 2)
            for m in range(KT, 2 * KT):
                mix_split(m)
            def wkv_build(p):
                if p:
                    act.wait_ge(built, p)
                A_(w_cum[:], rw_c[:, p, :], ACT.Exp, scale=-DECAY).then_inc(exp_ready, 1)
                A_(w_inv[:], rw_c[:, p, :], ACT.Exp, scale=DECAY).then_inc(exp_ready, 1)
                if p:
                    act.wait_ge(tok_done, 3 * p - 2)
                else:
                    act.wait_ge(sem("bd_zeroed"), 1)
                v = rw_v[:, p, :].rearrange("p (c s) -> p c s", c=CHUNKS)
                A_(v_bd[0:HD, :, 0:CHUNK], v[0:HD], ACT.Copy)
                A_(v_bd[HD:P, :, CHUNK:P], v[HD:P], ACT.Copy).then_inc(v_built, 1)

            def lora1_outs(n):
                if n == 0:
                    load_tables(2)
                act.wait_ge(lora1_done, n + 1)
                if n == 0:
                    A_(lora_h[0:RD, 0, :], acc[0][0:RD, 0, :], ACT.Tanh).then_inc(lora1_out, 1)
                elif n == 1:
                    A_(lora_h[RD:RD + RA, 1, :], acc[1][RD:RD + RA, 0, :], ACT.Copy).then_inc(lora1_out, 1)
                else:
                    A_(lora_h[:, 2, :], acc[2][:, 0, :], ACT.Sigmoid).then_inc(lora1_out, 1)
                    A_(lora_h[0:RG - P, 3, :], acc[3][0:RG - P, 0, :], ACT.Sigmoid).then_inc(lora1_out, 1)

            def lora2_outs(which):
                dst, vec = ((rw_a, VEC_A0), (rw_c, VEC_W0))[which]
                for t in range(KT):
                    if t % 2 == 0:
                        act.wait_ge(lora2_done, 4 * which + t // 2 + 1)
                    A_(dst[:, t, :], acc[t // 2][:, t % 2, :], ACT.Sigmoid, bias=vecT[:, vec + t:vec + t + 1]).then_inc(lora2_out, 1)

            for j in range(12):
                dst = (rw_k, rw_r, rw_v)[j // 4]
                evac(U_RWK + j, V_RKV + j, dst[:, 2 * (j % 4):2 * (j % 4) + 2, :])
                split(U_RWK + j + 2)
                if j == 3:
                    for m in range(2 * KT, 3 * KT):
                        mix_split(m)
                if 3 <= j <= 5:
                    lora1_outs(j - 3)
                if j == 7:
                    load_tables(2)
                if 7 <= j <= 8:
                    lora2_outs(j - 7)
                if j == 5:
                    act.wait_ge(lora_mixed, 3)
                    for k in range(4):
                        act.wait_ge(kk0_ready, k + 1)
                        A_(tmp[:, 2 * k:2 * k + 2, :], rw_kk[:, 2 * k:2 * k + 2, :], ACT.Square).then_inc(kksq_ready, 1)
                if j == 6:
                    load_tables(6)
                    for k in range(4):
                        s2 = slice(2 * k, 2 * k + 2)
                        act.wait_ge(ss_ready, k + 1)
                        link(A_(sq[:, s2, :], tmp[:, s2, :], ACT.Ln))
                        A_(sq[:, s2, :], sq[:, s2, :], ACT.Exp, scale=-0.5).then_inc(ss_root, 1)
                if j == 10:
                    load_tables(6)
                    act.wait_ge(sem("rw_ready"), 1)
                    for k in range(4):
                        act.wait_ge(lora2_done, 8 + k + 1)
                        A_(g_wkv[:, 2 * k:2 * k + 2, :], acc[k][:], ACT.Copy).then_inc(lora2_out, 1)
                    act.wait_ge(cum_ready, 1)
                    A_(w_end[:], rw_c[:].rearrange("p t (c s) -> p t c s", c=CHUNKS)[:, :, :, CHUNK - 1], ACT.Exp, scale=-DECAY).then_inc(end_ready, 1)
                    wkv_build(0)

            def group_step(step, j):
                if step == "square":
                    t = slice(*GN_GROUPS[j])
                    act.wait_ge(yc_ready, j + 1)
                    A_(rw_kk[:, t, :], y_wkv[:, t, :], ACT.Square).then_inc(ycsq_ready, 1)
                elif step == "root":
                    t = slice(*GN_GROUPS[j])
                    act.wait_ge(gn_var_done, j + 1)
                    link(A_(rw_kk[:, t, :], gn_bank[j][:, 0:GN_GROUPS[j][1] - GN_GROUPS[j][0], :], ACT.Ln, bias=eps_group))
                    A_(rw_kk[:, t, :], rw_kk[:, t, :], ACT.Exp, scale=-0.5).then_inc(gv_root, 1)
                else:
                    act.wait_ge(bonus_ready, j + 1)
                    for t in (2 * j, 2 * j + 1):
                        ins = A_(rw_v[:, t, :], rw_v[:, t, :], ACT.Identity, bias=vecT[:, VEC_LNB + t:VEC_LNB + t + 1])
                    ins.then_inc(bonus_shifted, 1)

            for slot in range(PAIRS + 1):
                for n, (step, p, j, h) in enumerate(wkv_steps(slot)):
                    half = slice(2 * h, 2 * h + 2)
                    if step == "tok":
                        for m, (dst, src) in ((0, (v_tok, un[0])), (1, (b_tok, un[1]))) if h == 0 else ((2, (k_tok, un[0])),):
                            act.wait_ge(tok_done, 3 * p + m + 1)
                            A_(dst[p % 2][:], bank4(src), ACT.Copy).then_inc(tok_out, 1)
                    elif step == "x1":
                        act.wait_ge(x1_done, 2 * p + h + 1)
                        A_(inv_x[:, half, :], bank4(acc[h])[:, 0:2, :], ACT.Copy).then_inc(x1_out, 1)
                        if h == 1 and p + 1 < PAIRS:
                            wkv_build(p + 1)
                    elif step == "t1":
                        act.wait_ge(t1_done, 10 * p + 2 * (j - 1) + h + 1)
                        A_(t1[:, half, :], bank4(acc[h])[:, 0:2, :], ACT.Copy).then_inc(t1_out, 1)
                    elif step == "rhs":
                        act.wait_ge(rhs_done, CHUNKS * p + j + 1)
                        A_(wkv_rhs[:], stat_ps[:, 0, 0:P], ACT.Copy).then_inc(rhs_out, 1)
                    elif step == "u":
                        act.wait_ge(u_done, CHUNKS * p + j + 1)
                        A_(wkv_u[:], stat_ps[:, 0, 0:P], ACT.Copy).then_inc(u_out, 1)
                    for group in GROUP_ACT.get(n, ()) if slot == PAIRS else ():
                        group_step(*group)
            def rw_split(j):
                act.wait_ge(group_done, min(j + 1, UPD))
                if j == UPD - 1:
                    act.wait_ge(last_done, 1)
                A_(z_hi[:, 2 * j:2 * j + 2, :], rw_k[:, 2 * j:2 * j + 2, :], ACT.Copy).then_inc(z_hi_made, 1)

            act.wait_ge(y_done, CHUNKS * PAIRS)
            rw_split(0)
            group_step("square", 4)
            rw_split(1)
            group_step("root", 4)
            rw_split(2)
            rw_split(3)
            last_splits(U_RWO, N_MLP1)
            norm_split(H_BASE[N_MLP1], h_hi, mods[1][:, 24:32])
            mlp(1, N_FIN1)

            def attention(kind, z0):
                b = HEADS * kind
                for i in range(HEADS + 6):
                    if i < HEADS:
                        act.wait_ge(max_ready, b + i + 1)
                        if b + i >= NA:
                            act.wait_ge(pt_done, b + i - NA + 1)
                        for qt in range(QT):
                            A_(probs[i % NA][:, QUERY[qt]], logit[i % NA][:, QUERY[qt]], ACT.Exp, bias=stat[i % NA][:, qt:qt + 1],
                               accum_out=stat[i % NA][:, 2 + qt:3 + qt]).then_inc(exp_done, 1)
                    if 1 <= i <= HEADS:
                        k = i - 1
                        act.wait_ge(sum_ready, b + k + 1)
                        A_(probs[k % NA][:, QUERY[0]], probs[k % NA][:, QUERY[0]], ACT.Copy, scale=stat[k % NA][:, 4:5]).then_inc(p0_ready, 1)
                    if 2 <= i < HEADS + 2:
                        k = i - 2
                        act.wait_ge(pt_done, b + k + 1)
                        if b + k >= 2:
                            act.wait_ge(pv_done, b + k - 1)
                        A_(probs_t[k % 2][:], flat((stat_ps, misc)[k % 2])[:, 0:3 * P]
                           .rearrange("p (c q) -> p c q", c=3), ACT.Copy).then_inc(pt_out, 1)
                    if i >= 9 and (i - 9) % 4 == 0:
                        z_split(z0 + (i - 9) // 4, (i - 9) // 4)

            norm_stats(N_A)
            norm_split(H_BASE[N_A], h_hi, None)

            def rope_load(u, v, r, n, scale=1.0, signal=None):
                act.wait_ge(unit_done, u + 1)
                if r >= 2:
                    act.wait_ge(rope_done, r - 1)
                A_(rope_in[r % 2][:, 0:n, :], un[v % 2][:, 0:n, :], ACT.Copy, scale=scale).then_inc(signal or un_free, 1)

            rope_load(U_KI, V_A, ROPE_KI, 1, signal=ki_loaded)
            split(U_KI + 2)
            act.wait_ge(un_free, freed(V_A))
            for j in range(2):
                rope_load(U_QI + j, V_A + 1 + j, ROPE_QI + j, 2)
                split(U_QI + j + 2)
            rope_load(U_KA, V_A + 3, ROPE_K, 2)
            split(U_KA + 2)
            def score_relus(qt):
                act.wait_ge(score_done, qt + 1)
                for n in range(IDX_HEADS // 2):
                    k = IDX_HEADS // 2 * qt + n
                    if k >= 2:
                        act.wait_ge(score_used, k - 1)
                    A_(score_r[n % 2][:, :, 0:KEYS[qt]], acc[n][:, :, 0:KEYS[qt]], ACT.Relu).then_inc(score_relu, 1)

            evac(U_VA, V_A + 4, vA_tok[:])
            split(U_VA + 2)
            score_relus(0)
            act.wait_ge(rope_done, ROPE_K + 1)
            for j in range(KV_HEADS):
                src = kA_fm[HD * (j % 2):HD * (j % 2) + HD, j // 2, :]
                A_(k_dup[0:HD, j, :], src, ACT.Copy)
                A_(k_dup[HD:P, j, :], src, ACT.Copy).then_inc(kdup_ready, 1)
            for j in range(UPD):
                rope_load(U_QA + j, V_A + 5 + j, ROPE_Q + j, 2, scale=HD ** -0.5)
                split(U_QA + j + 2)
                if j == 0:
                    score_relus(1)
            attention(0, Z_A)
            last_splits(U_OA, N_MLP2)
            norm_split(H_BASE[N_MLP2], h_hi, None)
            mlp(2, N_B)
            norm_split(H_BASE[N_B], h_hi, None)
            norm_split(H_BASE["B_q"], z_hi, None)
            split(U_F + 2)
            act.wait_ge(f_abs, 1)
            A_(f_l[:], f_e[:], ACT.Exp, scale=-1.0).then_inc(f_exp, 1)
            act.wait_ge(f_one, 1)
            A_(f_l[:], f_l[:], ACT.Ln).then_inc(f_log, 1)
            for j in range(UPD):
                evac(U_KB + j, V_B + 1 + j, kB_fm[:, 2 * j:2 * j + 2, :])
                split(U_KB + j + 2)
            for r in range(8):
                act.wait_ge(f_bcast, r + 1)
                A_(cum_k[:, 2 * r:2 * r + 2, :], acc[r % 4][:], ACT.Copy).then_inc(cumk_ready, 1)
            for j in range(UPD):
                evac(U_VB + j, V_B + 5 + j, vB_tok[:, :, UC * j:UC * (j + 1)])
                split(U_VB + j + 2)
            for j in range(UPD):
                evac(U_QB + j, V_B + 9 + j, q_fm[:, 2 * j:2 * j + 2, :], scale=HD ** -0.5)
                split(U_QB + j + 2)
            attention(1, Z_B)
            last_splits(U_OB, N_MLP3)
            norm_split(H_BASE[N_MLP3], h_hi, None)
            mlp(3, N_OUT)

        @block.vector
        def _(dve):
            V = nc.vector
            chain = sem("dve_chain")
            count = [0]

            def link(ins):
                count[0] += 1
                ins.then_inc(chain, 1)
                dve.wait_ge(chain, count[0])

            def split_half(u, s):
                if u >= NU:
                    return
                n = unit_cols(u)
                dve.wait_ge(hi_made, 2 * u + s + 1)
                half = W_HALF[s]
                V.tensor_tensor(w_lo[u % 2][:, half, 0:n], stage[u % NSTAGE][:, half, 0:n], w_hi[u % 2][:, half, 0:n].bitcast(F32),
                                ALU.subtract).then_inc(lo_made, 1)

            def split(u):
                split_half(u, 0)
                split_half(u, 1)

            def norm_stats(n):
                dve.wait_ge(log_done, n + 1)
                V.tensor_scalar(rstd[:, 0, :], stat_ps[:, 0, :], NORM_EPS, -0.5, ALU.add, ALU.mult).then_inc(ms_ready, 1)
                dve.wait_ge(root_ready, n + 1)
                dve.wait_ge(ms_ready, n + 1)
                link(V.tensor_tensor(rstd[:, 1, :], rstd[:, 0, :], rstd[:, 2, :], ALU.mult))
                link(V.tensor_tensor(rstd[:, 1, :], rstd[:, 1, :], rstd[:, 2, :], ALU.mult))
                link(V.scalar_tensor_tensor(out=rstd[:, 2, :], in0=rstd[:, 1, :], scalar=1.5, in1=rstd[:, 2, :], op0=ALU.add, op1=ALU.mult))

            def norm_mul(dst, t, g):
                return V.scalar_tensor_tensor(out=dst[:, t, :], in0=x[:, t, :], scalar=g[:, t:t + 1], in1=rstd[:, 2, :],
                                              op0=ALU.mult, op1=ALU.mult)

            def norm_split(base, g, shift, hi, lo):
                for t in range(KT + 2):
                    if t < KT:
                        norm_mul(tmp, t, g).then_inc(normed, 1)
                    if t >= 2:
                        k = t - 2
                        dve.wait_ge(h_hi_made, base + k + 1)
                        if shift is None:
                            ins = V.tensor_tensor(lo[:, k, :], tmp[:, k, :], hi[:, k, :].bitcast(F32), ALU.subtract)
                        else:
                            ins = V.scalar_tensor_tensor(out=lo[:, k, :], in0=tmp[:, k, :], scalar=shift[:, k:k + 1],
                                                         in1=hi[:, k, :].bitcast(F32), op0=ALU.add, op1=ALU.subtract)
                        ins.then_inc(h_lo_made, 1)

            def z_split(zc, j):
                dve.wait_ge(z_hi_made, zc + 1)
                V.tensor_tensor(z_lo[:, 2 * j:2 * j + 2, :], zf[zc % 2][:], z_hi[:, 2 * j:2 * j + 2, :].bitcast(F32),
                                ALU.subtract).then_inc(z_lo_made, 1)

            def residual(u, gate, j, b):
                dve.wait_ge(unit_done, u + 1)
                for m in range(2):
                    t = 2 * j + m
                    if gate is None:
                        ins = V.tensor_tensor(x[:, t, :], b[:, m, :], x[:, t, :], ALU.add)
                    else:
                        ins = V.scalar_tensor_tensor(out=x[:, t, :], in0=b[:, m, :], scalar=gate[:, t:t + 1], in1=x[:, t, :],
                                                     op0=ALU.mult, op1=ALU.add)
                    ins.then_inc(x_ready, 1)

            def last_residuals(u, gate, j):
                if j == UPD - 1:
                    residual(u + j, gate, j, acc[j])
                split(u + j + 2)
                if j < UPD - 1:
                    residual(u + j, gate, j, acc[j])

            def mlp(m, gate):
                u, v, zc = U_MLP[m], V_MLP[m], Z_MLP[m]
                for g in range(GROUPS):
                    for j in range(UPD):
                        uu = u + 2 * UPD * g + j
                        k = zc + UPD * g + j
                        dve.wait_ge(relu_ready, 4 * GROUPS * m + UPD * g + j + 1)
                        V.scalar_tensor_tensor(out=zf[k % 2][:], in0=un[(v + j) % 2][:], scalar=0.0, in1=relu_b[j % 2][:],
                                               op0=ALU.max, op1=ALU.mult).then_inc(zf_ready, 1)
                        dve.wait_ge(zf_ready, zf_count(k))
                        V.engine_nop().then_inc(un_free, 1)
                        if j < UPD - 1:
                            split(uu + 2)
                            z_split(k, j)
                        else:
                            split_half(uu + 2, 0)
                            z_split(k, j)
                            split_half(uu + 2, 1)
                    for j in range(UPD):
                        if g < GROUPS - 1:
                            split(u + 2 * UPD * g + UPD + j + 2)
                        else:
                            last_residuals(u + 2 * UPD * g + UPD, gate, j)
                        if m == 0 and j in (0, 2):
                            ada()

            V.memset(eps_norm, NORM_EPS)
            V.memset(eps_group, GN_EPS)
            dve.wait_ge(tp_done, 1)
            V.tensor_copy(vecT[:], flat(un[0])[:, 0:N_VEC]).then_inc(un_free, 1)
            for j in range(4):
                dve.wait_ge(tp_done, 2 + j)
                V.tensor_copy(x[:, 2 * j:2 * j + 2, :], un[(V_X + j) % 2][:]).then_inc(x_ready, 2)
            dve.wait_ge(silu_e, 1)
            link(V.tensor_scalar(small[:, 16:24], small[:, 8:16], 1.0, None, ALU.add))
            link(V.reciprocal(small[:, 24:32], small[:, 16:24]))
            V.tensor_tensor(c_silu, vecT[:, VEC_C:VEC_C + KT], small[:, 24:32], ALU.mult).then_inc(silu_ready, 1)
            dve.wait_ge(silu_ready, 1)
            norm_stats(N_CONV)

            ada_done = [0]

            def ada():
                k = ada_done[0]
                ada_done[0] += 1
                a = ADA_DVE[k]
                if a < ADA_FIRST:
                    dve.wait_ge(ada_first_landed[a], 16)
                    w = ada_first[a]
                else:
                    dve.wait_ge(ada_dve_landed, 16 * (k + 1 - ada_count(ADA_DVE, ADA_FIRST)))
                    w = ada_dve
                    if a >= N_ADA > ADA_DVE[k - 1]:
                        dve.wait_ge(ada_summed, 4)
                dst = ada_acc[:, a % N_ADA * UC:(a % N_ADA + 1) * UC]
                link(V.tensor_scalar(dst, w[:, 0, :], c_silu[:, 0:1], None, ALU.mult))
                for t in range(1, KT):
                    ins = V.scalar_tensor_tensor(out=dst, in0=w[:, t, :], scalar=c_silu[:, t:t + 1], in1=dst, op0=ALU.mult, op1=ALU.add)
                    if t < KT - 1:
                        link(ins)
                ins.then_inc(ada_dve_done, 1)

            def mod_out(layer, c0, c1, k):
                dve.wait_ge(ada_summed_pe, k)
                V.tensor_tensor(mods[layer][:, c0:c1], misc[:, 0, c0:c1], vecT[:, VEC_ADA_B + 48 * layer + c0:VEC_ADA_B + 48 * layer + c1],
                                ALU.add).then_inc(ada_summed, 1)
                dve.wait_ge(ada_summed, k)

            def mod_gain(layer, sub):
                link(V.scalar_tensor_tensor(out=gain[:, 2 * layer + sub, :], in0=mods[layer][:, 24 * sub + 8:24 * sub + 16], scalar=1.0,
                                            in1=vecT[:, VEC_NORM_G + 8 * (2 * layer + sub):VEC_NORM_G + 8 * (2 * layer + sub) + 8],
                                            op0=ALU.add, op1=ALU.mult))

            for _ in range(ada_count(ADA_DVE, ADA_FIRST)):
                ada()
            split(0)
            split(1)
            mod_out(0, 0, 16, 1)
            mod_gain(0, 0)
            norm_split(H_BASE[N_CONV], gain[:, 0, :], mods[0][:, 0:8], h_hi, h_lo)
            link(V.memset(u_pad[:, :, 0:2], 0.0))
            conv_w = [vecT[:, VEC_CONV_W + 8 * k:VEC_CONV_W + 8 * k + 8] for k in range(3)]
            for j in range(12):
                if j < 8:
                    split(U_CONV_IN + j + 2)
                else:
                    k = j - 8
                    t0 = 2 * k
                    dve.wait_ge(unit_done, U_CONV_IN + j + 1)
                    dve.wait_ge(un_free, freed(V_CONV + 7))
                    V.tensor_tensor(u_pad[:, t0:t0 + 2, 2:PADT], un[(V_CONV + j) % 2][:], tmp[:, t0:t0 + 2, :], ALU.mult).then_inc(un_free, 1)
                    dve.wait_ge(un_free, freed(V_CONV + j))
                    for m in range(2):
                        ins = V.tensor_scalar(conv_y[:, m, :], u_pad[:, t0 + m, 2:PADT], conv_w[2][:, t0 + m:t0 + m + 1], None, ALU.mult)
                    link(ins)
                    for tap in (1, 0):
                        for m in range(2):
                            ins = V.scalar_tensor_tensor(out=conv_y[:, m, :], in0=u_pad[:, t0 + m, tap:tap + SEQ],
                                                         scalar=conv_w[tap][:, t0 + m:t0 + m + 1], in1=conv_y[:, m, :],
                                                         op0=ALU.mult, op1=ALU.add)
                        link(ins)
                    V.tensor_tensor(zf[(Z_CONV + k) % 2][:], conv_y[:], b_gate[:, t0:t0 + 2, :], ALU.mult).then_inc(zf_ready, 1)
                    split(U_CONV_IN + j + 2)
                    z_split(Z_CONV + k, k)
                if j % 2:
                    ada()
            mod_out(0, 16, 24, 2)
            for j in range(UPD):
                last_residuals(U_CONV_OUT, mods[0][:, 16:24], j)
            norm_stats(N_MLP0)
            mod_out(0, 24, 40, 3)
            mod_gain(0, 1)
            norm_split(H_BASE[N_MLP0], gain[:, 1, :], mods[0][:, 24:32], h_hi, h_lo)
            mod_out(0, 40, 48, 4)
            mlp(0, mods[0][:, 40:48])
            mod_out(1, 0, 16, 5)
            mod_gain(1, 0)
            norm_stats(N_RW)
            def mix(dst, t, which):
                c = VEC_MU + 8 * which + t
                return V.scalar_tensor_tensor(out=dst, in0=sq[:, t, :], scalar=vecT[:, c:c + 1], in1=tmp[:, t, :], op0=ALU.mult, op1=ALU.add)

            mix_dst = ((h_hi, h_lo), (z_hi, z_lo), (h_hi, h_lo))
            mix_mu = (2, 0, 3)

            def mix_in(m):
                if m >= 4:
                    dve.wait_ge(mix_lo, m - 3)
                mix(mixf[:, m % 4, :], m % KT, mix_mu[m // KT]).then_inc(mix_ready, 1)

            def mix_low(m):
                hi, lo = mix_dst[m // KT]
                dve.wait_ge(mix_hi, m + 1)
                V.tensor_tensor(lo[:, m % KT, :], mixf[:, m % 4, :], hi[:, m % KT, :].bitcast(F32), ALU.subtract).then_inc(mix_lo, 1)

            dve.wait_ge(ada_pool_done, len(ADA_POOL))
            for t in range(KT + 3):
                if t < KT:
                    norm_mul(tmp, t, gain[:, 2, :]).then_inc(hs_normed, 1)
                if 1 <= t <= KT:
                    k = t - 1
                    dve.wait_ge(hs_shifted, k + 1)
                    V.tensor_tensor(sq[:, k, 1:SEQ], tmp[:, k, 0:SEQ - 1], tmp[:, k, 1:SEQ], ALU.subtract)
                    V.tensor_scalar(sq[:, k, 0:1], tmp[:, k, 0:1], -1.0, None, ALU.mult).then_inc(xx_ready, 1)
                    dve.wait_ge(xx_ready, k + 1)
                    mix_in(k)
                if t >= 3:
                    mix_low(t - 3)

            def mixes(m0, m1):
                for m in range(m0, m1 + 2):
                    if m < m1:
                        mix_in(m)
                    if m - 2 >= m0:
                        mix_low(m - 2)

            mod_out(1, 16, 48, 6)
            mod_gain(1, 1)
            mixes(KT, 2 * KT)
            for j in range(12):
                if j == 4:
                    dve.wait_ge(unit_done, U_RWK + 4)
                    mixes(2 * KT, 3 * KT)
                split(U_RWK + j + 2)
                if j == 4:
                    dve.wait_ge(un_free, freed(V_RKV + 3))
                    dve.wait_ge(mix_lo, 3 * KT)
                    for k in range(4):
                        for t in (2 * k, 2 * k + 1):
                            ins = V.tensor_scalar(rw_kk[:, t, :], rw_k[:, t, :], vecT[:, VEC_KK + t:VEC_KK + t + 1], None, ALU.mult)
                        ins.then_inc(kk0_ready, 1)
                if j == 6:
                    for k in range(4):
                        dve.wait_ge(ss_done, k + 1)
                        V.tensor_scalar(tmp[:, 2 * k:2 * k + 2, :], acc[k][:], 1e-24, None, ALU.max).then_inc(ss_ready, 1)
                if j == 7:
                    dve.wait_ge(ss_ready, 4)
                    dve.wait_ge(ss_root, 4)
                    link(V.tensor_tensor(tmp[:], tmp[:], sq[:], ALU.mult))
                    link(V.tensor_tensor(tmp[:], tmp[:], sq[:], ALU.mult))
                if j == 8:
                    link(V.scalar_tensor_tensor(out=tmp[:], in0=tmp[:], scalar=-3.0, in1=sq[:], op0=ALU.add, op1=ALU.mult))
                    link(V.scalar_tensor_tensor(out=rw_kk[:], in0=rw_kk[:], scalar=0.5, in1=tmp[:], op0=ALU.mult, op1=ALU.mult))
                if j == 9:
                    dve.wait_ge(lora2_out, 16)
                    for t in range(KT):
                        ins = V.tensor_tensor_scan(rw_c[:, t, :], c_("resets"), rw_c[:, t, :], 0.0, ALU.mult, ALU.add)
                    ins.then_inc(cum_ready, 1)
                    for t in range(KT):
                        ins = V.tensor_scalar(tmp[:, t, :], rw_a[:, t, :], -1.0, vecT[:, VEC_KA + t:VEC_KA + t + 1], ALU.add, ALU.mult)
                    link(ins)
                    V.scalar_tensor_tensor(out=rw_k[:], in0=tmp[:], scalar=1.0, in1=rw_k[:], op0=ALU.add, op1=ALU.mult)
                    V.scalar_tensor_tensor(out=rw_a[:], in0=rw_a[:], scalar=-1.0, in1=rw_kk[:], op0=ALU.mult, op1=ALU.mult).then_inc(sem("rw_ready"), 1)
            dve.wait_ge(unit_done, U_RWV + 4)
            dve.wait_ge(end_ready, 1)
            bc4 = lambda m, n: m.unsqueeze(1).to_broadcast([P, n, m.shape[-1]])

            def group_step(step, j):
                if step == "bonus":
                    t = slice(2 * j, 2 * j + 2)
                    dve.wait_ge(bonus_done, j + 1)
                    V.tensor_tensor(rw_v[:, t, :], bonus_bank[j][:], rw_v[:, t, :], ALU.mult).then_inc(bonus_ready, 1)
                    return
                t, bank = slice(*GN_GROUPS[j]), gn_bank[j][:, 0:GN_GROUPS[j][1] - GN_GROUPS[j][0], :]
                if step == "center":
                    dve.wait_ge(gn_mean_done, j + 1)
                    V.tensor_tensor(y_wkv[:, t, :], y_wkv[:, t, :], bank, ALU.subtract).then_inc(yc_ready, 1)
                else:
                    dve.wait_ge(gv_root, j + 1)
                    s, r = rw_a[:, t, :], rw_kk[:, t, :]
                    link(V.scalar_tensor_tensor(out=s, in0=bank, scalar=GN_EPS, in1=r, op0=ALU.add, op1=ALU.mult))
                    link(V.tensor_tensor(s, s, r, ALU.mult))
                    link(V.scalar_tensor_tensor(out=s, in0=s, scalar=-3.0, in1=r, op0=ALU.add, op1=ALU.mult))
                    dve.wait_ge(weighed, j + 1)
                    V.scalar_tensor_tensor(out=rw_k[:, t, :], in0=rw_k[:, t, :], scalar=-0.5, in1=s, op0=ALU.mult, op1=ALU.mult).then_inc(scaled, 1)

            for slot in range(PAIRS + 1):
                for n, (step, p, j, h) in enumerate(wkv_steps(slot)):
                    half, half2 = slice(2 * h, 2 * h + 2), slice(2 * P * h, 2 * P * (h + 1))
                    xt = inv_t[p % 2]
                    if step == "gram":
                        dve.wait_ge(g_done, 2 * p + h + 1)
                        raw_n = acc[h][:, :, 0:P]
                        V.tensor_tensor(xt[:, half, :], raw_n, bc4(level_t[:, 0, :], 2), ALU.mult)
                        V.tensor_tensor(n_t[:, half, :], raw_n, bc4(c_("before"), 2), ALU.mult)
                        V.tensor_tensor(n_m[0][:, half, :], raw_n, bc4(level_t[:, 1, :], 2), ALU.mult)
                        link(V.tensor_tensor(lrb_t[p % 2][:, half, :], acc[h][:, :, P:P + CHUNK], bc4(c_("upto"), 2), ALU.mult))
                        V.tensor_tensor(xt[:, half, :], xt[:, half, :], bc4(ident, 2), ALU.add).then_inc(inv_ready, 1)
                    elif step == "tok":
                        raw_k = acc[2 + h]
                        V.tensor_tensor(lak_t[p % 2][:, half, :], raw_k[:, :, 0:P], bc4(c_("before"), 2), ALU.mult)
                        V.tensor_tensor(lrk_t[p % 2][:, half, :], raw_k[:, :, P:P + CHUNK], bc4(c_("upto"), 2), ALU.mult).then_inc(lak_ready, 1)
                    elif step == "dx":
                        dve.wait_ge(dx_done, 10 * p + 2 * (j - 1) + h + 1)
                        if j < WKV_LEVELS[-1]:
                            x_ = early(flat(inv_x)[:, half2], j)
                            V.tensor_tensor(x_, early(flat(acc[2 + h])[:, 0:2 * P], j), x_, ALU.add)
                        x_ = late(flat(xt)[:, half2], j)
                        V.tensor_tensor(x_, late(flat(un[h])[:, 0:2 * P], j), x_, ALU.add).then_inc(inv_ready, 1)
                    elif step == "sy":
                        c = j
                        last = w_end[:, p, c:c + 1]
                        if c < CHUNKS - 1:
                            k = (CHUNKS - 1) * p + c
                            if c:
                                dve.wait_ge(state_ready, k)
                                link(V.tensor_scalar(state_kept[:], state[(c - 1) % 2][:], last, None, ALU.mult))
                            dve.wait_ge(s_done, k + 1)
                            if c == 0:
                                V.tensor_scalar(state[0][:], stat_ps[:, 0, 0:P], last, None, ALU.mult).then_inc(state_ready, 1)
                            else:
                                V.scalar_tensor_tensor(out=state[c % 2][:], in0=stat_ps[:, 0, 0:P], scalar=last, in1=state_kept[:],
                                                       op0=ALU.mult, op1=ALU.add).then_inc(state_ready, 1)
                        dve.wait_ge(y_done, CHUNKS * p + c + 1)
                        V.tensor_copy(y_wkv[:, p, CHUNK * c:CHUNK * (c + 1)], misc[:, 0, 0:CHUNK]).then_inc(y_out, 1)
                    for group in GROUP_DVE.get(n, ()) if slot == PAIRS else ():
                        group_step(*group)
            def rw_split(j):
                dve.wait_ge(z_hi_made, Z_RW + j + 1)
                t = slice(2 * j, 2 * j + 2)
                V.tensor_tensor(z_lo[:, t, :], rw_k[:, t, :], z_hi[:, t, :].bitcast(F32), ALU.subtract).then_inc(z_lo_made, 1)

            group_step("center", 4)
            rw_split(0)
            rw_split(1)
            group_step("scale", 4)
            dve.wait_ge(scaled, len(GN_GROUPS))
            dve.wait_ge(bonus_gated, UPD)
            V.tensor_tensor(rw_k[:, KT - 1, :], rw_k[:, KT - 1, :], rw_v[:, KT - 1, :], ALU.add).then_inc(last_done, 1)
            rw_split(2)
            rw_split(3)
            for j in range(UPD):
                last_residuals(U_RWO, mods[1][:, 16:24], j)
            norm_stats(N_MLP1)
            norm_split(H_BASE[N_MLP1], gain[:, 3, :], mods[1][:, 24:32], h_hi, h_lo)
            mlp(1, mods[1][:, 40:48])
            norm_stats(N_FIN1)
            for t in range(KT):
                norm_mul(x, t, vecT[:, VEC_FINAL:VEC_FINAL + KT]).then_inc(x_ready, 1)

            def rope(r, n, dst):
                dve.wait_ge(rot_done, r + 1)
                link(V.tensor_tensor(dst, misc[:, 0:n, :], bc4(c_("sin"), n), ALU.mult))
                dve.wait_ge(cos_done, r + 1)
                V.tensor_tensor(dst, dst, rope_c[:, 0:n, :], ALU.add).then_inc(rope_done, 1)

            def attention(kind, z0):
                b = HEADS * kind
                for i in range(HEADS + 6):
                    if i < HEADS:
                        lg, st = logit[i % NA], stat[i % NA]
                        dve.wait_ge(qk_done, b + i + 1)
                        if kind == 0:
                            link(V.tensor_tensor(lg[:], flat(acc[i % 4])[:, 0:PACK], sel_bias[:], ALU.add))
                        else:
                            dve.wait_ge(sem("bias_ready"), i + 1)
                            for qt in range(QT):
                                ins = V.scalar_tensor_tensor(out=lg[:, QUERY[qt]], in0=flat(acc[i % 4])[:, QUERY[qt]], scalar=cum_q[:, qt, i:i + 1],
                                                             in1=head_bias[i % 2][:, QUERY[qt]], op0=ALU.add, op1=ALU.add)
                            link(ins)
                        for qt in range(QT):
                            ins = V.tensor_reduce(st[:, qt:qt + 1], lg[:, QUERY[qt]], AX_X, ALU.max, negate=True)
                        ins.then_inc(max_ready, 1)
                    if 1 <= i <= HEADS:
                        k = i - 1
                        st = stat[k % NA]
                        dve.wait_ge(exp_done, QT * (b + k + 1))
                        V.reciprocal(st[:, 4:4 + QT], st[:, 2:2 + QT]).then_inc(sum_ready, 1)
                        dve.wait_ge(sum_ready, b + k + 1)
                        V.tensor_scalar(probs[k % NA][:, QUERY[1]], probs[k % NA][:, QUERY[1]], st[:, 5:6], None, ALU.mult).then_inc(p1_ready, 1)
                    if i >= 7 and (i - 7) % 4 == 0:
                        j = (i - 7) // 4
                        dve.wait_ge(pv_done, b + 4 * j + 4)
                        V.tensor_copy(zf[(z0 + j) % 2][:], un[j % 2][:]).then_inc(zf_ready, 1)
                    if i >= 9 and (i - 9) % 4 == 0:
                        z_split(z0 + (i - 9) // 4, (i - 9) // 4)

            norm_stats(N_A)
            norm_split(H_BASE[N_A], vecT[:, VEC_GA:VEC_GA + KT], None, h_hi, h_lo)
            dve.wait_ge(const_b_in, 16)
            dve.wait_ge(ki_loaded, 1)
            V.tensor_scalar(wi_tok[:], un[V_A % 2][:, 1, 0:QT * IDX_HEADS].rearrange("p (a h) -> p a h", a=QT),
                            IDX_HEADS ** -0.5 * HD ** -0.5, None, ALU.mult).then_inc(un_free, 1)

            def scores(qt):
                dst = score[:, QUERY[qt]]
                for n in range(IDX_HEADS // 2):
                    dve.wait_ge(score_relu, IDX_HEADS // 2 * qt + n + 1)
                    for o in range(2):
                        h = 4 * (n // 2) + n % 2 + 2 * o
                        before = admit[:, QUERY[qt]] if n == 0 and o == 0 else dst
                        link(V.scalar_tensor_tensor(out=dst, in0=score_r[n % 2][:, o, 0:KEYS[qt]], scalar=wi_tok[:, qt, h:h + 1], in1=before,
                                                    op0=ALU.mult, op1=ALU.add))
                    V.engine_nop().then_inc(score_used, 1)

            def select(rounds):
                for _ in range(rounds):
                    for qt in range(QT):
                        ins = V.max(top8[:, qt, :], score[:, QUERY[qt]])
                    link(ins)
                    for qt in range(QT):
                        ins = V.match_replace(score[:, QUERY[qt]], top8[:, qt, :], score[:, QUERY[qt]], TAKEN)
                    link(ins)

            split(U_KI + 2)
            split(U_QI + 2)
            rope(ROPE_KI, 1, ki_fm[:])
            split(U_QI + 3)
            rope(ROPE_QI, 2, qi_fm[:, 0:2, :])
            split(U_KA + 2)
            rope(ROPE_QI + 1, 2, qi_fm[:, 2:4, :])
            split(U_VA + 2)
            rope(ROPE_K, 2, kA_fm[:])
            scores(0)
            split(U_QA + 2)
            scores(1)
            split(U_QA + 3)
            rope(ROPE_Q, 2, q_fm[:, 0:2, :])
            rounds = TOPK // 8
            select(rounds // 3)
            split(U_QA + 4)
            rope(ROPE_Q + 1, 2, q_fm[:, 2:4, :])
            select(rounds // 3)
            split(U_QA + 5)
            rope(ROPE_Q + 2, 2, q_fm[:, 4:6, :])
            select(rounds - 2 * (rounds // 3))
            link(V.tensor_scalar(sel_bias[:], score[:], 0.5 * TAKEN, NEG, ALU.is_gt, ALU.mult))
            rope(ROPE_Q + 3, 2, q_fm[:, 6:8, :])
            attention(0, Z_A)
            for j in range(UPD):
                last_residuals(U_OA, None, j)
            norm_stats(N_MLP2)
            norm_split(H_BASE[N_MLP2], vecT[:, VEC_GMLP:VEC_GMLP + KT], None, h_hi, h_lo)
            mlp(2, None)
            norm_stats(N_B)
            norm_split(H_BASE[N_B], vecT[:, VEC_GKV:VEC_GKV + KT], None, h_hi, h_lo)
            norm_split(H_BASE["B_q"], vecT[:, VEC_GB:VEC_GB + KT], None, z_hi, z_lo)
            split(U_F + 2)
            dve.wait_ge(unit_done, U_F + 1)
            dve.wait_ge(bf_loaded, 16)
            V.tensor_scalar(f_z[:], un[V_B % 2][0:HEADS, 0, :], b_f[:, 0:1], None, ALU.add).then_inc(un_free, 1)
            dve.wait_ge(un_free, freed(V_B))
            V.scalar_tensor_tensor(out=f_e[:], in0=f_z[:], scalar=-1.0, in1=f_z[:], op0=ALU.mult, op1=ALU.max).then_inc(f_abs, 1)
            dve.wait_ge(f_exp, 1)
            V.tensor_scalar(f_l[:], f_l[:], 1.0, None, ALU.add).then_inc(f_one, 1)
            dve.wait_ge(f_log, 1)
            link(V.scalar_tensor_tensor(out=f_e[:], in0=f_z[:], scalar=0.0, in1=f_l[:], op0=ALU.min, op1=ALU.subtract))
            link(V.tensor_tensor_scan(f_cum[:], ones_w[0:HEADS, 0:1].to_broadcast([HEADS, SEQ]), f_e[:], 0.0, ALU.mult, ALU.add))
            V.tensor_scalar(f_neg[:], f_cum[:], -1.0, None, ALU.mult).then_inc(f_ready, 1)
            for j in range(2 * UPD):
                split(U_KB + j + 2)
                if j == UPD:
                    dve.wait_ge(cumq_ready, 1)
                    link(V.tensor_copy(cum_q[:], misc[:, 0, 0:QT * HEADS].rearrange("p (a h) -> p a h", a=QT)))
            for j in range(UPD):
                split(U_QB + j + 2)
            attention(1, Z_B)
            for j in range(UPD):
                last_residuals(U_OB, None, j)
            norm_stats(N_MLP3)
            norm_split(H_BASE[N_MLP3], vecT[:, VEC_GMLP + KT:VEC_GMLP + 2 * KT], None, h_hi, h_lo)
            mlp(3, None)
            norm_stats(N_OUT)
            for t in range(KT):
                norm_mul(tmp, t, vecT[:, VEC_GFIN:VEC_GFIN + KT]).then_inc(normed, 1)
            for k in range(4):
                dve.wait_ge(tp_done, 5 + k + 1)
                V.tensor_copy(out_tok[:, k // 2, 512 * (k % 2):512 * (k % 2) + 512],
                              flat(un[(V_OUT + k) % 2])).then_inc(un_free, 1)

        @block.tensor
        def _(pe):
            MM = nc.tensor.matmul

            def three(out, hi_l, lo_l, hi_r, lo_r, start, stop):
                MM(out, hi_l, hi_r, start=start, stop=False, skip_group_check=True)
                MM(out, hi_l, lo_r, start=False, stop=False, skip_group_check=True)
                return MM(out, lo_l, hi_r, start=False, stop=stop, skip_group_check=True)

            def free_bank(v):
                if v >= V_CONV + 2:
                    pe.wait_ge(un_free, freed(v - 2))

            def unit(u, bank, xs, ready=None, tokens=False, first=True, last=True):
                xh, xl = xs
                wh, wl = w_hi[u % 2], w_lo[u % 2]
                for kt in range(KT):
                    if kt % (KT // 2) == 0:
                        pe.wait_ge(lo_made, 2 * u + kt // (KT // 2) + 1)
                    if ready is not None:
                        ready(kt)
                    for m in range(2):
                        s = first and kt == 0 and m == 0
                        if tokens:
                            q = slice(P * m, P * m + P)
                            ins = three(bank[:, m, :], xh[:, kt, q], xl[:, kt, q], wh[:, kt, :], wl[:, kt, :], s, last and kt == KT - 1)
                        else:
                            c = slice(P * m, P * m + P)
                            ins = three(bank[:, m, :], wh[:, kt, c], wl[:, kt, c], xh[:, kt, :], xl[:, kt, :], s, last and kt == KT - 1)
                ins.then_inc(unit_done, 1)

            def sum_squares(n, t):
                pe.wait_ge(sq_ready, 8 * n + t + 1)
                if t == 0 and n:
                    pe.wait_ge(ms_ready, n)
                    pe.wait_ge(root_ready, n)
                ins = MM(stat_ps[:, 0, :], mean_w, sq[:, t, :], start=(t == 0), stop=(t == KT - 1))
                if t == KT - 1:
                    ins.then_inc(stat_done, 1)

            def norm_stats(n):
                for t in range(KT):
                    sum_squares(n, t)

            def last_units(u, n, ready, first=True):
                for j in range(UPD):
                    unit(u + j, acc[j], (z_hi, z_lo), ready if j == 0 else None, first=first)
                    if j:
                        sum_squares(n, 2 * j - 2)
                        sum_squares(n, 2 * j - 1)
                sum_squares(n, KT - 2)
                sum_squares(n, KT - 1)

            def h_ready(base):
                return lambda kt: pe.wait_ge(h_lo_made, base + kt + 1)

            def z_ready(zc):
                return lambda kt: pe.wait_ge(z_lo_made, zc + kt // 2 + 1) if kt % 2 == 0 else None

            def mlp(m, n, n_next):
                u, v, zc = U_MLP[m], V_MLP[m], Z_MLP[m]
                for g in range(GROUPS):
                    for j in range(UPD):
                        free_bank(v + UPD * g + j)
                        unit(u + 2 * UPD * g + j, un[(v + j) % 2], (h_hi, h_lo), h_ready(H_BASE[n]) if g == 0 and j == 0 else None)
                    if g == GROUPS - 1:
                        if m == 0:
                            ada_sum(0, 16, 5)
                        last_units(u + 2 * UPD * g + UPD, n_next, z_ready(zc + UPD * g), first=False)
                        continue
                    for j in range(UPD):
                        unit(u + 2 * UPD * g + UPD + j, acc[j], (z_hi, z_lo), z_ready(zc + UPD * g) if j == 0 else None,
                             first=(g == 0), last=False)

            pe.wait_ge(const_in, 32)
            pe.wait_ge(vec_loaded, 16 * VEC_DMAS)
            flat0 = flat(un[0])
            for i, n in enumerate((P, P, N_VEC - 2 * P)):
                ins = nc.tensor.transpose(flat0[:, P * i:P * i + n], vec_in[0:n, i, :], ident[0:n, 0:n])
            ins.then_inc(tp_done, 1)
            pe.wait_ge(x_loaded, 16)
            for j in range(4):
                if j == 1:
                    pe.wait_ge(un_free, freed(V_VEC))
                if j >= 2:
                    pe.wait_ge(x_ready, 2 * (j - 1))
                for m in range(2):
                    for a in range(QT):
                        ins = nc.tensor.transpose(un[(V_X + j) % 2][:, m, P * a:P * a + P], x_in[:, a, P * (2 * j + m):P * (2 * j + m) + P], ident)
                ins.then_inc(tp_done, 1)

            def ada_sum(c0, c1, k):
                if k > 1:
                    pe.wait_ge(ada_summed, k - 1)
                for c in range(c0, c1):
                    if c * P % UC == 0:
                        a_end = (N_ADA if k >= 5 else 0) + c * P // UC + 1
                        pe.wait_ge(ada_dve_done, ada_count(ADA_DVE, a_end))
                        pe.wait_ge(ada_pool_done, ada_count(ADA_POOL, a_end))
                    ins = MM(misc[:, 0, c:c + 1], ada_acc[:, P * c:P * c + P], ones_w[:, 0:1], start=True, stop=True)
                ins.then_inc(ada_summed_pe, 1)

            norm_stats(N_CONV)
            ada_sum(0, 16, 1)
            for j in range(12):
                free_bank(V_CONV + j)
                unit(U_CONV_IN + j, un[(V_CONV + j) % 2], (h_hi, h_lo), h_ready(H_BASE[N_CONV]) if j == 0 else None)
            ada_sum(16, 24, 2)
            last_units(U_CONV_OUT, N_MLP0, z_ready(Z_CONV))
            ada_sum(24, 40, 3)
            ada_sum(40, 48, 4)
            mlp(0, N_MLP0, N_RW)
            ada_sum(16, 48, 6)
            def lora1_products(n):
                if n == 0:
                    pe.wait_ge(lora_loaded, 16 * 7)
                pe.wait_ge(lora_mixed, n + 1)
                c0 = (0, RD, RD + RA)[n]
                outs = ((acc[0][0:RD, 0, :], c0, RD),), ((acc[1][RD:RD + RA, 0, :], c0, RA),), ((acc[2][:, 0, :], c0, P), (acc[3][0:RG - P, 0, :], c0 + P, RG - P))
                for out_, c, m in outs[n]:
                    for t in range(KT):
                        ins = MM(out_, lora1[:, t, c:c + m], (lora_in_w, lora_in_a, lora_in_g)[n][:, t, :], start=(t == 0), stop=(t == KT - 1))
                ins.then_inc(lora1_done, 1)

            def lora2_products(which):
                rows_, w = ((slice(RD, RD + RA), lora_a2), (slice(0, RD), lora_w2))[which]
                for t in range(KT):
                    if t % 2 == 0:
                        if which == 0:
                            pe.wait_ge(ss_ready, t // 2 + 1)
                        else:
                            pe.wait_ge(lora2_out, t + 2)
                    ins = MM(acc[t // 2][:, t % 2, :], w[rows_, P * t:P * t + P], lora_h[rows_, 1 - which, :], start=True, stop=True)
                    if t % 2:
                        ins.then_inc(lora2_done, 1)

            def mix_done(m0):
                return lambda kt: pe.wait_ge(mix_lo, m0 + kt + 1)

            for j in range(12):
                free_bank(V_RKV + j)
                unit(U_RWK + j, un[(V_RKV + j) % 2], ((h_hi, h_lo), (z_hi, z_lo), (h_hi, h_lo))[j // 4],
                     mix_done(KT * (j // 4)) if j % 4 == 0 else None)
                if 3 <= j <= 5:
                    lora1_products(j - 3)
                if 7 <= j <= 8:
                    lora2_products(j - 7)
                if j == 6:
                    pe.wait_ge(lora1_out, 4)
                    for k in range(4):
                        pe.wait_ge(kksq_ready, k + 1)
                        for m in range(2):
                            ins = MM(acc[k][:, m, :], head_ones, tmp[:, 2 * k + m, :], start=True, stop=True)
                        ins.then_inc(ss_done, 1)
                if j == 9:
                    for t in range(KT):
                        if t % 2 == 0:
                            pe.wait_ge(lora2_out, KT + t + 2)
                        MM(acc[t // 2][:, t % 2, :], lora_g2a[:, P * t:P * t + P], lora_h[:, 2, :], start=True, stop=False)
                        ins = MM(acc[t // 2][:, t % 2, :], lora_g2b[:, P * t:P * t + P], lora_h[0:RG - P, 3, :], start=False, stop=True)
                        if t % 2:
                            ins.then_inc(lora2_done, 1)
            pe.wait_ge(lora2_out, 20)
            pe.wait_ge(un_free, freed(V_RKV + 11))

            def group_step(step, j):
                if step == "bonus":
                    pe.wait_ge(inv_ready, 12 * PAIRS)
                    if j >= 2:
                        pe.wait_ge(bonus_ready, j - 1)
                    pe.wait_ge(rk_ready, 2 * j + 2)
                    for m in range(2):
                        ins = MM(bonus_bank[j][:, m, :], head_ones, rw_c[:, 2 * j + m, :], start=True, stop=True)
                    ins.then_inc(bonus_done, 1)
                    return
                if step == "var":
                    pe.wait_ge(ycsq_ready, j + 1)
                elif j == 0:
                    pe.wait_ge(inv_ready, 12 * PAIRS)
                for m, t in enumerate(range(*GN_GROUPS[j])):
                    ins = MM(gn_bank[j][:, m, :], head_mean, (y_wkv if step == "mean" else rw_kk)[:, t, :], start=True, stop=True)
                ins.then_inc(gn_mean_done if step == "mean" else gn_var_done, 1)

            for slot in range(PAIRS + 1):
                for n, (step, p, j, h) in enumerate(wkv_steps(slot)):
                    half = (2 * h, 2 * h + 1)
                    xt = inv_t[p % 2]
                    if step == "gram":
                        pe.wait_ge(built, p + 1)
                        for c in half:
                            MM(acc[h][:, c % 2, 0:P + CHUNK], b_bd[:, c, :], ar[p % 2][:, c, :], start=True, stop=True)
                            ins = MM(acc[2 + h][:, c % 2, 0:P + CHUNK], k_bd[:, c, :], ar[p % 2][:, c, :], start=True, stop=True)
                        ins.then_inc(g_done, 1)
                    elif step == "tok":
                        if h == 0:
                            pe.wait_ge(v_built, p + 1)
                            if p:
                                pe.wait_ge(inv_ready, 12 * p)
                        else:
                            pe.wait_ge(tok_out, 3 * p + 1)
                        for src, dst in ((v_bd, un[0]), (b_bd, un[1])) if h == 0 else ((k_bd, un[0]),):
                            for c in range(CHUNKS):
                                ins = nc.tensor.transpose(bank4(dst)[:, c, :], src[:, c, :], ident)
                            ins.then_inc(tok_done, 1)
                    elif step == "x1":
                        pe.wait_ge(inv_ready, 12 * p + h + 1)
                        for c in half:
                            ins = nc.tensor.transpose(bank4(acc[h])[:, c % 2, :], xt[:, c, :], ident)
                        ins.then_inc(x1_done, 1)
                    elif step == "t1":
                        if j == 1:
                            pe.wait_ge(x1_out, 2 * p + h + 1)
                        else:
                            pe.wait_ge(nm_ready, 4 * p + j - 1)
                            pe.wait_ge(inv_ready, 12 * p + 2 * (j - 1) + h + 1)
                        for c in half:
                            ins = MM(bank4(acc[h])[:, c % 2, :], n_m[(j - 1) % 2][:, c, :], inv_x[:, c, :], start=True, stop=True)
                        ins.then_inc(t1_done, 1)
                    elif step == "dx":
                        if j == 1:
                            pe.wait_ge(lak_ready, 2 * p + h + 1)
                            pe.wait_ge(tok_out, 3 * p + 3)
                        pe.wait_ge(t1_out, 10 * p + 2 * (j - 1) + h + 1)
                        for c in half:
                            if j < WKV_LEVELS[-1]:
                                MM(early(bank4(acc[2 + h])[:, c % 2, :], j), xt[:, c, :], early(t1[:, c, :], j), start=True, stop=True)
                            ins = MM(late(bank4(un[h])[:, c % 2, :], j), t1[:, c, :], late(xt[:, c, :], j), start=True, stop=True)
                        ins.then_inc(dx_done, 1)
                    else:
                        c, i, q = j, CHUNKS * p + j, p % 2
                        before = state[(c - 1) % 2]
                        if step == "rhs":
                            out_ = stat_ps[:, 0, 0:P]
                            if c:
                                pe.wait_ge(state_ready, (CHUNKS - 1) * p + c)
                                MM(out_, ar[q][:, c, 0:P], before[:], start=True, stop=False)
                            MM(out_, lak_t[q][:, c, :], v_tok[q][:, c, :], start=(c == 0), stop=True).then_inc(rhs_done, 1)
                        elif step == "u":
                            pe.wait_ge(rhs_out, i + 1)
                            pe.wait_ge(inv_ready, 12 * p + 11 + h)
                            MM(stat_ps[:, 0, 0:P], xt[:, c, :], wkv_rhs[:], start=True, stop=True).then_inc(u_done, 1)
                        else:
                            pe.wait_ge(u_out, i + 1)
                            if c < CHUNKS - 1:
                                MM(stat_ps[:, 0, 0:P], b_tok[q][:, c, :], wkv_u[:], start=True, stop=False)
                                MM(stat_ps[:, 0, 0:P], k_tok[q][:, c, :], v_tok[q][:, c, :], start=False, stop=True).then_inc(s_done, 1)
                            if i:
                                pe.wait_ge(y_out, i)
                            y = misc[:, 0, 0:CHUNK]
                            if c:
                                MM(y, before[:], ar[q][:, c, P:P + CHUNK], start=True, stop=False)
                            MM(y, wkv_u[:], lrb_t[q][:, c, :], start=(c == 0), stop=False)
                            MM(y, v_tok[q][:, c, :], lrk_t[q][:, c, :], start=False, stop=True).then_inc(y_done, 1)
                    for group in GROUP_PE.get(n, ()) if slot == PAIRS else ():
                        group_step(*group)
            pe.wait_ge(y_out, CHUNKS * PAIRS)
            group_step("mean", 4)
            group_step("var", 4)
            last_units(U_RWO, N_MLP1, z_ready(Z_RW))
            mlp(1, N_MLP1, N_FIN1)

            def rot(r, n, v):
                pe.wait_ge(un_free, freed(v))
                if r:
                    pe.wait_ge(rope_done, r)
                MM(misc[:, 0:n, :], rot_w, rope_in[r % 2][:, 0:n, :], start=True, stop=True).then_inc(rot_done, 1)

            def attention(kind, k_of, v_of):
                b = HEADS * kind
                for i in range(-3, HEADS + 1):
                    k = i + 3
                    if k < HEADS:
                        lo = HD * (k % 2)
                        if k >= 4:
                            pe.wait_ge(max_ready, b + k - 3)
                        if kind == 0:
                            pe.wait_ge(rope_done, ROPE_Q + k // 4 + 1)
                        for qt in range(QT):
                            ins = MM(flat(acc[k % 4])[:, QUERY[qt]], q_fm[lo:lo + HD, k // 2, P * qt:P * qt + P], k_of(k)[:, 0:KEYS[qt]], start=True, stop=True)
                        ins.then_inc(qk_done, 1)
                    if 0 <= i < HEADS:
                        pe.wait_ge(p0_ready, b + i + 1)
                        pe.wait_ge(p1_ready, b + i + 1)
                        if i >= 2:
                            pe.wait_ge(pt_out, b + i - 1)
                        dst = flat((stat_ps, misc)[i % 2])
                        for n in range(PACK // P):
                            ins = nc.tensor.transpose(dst[:, P * n:P * n + P], probs[i % NA][:, P * n:P * n + P], ident)
                        ins.then_inc(pt_done, 1)
                    if i >= 1:
                        h = i - 1
                        lo = HD * (h % 2)
                        pe.wait_ge(pt_out, b + h + 1)
                        if h % 4 == 0 and h >= 8:
                            pe.wait_ge(zf_ready, zf_count((Z_A, Z_B)[kind] + h // 4 - 2))
                        o = un[h // 4 % 2][lo:lo + HD, h // 2 % 2, :]
                        pt = probs_t[h % 2]
                        MM(o[:, 0:P], v_of(h, 0), pt[:, 0, :], start=True, stop=True, skip_group_check=True)
                        MM(o[:, P:2 * P], v_of(h, 0), pt[:, 1, :], start=True, stop=False, skip_group_check=True)
                        MM(o[:, P:2 * P], v_of(h, 1), pt[:, 2, :], start=False, stop=True, skip_group_check=True).then_inc(pv_done, 1)

            norm_stats(N_A)
            h_tiles = (h_hi, h_lo)
            free_bank(V_A)
            pe.wait_ge(lo_made, 2 * U_KI + 2)
            wh, wl = w_hi[U_KI % 2], w_lo[U_KI % 2]
            bank = un[V_A % 2]
            for kt in range(KT):
                pe.wait_ge(h_lo_made, H_BASE[N_A] + kt + 1)
                three(bank[:, 0, :], wh[:, kt, 0:P], wl[:, kt, 0:P], h_hi[:, kt, :], h_lo[:, kt, :], kt == 0, kt == KT - 1)
            for a in range(QT):
                q = slice(P * a, P * a + P)
                for kt in range(KT):
                    ins = three(bank[:, 1, IDX_HEADS * a:IDX_HEADS * (a + 1)], h_hi[:, kt, q], h_lo[:, kt, q], wh[:, kt, P:KI_COLS],
                                wl[:, kt, P:KI_COLS], False, kt == KT - 1)
            ins.then_inc(unit_done, 1)

            def a_unit(k, tokens=False):
                free_bank(V_A + k)
                unit(U_KI + k, un[(V_A + k) % 2], h_tiles, tokens=tokens)

            def index_scores(qt):
                if qt == 0:
                    pe.wait_ge(rope_done, ROPE_QI + 2)
                else:
                    pe.wait_ge(score_relu, IDX_HEADS // 2 * qt)
                for h in range(IDX_HEADS):
                    lo = HD * (h % 2)
                    ins = MM(acc[2 * (h // 4) + h % 2][:, h // 2 % 2, 0:KEYS[qt]], qi_fm[lo:lo + HD, h // 2, P * qt:P * qt + P],
                             ki_fm[lo:lo + HD, 0, 0:KEYS[qt]], start=True, stop=True)
                ins.then_inc(score_done, 1)

            a_unit(1)
            rot(ROPE_KI, 1, V_A)
            a_unit(2)
            rot(ROPE_QI, 2, V_A + 1)
            a_unit(3)
            rot(ROPE_QI + 1, 2, V_A + 2)
            a_unit(4, tokens=True)
            rot(ROPE_K, 2, V_A + 3)
            index_scores(0)
            a_unit(5)
            index_scores(1)
            a_unit(6)
            rot(ROPE_Q, 2, V_A + 5)
            a_unit(7)
            rot(ROPE_Q + 1, 2, V_A + 6)
            a_unit(8)
            rot(ROPE_Q + 2, 2, V_A + 7)
            rot(ROPE_Q + 3, 2, V_A + 8)
            pe.wait_ge(kdup_ready, KV_HEADS)
            pe.wait_ge(score_relu, QT * IDX_HEADS // 2)
            group = HEADS // KV_HEADS
            attention(0, lambda h: k_dup[HD * (h % 2):HD * (h % 2) + HD, h // group, :],
                      lambda h, s: vA_tok[:, s, HD * (h // group):HD * (h // group) + HD])
            last_units(U_OA, N_MLP2, z_ready(Z_A))
            mlp(2, N_MLP2, N_B)
            free_bank(V_B)
            pe.wait_ge(lo_made, 2 * U_F + 2)
            wh, wl = w_hi[U_F % 2], w_lo[U_F % 2]
            for kt in range(KT):
                pe.wait_ge(h_lo_made, H_BASE[N_B] + kt + 1)
                ins = three(un[V_B % 2][:, 0, :], wh[:, kt, 0:P], wl[:, kt, 0:P], h_hi[:, kt, :], h_lo[:, kt, :], kt == 0, kt == KT - 1)
            ins.then_inc(unit_done, 1)
            for j in range(UPD):
                free_bank(V_B + 1 + j)
                unit(U_KB + j, un[(V_B + 1 + j) % 2], h_tiles)
            pe.wait_ge(f_ready, 1)
            for a in range(QT):
                ins = nc.tensor.transpose(misc[:, 0, HEADS * a:HEADS * (a + 1)], f_cum[:, P * a:P * a + P], ident[0:HEADS, 0:HEADS])
            ins.then_inc(cumq_ready, 1)
            for r in range(8):
                if r >= 4:
                    pe.wait_ge(cumk_ready, r - 3)
                for m in range(2):
                    ins = MM(acc[r % 4][:, m, :], ident[0:HEADS, 2 * r + m:2 * r + m + 1].to_broadcast([HEADS, P]), f_neg[:], start=True, stop=True)
                ins.then_inc(f_bcast, 1)
            for j in range(UPD):
                free_bank(V_B + 5 + j)
                unit(U_VB + j, un[(V_B + 5 + j) % 2], h_tiles, tokens=True)
            for j in range(UPD):
                free_bank(V_B + 9 + j)
                unit(U_QB + j, un[(V_B + 9 + j) % 2], (z_hi, z_lo), h_ready(H_BASE["B_q"]) if j == 0 else None)
            pe.wait_ge(un_free, freed(V_B + 12))
            attention(1, lambda h: kB_fm[HD * (h % 2):HD * (h % 2) + HD, h // 2, :], lambda h, s: vB_tok[:, s, HD * h:HD * h + HD])
            last_units(U_OB, N_MLP3, z_ready(Z_B))
            mlp(3, N_MLP3, N_OUT)
            pe.wait_ge(normed, 64 + KT)
            for k in range(4):
                free_bank(V_OUT + k)
                for n in range(4):
                    t = 4 * (k % 2) + n
                    ins = nc.tensor.transpose(bank4(un[(V_OUT + k) % 2])[:, n, :], tmp[:, t, P * (k // 2):P * (k // 2) + P], ident)
                ins.then_inc(tp_done, 1)


INPUTS = ("x", "c", "norm_g", "final_g", "ada_w", "ada_b", "conv_w_in", "conv_w", "conv_w_out", "rw_mu", "rw_w_rkv", "rw_w_o",
          "rw_w0", "rw_w1", "rw_w2", "rw_a0", "rw_a1", "rw_a2", "rw_g1", "rw_g2", "rw_k_k", "rw_k_a", "rw_r_k", "rw_ln_w",
          "rw_ln_b", "mlp_w1", "mlp_w2", "g_attn_a_2", "w_in_a_2", "w_o_a_2", "g_kv_2", "w_kv_b_2", "b_f_2", "g_attn_b_2",
          "w_q_b_2", "w_o_b_2", "g_mlp_2", "w_up_2", "w_down_2", "g_final_2")


def kernel(**inputs):
    import concourse.bacc as bacc
    from concourse.bass_utils import run_bass_kernel_spmd

    nc = bacc.Bacc("TRN2", target_bir_lowering=False, num_devices=1)
    arrays = {f"in_{n}": np.ascontiguousarray(inputs[n]) for n in INPUTS}
    arrays["in_const_table"] = constant_table()
    aps = {n[3:]: nc.dram_tensor(n, a.shape, mybir.dt.from_np(a.dtype), kind="ExternalInput").ap() for n, a in arrays.items()}
    out = nc.dram_tensor("out_x", (1, SEQ, D), F32, kind="ExternalOutput").ap()
    build(nc, aps, out)
    return run_bass_kernel_spmd(nc, [arrays], core_ids=[0]).results[0]["out_x"]
```
